# Optimizing a Trainium2 kernel written in Bass

```python
import jax
import jax.numpy as jnp
from jax import lax
import numpy as np

D_MODEL = 1024
BATCH = 1
SEQ = 256
DEPTH = 1
DEC_BATCH = 8
DEC_SEQ = 1
PAST_LEN = 2048
PAGE_SIZE = 128

GDN_HEADS = 4
GDN_DK = 128
GDN_DV = 128
CONV_WIDTH = 4
GDN_CHUNK = 64
MLA_HEADS = 4
MLA_NOPE = 128
MLA_ROPE = 64
MLA_V = 128
MLA_Q_RANK = 384
MLA_KV_RANK = 256
ROPE_THETA = 10000.0
Q_BLOCK = 128
MLA_SCALE = (MLA_NOPE + MLA_ROPE) ** -0.5
MEM_TOKENS = 256
X_HEADS = 4
X_HEAD_DIM = D_MODEL // X_HEADS
N_EXPERTS = 32
TOP_K = 4
D_FF = D_MODEL
SWIGLU_LIMIT = 7.0
SWIGLU_ALPHA = 1.702
NORM_EPS = 1e-6

GDN_QK_W = GDN_HEADS * GDN_DK
GDN_V_W = GDN_HEADS * GDN_DV
CONV_CH = 2 * GDN_QK_W + GDN_V_W
MLA_OUT_W = MLA_HEADS * MLA_V
MIX_WIDTH = GDN_V_W + MLA_OUT_W
IN_SPLITS = (CONV_CH, GDN_V_W, GDN_HEADS, GDN_HEADS, MLA_Q_RANK, MLA_KV_RANK, MLA_ROPE)
IN_COLS = CONV_CH + GDN_V_W + 2 * GDN_HEADS + MLA_Q_RANK + MLA_KV_RANK + MLA_ROPE

kernel_name = 'hybrid_gdn_mla_xmem_moe_step'

def rms_norm(x, gain):
    xf = x.astype(jnp.float32)
    y = xf * lax.rsqrt(jnp.mean(xf * xf, axis=-1, keepdims=True) + NORM_EPS)
    return (y * gain.astype(jnp.float32)).astype(x.dtype)

def l2_normalize(x):
    return x * lax.rsqrt(jnp.sum(x * x, axis=-1, keepdims=True) + NORM_EPS)

def apply_rope(x, pos):
    half = MLA_ROPE // 2
    inv_freq = 1.0 / (ROPE_THETA ** (jnp.arange(half, dtype=jnp.float32) / half))
    ang = pos.astype(jnp.float32)[:, None] * inv_freq[None, :]
    cos = jnp.cos(ang)[None, :, None, :]
    sin = jnp.sin(ang)[None, :, None, :]
    xf = x.astype(jnp.float32)
    x1, x2 = xf[..., :half], xf[..., half:]
    return jnp.concatenate([x1 * cos - x2 * sin, x2 * cos + x1 * sin], axis=-1).astype(x.dtype)

def split_projection(xn, w_in):
    offs = np.cumsum(IN_SPLITS)[:-1].tolist()
    return jnp.split(xn @ w_in, offs, axis=-1)

def causal_short_conv(xh, w):
    t_new = xh.shape[1] - (CONV_WIDTH - 1)
    out = xh[:, 0:t_new] * w[0]
    for j in range(1, CONV_WIDTH):
        out = out + xh[:, j:j + t_new] * w[j]
    return jax.nn.silu(out)

def gdn_gates(conv_out, b_logit, a_logit, a_log, dt_bias):
    B, T, _ = conv_out.shape
    cf = conv_out.astype(jnp.float32)
    q = l2_normalize(cf[..., :GDN_QK_W].reshape(B, T, GDN_HEADS, GDN_DK)) * (GDN_DK ** -0.5)
    k = l2_normalize(cf[..., GDN_QK_W:2 * GDN_QK_W].reshape(B, T, GDN_HEADS, GDN_DK))
    v = cf[..., 2 * GDN_QK_W:].reshape(B, T, GDN_HEADS, GDN_DV)
    beta = jax.nn.sigmoid(b_logit.astype(jnp.float32))
    g = -jnp.exp(a_log.astype(jnp.float32)) * jax.nn.softplus(a_logit.astype(jnp.float32) + dt_bias.astype(jnp.float32))
    return q, k, v, g, beta

def gdn_chunked(q, k, v, g, beta):
    B, T, H, DK = q.shape
    DV = v.shape[-1]
    C = GDN_CHUNK
    N = T // C

    def chunks(t):
        return jnp.moveaxis(t.reshape((B, N, C) + t.shape[2:]), 2, 3)

    qc, kc, vc, gc, bc = (chunks(t) for t in (q, k, v, g, beta))
    gc = jnp.cumsum(gc, axis=-1)
    incl = jnp.tril(jnp.ones((C, C), dtype=bool))
    strict = jnp.tril(jnp.ones((C, C), dtype=bool), -1)
    decay = jnp.exp(jnp.where(incl, gc[..., :, None] - gc[..., None, :], -jnp.inf))
    kb = kc * bc[..., None]
    vb = vc * bc[..., None]
    lower = jnp.where(strict, jnp.einsum('bnhcd,bnhsd->bnhcs', kb, kc) * decay, 0.0)
    eye = jnp.eye(C, dtype=jnp.float32)
    wy = lax.linalg.triangular_solve(eye + lower, jnp.broadcast_to(eye, lower.shape),
                                     left_side=True, lower=True, unit_diagonal=True)
    u = jnp.einsum('bnhcs,bnhse->bnhce', wy, vb)
    w = jnp.einsum('bnhcs,bnhsd->bnhcd', wy, kb * jnp.exp(gc)[..., None])
    intra = jnp.einsum('bnhcd,bnhsd->bnhcs', qc, kc) * decay

    def step(S, xs):
        q_i, k_i, u_i, w_i, g_i, a_i = xs
        v_new = u_i - jnp.einsum('bhcd,bhde->bhce', w_i, S)
        o_i = (jnp.einsum('bhcd,bhde->bhce', q_i * jnp.exp(g_i)[..., None], S)
               + jnp.einsum('bhcs,bhse->bhce', a_i, v_new))
        g_last = g_i[..., -1:]
        S = (S * jnp.exp(g_last)[..., None]
             + jnp.einsum('bhcd,bhce->bhde', k_i * jnp.exp(g_last - g_i)[..., None], v_new))
        return S, o_i

    S0 = jnp.zeros((B, H, DK, DV), jnp.float32)
    xs = tuple(jnp.moveaxis(t, 1, 0) for t in (qc, kc, u, w, gc, intra))
    S, o = lax.scan(step, S0, xs)
    return S, jnp.transpose(o, (1, 0, 3, 2, 4)).reshape(B, T, H, DV)

def gdn_recurrent(S, q, k, v, g, beta):
    def step(S, xs):
        q_t, k_t, v_t, g_t, b_t = xs
        S = S * jnp.exp(g_t)[..., None, None]
        pred = jnp.einsum('bhd,bhde->bhe', k_t, S)
        S = S + jnp.einsum('bhd,bhe->bhde', k_t, (v_t - pred) * b_t[..., None])
        return S, jnp.einsum('bhd,bhde->bhe', q_t, S)

    S, o = lax.scan(step, S, tuple(jnp.moveaxis(t, 1, 0) for t in (q, k, v, g, beta)))
    return S, jnp.moveaxis(o, 0, 1)

def gdn_output(o, z, gdn_norm):
    B, T = z.shape[:2]
    zz = z.astype(jnp.float32).reshape(B, T, GDN_HEADS, GDN_DV)
    return (rms_norm(o, gdn_norm) * jax.nn.silu(zz)).reshape(B, T, GDN_V_W).astype(z.dtype)

def mla_project(c_q, c_kv, k_pe, pos, q_norm, w_uq, kv_norm):
    q = jnp.einsum('btr,rhd->bthd', rms_norm(c_q, q_norm), w_uq)
    q_nope = q[..., :MLA_NOPE]
    q_pe = apply_rope(q[..., MLA_NOPE:], pos)
    lat = rms_norm(c_kv, kv_norm)
    kpe = apply_rope(k_pe[:, :, None, :], pos)[:, :, 0, :]
    return q_nope, q_pe, lat, kpe

def mla_prompt(q_nope, q_pe, lat, kpe, w_uk, w_uv):
    B, T, H, _ = q_nope.shape
    k_nope = jnp.einsum('bsr,rhd->bshd', lat, w_uk)
    v = jnp.einsum('bsr,rhd->bshd', lat, w_uv)
    nb = T // Q_BLOCK
    qn_b = jnp.moveaxis(q_nope.reshape(B, nb, Q_BLOCK, H, MLA_NOPE), 1, 0)
    qp_b = jnp.moveaxis(q_pe.reshape(B, nb, Q_BLOCK, H, MLA_ROPE), 1, 0)
    kpos = jnp.arange(T)

    def block(args):
        i, qn, qp = args
        s = (jnp.einsum('bqhd,bshd->bhqs', qn, k_nope)
             + jnp.einsum('bqhd,bsd->bhqs', qp, kpe)).astype(jnp.float32) * MLA_SCALE
        qpos = i * Q_BLOCK + jnp.arange(Q_BLOCK)
        s = jnp.where(kpos[None, :] <= qpos[:, None], s, -jnp.inf)
        p = jax.nn.softmax(s, axis=-1).astype(v.dtype)
        return jnp.einsum('bhqs,bshd->bqhd', p, v)

    o = lax.map(block, (jnp.arange(nb), qn_b, qp_b))
    return jnp.moveaxis(o, 0, 1).reshape(B, T, H * MLA_V)

def mla_sample(q_nope, q_pe, lat_new, kpe_new, cache_latent, cache_krope, page_table, layer, w_uk, w_uv):
    B, T, H, _ = q_nope.shape
    q_lat = jnp.einsum('bthd,rhd->bthr', q_nope, w_uk)

    def scores(lat, kpe):
        return (jnp.einsum('bthr,bsr->bhts', q_lat, lat)
                + jnp.einsum('bthd,bsd->bhts', q_pe, kpe)).astype(jnp.float32) * MLA_SCALE

    s_new = jnp.where(jnp.tril(jnp.ones((T, T), dtype=bool)), scores(lat_new, kpe_new), -jnp.inf)
    m0 = jnp.max(s_new, axis=-1)
    p0 = jnp.exp(s_new - m0[..., None])
    l0 = jnp.sum(p0, axis=-1)
    acc0 = jnp.einsum('bhts,bsr->bhtr', p0, lat_new.astype(jnp.float32))

    def page_step(carry, pages):
        m, l, acc = carry
        lat = cache_latent[pages, layer]
        kpe = cache_krope[pages, layer]
        s = scores(lat, kpe)
        m_new = jnp.maximum(m, jnp.max(s, axis=-1))
        corr = jnp.exp(m - m_new)
        p = jnp.exp(s - m_new[..., None])
        l = l * corr + jnp.sum(p, axis=-1)
        acc = acc * corr[..., None] + jnp.einsum('bhts,bsr->bhtr', p, lat.astype(jnp.float32))
        return (m_new, l, acc), None

    (m, l, acc), _ = lax.scan(page_step, (m0, l0, acc0), page_table.T)
    o_lat = (acc / l[..., None]).astype(q_nope.dtype)
    o = jnp.einsum('bhtr,rhd->bthd', o_lat, w_uv)
    return o.reshape(B, T, H * MLA_V)

def memory_kv(mem, mem_norm, w_xk, w_xv):
    B, M, _ = mem.shape
    mn = rms_norm(mem, mem_norm)
    return ((mn @ w_xk).reshape(B, M, X_HEADS, X_HEAD_DIM),
            (mn @ w_xv).reshape(B, M, X_HEADS, X_HEAD_DIM))

def cross_attend(hn, mem_k, mem_v, w_xq, w_xo):
    B, T, _ = hn.shape
    q = (hn @ w_xq).reshape(B, T, X_HEADS, X_HEAD_DIM)
    s = jnp.einsum('bthd,bmhd->bhtm', q, mem_k).astype(jnp.float32) * (X_HEAD_DIM ** -0.5)
    p = jax.nn.softmax(s, axis=-1).astype(mem_v.dtype)
    o = jnp.einsum('bhtm,bmhd->bthd', p, mem_v).reshape(B, T, X_HEADS * X_HEAD_DIM)
    return o @ w_xo

def moe_ffn(h, w_router, b_router, w_e1, b_e1, w_e2, b_e2):
    B, T, D = h.shape
    xt = h.reshape(B * T, D)
    logits = (xt @ w_router + b_router).astype(jnp.float32)
    top_v, top_i = lax.top_k(logits, TOP_K)
    gates = jax.nn.softmax(top_v, axis=-1)
    gate_w = jnp.sum(jax.nn.one_hot(top_i, N_EXPERTS, dtype=jnp.float32) * gates[..., None], axis=1)

    def expert(acc, ew):
        w1, b1, w2, b2, g_col = ew
        hh = xt @ w1 + b1
        glu = jnp.minimum(hh[:, 0::2], SWIGLU_LIMIT)
        lin = jnp.clip(hh[:, 1::2], -SWIGLU_LIMIT, SWIGLU_LIMIT)
        y = ((lin + 1.0) * (glu * jax.nn.sigmoid(SWIGLU_ALPHA * glu))) @ w2 + b2
        return acc + g_col[:, None].astype(y.dtype) * y, None

    out, _ = lax.scan(expert, jnp.zeros_like(xt), (w_e1, b_e1, w_e2, b_e2, gate_w.T))
    return out.reshape(B, T, D)

def layer_tail(h, mem_k, mem_v, norm_x, w_xq, w_xo, norm_ffn, w_router, b_router, w_e1, b_e1, w_e2, b_e2):
    h = h + cross_attend(rms_norm(h, norm_x), mem_k, mem_v, w_xq, w_xo)
    return h + moe_ffn(rms_norm(h, norm_ffn), w_router, b_router, w_e1, b_e1, w_e2, b_e2)

def prompt_layer(x, mem, mem_norm, w_xk, w_xv, norm_mix, w_in, conv_w, a_log, dt_bias, gdn_norm,
                 q_norm, w_uq, kv_norm, w_uk, w_uv, w_out, norm_x, w_xq, w_xo, norm_ffn,
                 w_router, b_router, w_e1, b_e1, w_e2, b_e2):
    B, T, _ = x.shape
    conv_in, z, b_logit, a_logit, c_q, c_kv, k_pe = split_projection(rms_norm(x, norm_mix), w_in)
    conv_hist = jnp.concatenate([jnp.zeros((B, CONV_WIDTH - 1, CONV_CH), conv_in.dtype), conv_in], axis=1)
    q, k, v, g, beta = gdn_gates(causal_short_conv(conv_hist, conv_w), b_logit, a_logit, a_log, dt_bias)
    S, o = gdn_chunked(q, k, v, g, beta)
    y_gdn = gdn_output(o, z, gdn_norm)
    pos = jnp.arange(T, dtype=jnp.int32)
    q_nope, q_pe, lat, kpe = mla_project(c_q, c_kv, k_pe, pos, q_norm, w_uq, kv_norm)
    y_mla = mla_prompt(q_nope, q_pe, lat, kpe, w_uk, w_uv)
    h = x + jnp.concatenate([y_gdn, y_mla], axis=-1) @ w_out
    mem_k, mem_v = memory_kv(mem, mem_norm, w_xk, w_xv)
    y = layer_tail(h, mem_k, mem_v, norm_x, w_xq, w_xo, norm_ffn, w_router, b_router, w_e1, b_e1, w_e2, b_e2)
    return y, S.astype(x.dtype), conv_hist[:, -(CONV_WIDTH - 1):], lat, kpe, mem_k, mem_v

def sample_layer(x, layer, state_gdn, state_conv, cache_latent, cache_krope, page_table, mem_k, mem_v,
                 norm_mix, w_in, conv_w, a_log, dt_bias, gdn_norm, q_norm, w_uq, kv_norm, w_uk, w_uv,
                 w_out, norm_x, w_xq, w_xo, norm_ffn, w_router, b_router, w_e1, b_e1, w_e2, b_e2):
    B, T, _ = x.shape
    conv_in, z, b_logit, a_logit, c_q, c_kv, k_pe = split_projection(rms_norm(x, norm_mix), w_in)
    conv_hist = jnp.concatenate([state_conv.astype(conv_in.dtype), conv_in], axis=1)
    q, k, v, g, beta = gdn_gates(causal_short_conv(conv_hist, conv_w), b_logit, a_logit, a_log, dt_bias)
    S, o = gdn_recurrent(state_gdn.astype(jnp.float32), q, k, v, g, beta)
    y_gdn = gdn_output(o, z, gdn_norm)
    pos = PAST_LEN + jnp.arange(T, dtype=jnp.int32)
    q_nope, q_pe, lat, kpe = mla_project(c_q, c_kv, k_pe, pos, q_norm, w_uq, kv_norm)
    y_mla = mla_sample(q_nope, q_pe, lat, kpe, cache_latent, cache_krope, page_table, layer, w_uk, w_uv)
    h = x + jnp.concatenate([y_gdn, y_mla], axis=-1) @ w_out
    y = layer_tail(h, mem_k, mem_v, norm_x, w_xq, w_xo, norm_ffn, w_router, b_router, w_e1, b_e1, w_e2, b_e2)
    return y, S.astype(state_gdn.dtype), conv_hist[:, -(CONV_WIDTH - 1):], lat, kpe

def setup_inputs(seed: int = 0) -> dict:
    key = jax.random.key(seed)
    ks = iter(jax.random.split(key, 48))
    f32 = jnp.float32

    def nrm(shape, scale):
        return jax.random.normal(next(ks), shape, f32) * scale

    def gain(shape):
        return 1.0 + nrm(shape, 0.02)

    L = DEPTH
    n_pages = PAST_LEN // PAGE_SIZE
    n_used = DEC_BATCH * n_pages
    n_pool = n_used + max(1, n_used // 4)
    page_table = jax.random.permutation(next(ks), n_pool)[:n_used].reshape(DEC_BATCH, n_pages).astype(jnp.int32)
    dt = jnp.exp(jax.random.uniform(next(ks), (L, GDN_HEADS), f32, float(np.log(1e-3)), float(np.log(1e-1))))
    xw = X_HEADS * X_HEAD_DIM
    return {
        'x_prompt': nrm((BATCH, SEQ, D_MODEL), 1.0),
        'x_sample': nrm((DEC_BATCH, DEC_SEQ, D_MODEL), 1.0),
        'state_gdn': nrm((L, DEC_BATCH, GDN_HEADS, GDN_DK, GDN_DV), 0.3),
        'state_conv': nrm((L, DEC_BATCH, CONV_WIDTH - 1, CONV_CH), 1.0),
        'cache_latent': nrm((n_pool, L, PAGE_SIZE, MLA_KV_RANK), 1.0),
        'cache_krope': nrm((n_pool, L, PAGE_SIZE, MLA_ROPE), 1.0),
        'page_table': page_table,
        'cache_mem_k': nrm((L, DEC_BATCH, MEM_TOKENS, X_HEADS, X_HEAD_DIM), 1.0),
        'cache_mem_v': nrm((L, DEC_BATCH, MEM_TOKENS, X_HEADS, X_HEAD_DIM), 1.0),
        'mem_prompt': nrm((BATCH, MEM_TOKENS, D_MODEL), 1.0),
        'norm_mix': gain((L, D_MODEL)),
        'w_in': nrm((L, D_MODEL, IN_COLS), D_MODEL ** -0.5),
        'conv_w': nrm((L, CONV_WIDTH, CONV_CH), CONV_WIDTH ** -0.5),
        'a_log': jnp.log(jax.random.uniform(next(ks), (L, GDN_HEADS), f32, 1.0, 16.0)),
        'dt_bias': dt + jnp.log(-jnp.expm1(-dt)),
        'gdn_norm': gain((L, GDN_DV)),
        'q_norm': gain((L, MLA_Q_RANK)),
        'w_uq': nrm((L, MLA_Q_RANK, MLA_HEADS, MLA_NOPE + MLA_ROPE), MLA_Q_RANK ** -0.5),
        'kv_norm': gain((L, MLA_KV_RANK)),
        'w_uk': nrm((L, MLA_KV_RANK, MLA_HEADS, MLA_NOPE), MLA_KV_RANK ** -0.5),
        'w_uv': nrm((L, MLA_KV_RANK, MLA_HEADS, MLA_V), MLA_KV_RANK ** -0.5),
        'w_out': nrm((L, MIX_WIDTH, D_MODEL), MIX_WIDTH ** -0.5),
        'norm_x': gain((L, D_MODEL)),
        'mem_norm': gain((L, D_MODEL)),
        'w_xq': nrm((L, D_MODEL, xw), D_MODEL ** -0.5),
        'w_xk': nrm((L, D_MODEL, xw), D_MODEL ** -0.5),
        'w_xv': nrm((L, D_MODEL, xw), D_MODEL ** -0.5),
        'w_xo': nrm((L, xw, D_MODEL), xw ** -0.5),
        'norm_ffn': gain((L, D_MODEL)),
        'w_router': nrm((L, D_MODEL, N_EXPERTS), D_MODEL ** -0.5),
        'b_router': nrm((L, N_EXPERTS), 0.01),
        'w_e1': nrm((L, N_EXPERTS, D_MODEL, 2 * D_FF), D_MODEL ** -0.5),
        'b_e1': nrm((L, N_EXPERTS, 2 * D_FF), 0.01),
        'w_e2': nrm((L, N_EXPERTS, D_FF, D_MODEL), D_FF ** -0.5),
        'b_e2': nrm((L, N_EXPERTS, D_MODEL), 0.01),
        'norm_final': gain((D_MODEL,)),
    }

def reference(x_prompt, x_sample, state_gdn, state_conv, cache_latent, cache_krope, page_table,
              cache_mem_k, cache_mem_v, mem_prompt, norm_mix, w_in, conv_w, a_log, dt_bias, gdn_norm,
              q_norm, w_uq, kv_norm, w_uk, w_uv, w_out, norm_x, mem_norm, w_xq, w_xk, w_xv, w_xo,
              norm_ffn, w_router, b_router, w_e1, b_e1, w_e2, b_e2, norm_final):
    hp, hs = x_prompt, x_sample
    gdn_p, conv_p, lat_p, kpe_p, mk_p, mv_p = [], [], [], [], [], []
    gdn_s, conv_s, lat_s, kpe_s = [], [], [], []
    for layer in range(DEPTH):
        shared = (norm_mix[layer], w_in[layer], conv_w[layer], a_log[layer], dt_bias[layer], gdn_norm[layer],
                  q_norm[layer], w_uq[layer], kv_norm[layer], w_uk[layer], w_uv[layer], w_out[layer],
                  norm_x[layer], w_xq[layer], w_xo[layer], norm_ffn[layer], w_router[layer], b_router[layer],
                  w_e1[layer], b_e1[layer], w_e2[layer], b_e2[layer])
        hp, s1, c1, lt1, kp1, mk1, mv1 = prompt_layer(hp, mem_prompt, mem_norm[layer], w_xk[layer], w_xv[layer], *shared)
        gdn_p.append(s1)
        conv_p.append(c1)
        lat_p.append(lt1)
        kpe_p.append(kp1)
        mk_p.append(mk1)
        mv_p.append(mv1)
        hs, s2, c2, lt2, kp2 = sample_layer(hs, layer, state_gdn[layer], state_conv[layer], cache_latent, cache_krope,
                                            page_table, cache_mem_k[layer], cache_mem_v[layer], *shared)
        gdn_s.append(s2)
        conv_s.append(c2)
        lat_s.append(lt2)
        kpe_s.append(kp2)
    y_prompt = rms_norm(hp, norm_final)
    y_sample = rms_norm(hs, norm_final)
    return (y_prompt, y_sample,
            jnp.stack(gdn_p), jnp.stack(conv_p), jnp.stack(lat_p, axis=1), jnp.stack(kpe_p, axis=1),
            jnp.stack(mk_p), jnp.stack(mv_p),
            jnp.stack(gdn_s), jnp.stack(conv_s), jnp.stack(lat_s, axis=1), jnp.stack(kpe_s, axis=1))


_drawn_inputs = setup_inputs


def setup_inputs(seed=0):
    import zlib

    import numpy as np

    out = dict(_drawn_inputs(seed))
    spreads = {}
    factors = {'cache_krope': 4.088,
     'q_norm': 2.891,
     'kv_norm': 2.883,
     'norm_x': 4.506,
     'mem_norm': 2.907,
     'b_e1': 8.0,
     'b_e2': 8.0,
     'norm_final': 2.957}
    for name, (base, spread) in spreads.items():
        noise = np.random.default_rng([zlib.crc32(name.encode()), seed]).standard_normal(out[name].shape)
        drawn = base * np.exp(spread * noise) if base else spread * noise
        out[name] = jnp.asarray(drawn.astype(out[name].dtype))
    for name, factor in factors.items():
        out[name] = (out[name] * factor).astype(out[name].dtype)
    return out
```

```python
from contextlib import ExitStack

import numpy as np

import concourse.bass as bass
from concourse import mybir

F32 = mybir.dt.float32
BF16 = mybir.dt.bfloat16
I32 = mybir.dt.int32
ALU = mybir.AluOpType
ACT = mybir.ActivationFunctionType
AX = mybir.AxisListType.X

P = 128
D = 1024
KD = D // P
SEQ, DEC = 256, 8
TOK = SEQ + DEC
NT = 3
ROWS = (P, P, DEC)
H = 4
CHUNK = 64
CONV = 1536
CB = CONV // P
TAPS = 4
REST = 1224
Z0, B0, A0, CQ0, CKV0, KR0 = 0, 512, 516, 520, 904, 1160
IN_COLS = CONV + REST
QR, KVR, ROPE, NOPE = 384, 256, 64, 128
QK = NOPE + ROPE
PAST, PAGE = 2048, 128
NPAGE = PAST // PAGE
MLA_SCALE = QK ** -0.5
XD = 256
MEM = 256
NE, TOPK = 32, 4
SLOTS = 64
EPS = 1e-6
NEG = -1e30
LEVELS = 6

C_ID, C_ONE, C_TRI, C_BLK, C_LVL = 0, 128, 256, 384, 512
C_BEF = C_LVL + LEVELS * P
C_CAUS = C_BEF + P
C_IOTA = C_CAUS + P
C_CH2 = C_IOTA + SLOTS
C_SEQ = C_CH2 + 2
C_COS = C_SEQ + 2 * P
C_SIN = C_COS + NT * 32
C_ALL = C_SIN + NT * 32

V_CONV, V_MIX, V_MEM, V_X, V_FFN, V_Q, V_GDN, V_ALL = 0, 48, 56, 64, 72, 80, 83, 84


def constants():
    r = np.arange(P)
    row, col = r[:, None], r[None, :]
    c = np.zeros((P, C_ALL), np.float32)
    c[:, C_ID:C_ID + P] = row == col
    c[:, C_ONE:C_ONE + P] = 1.0
    same = row // CHUNK == col // CHUNK
    c[:, C_TRI:C_TRI + P] = (row <= col) & same
    c[:, C_BLK:C_BLK + P] = same
    for m in range(LEVELS):
        c[:, C_LVL + m * P:C_LVL + (m + 1) * P] = (row < col) & ((row ^ col) >> m == 1)
    c[:, C_BEF:C_BEF + P] = row < col
    c[:, C_CAUS:C_CAUS + P] = np.where(col <= row, 0.0, NEG)
    c[:, C_IOTA:C_IOTA + SLOTS] = np.arange(SLOTS)[None, :]
    c[:, C_CH2:C_CH2 + 2] = row // CHUNK == np.arange(2)[None, :]
    for g in range(2):
        c[:, C_SEQ + g * P:C_SEQ + (g + 1) * P] = row == 4 * g + col // 32
    half = ROPE // 2
    freq = (1.0 / (np.float32(10000.0) ** (np.arange(half, dtype=np.float32) / np.float32(half)))).astype(np.float32)
    for t in range(NT):
        pos = (t * P + r if t < 2 else np.full(P, PAST)).astype(np.float32)
        ang = (pos[:, None] * freq[None, :]).astype(np.float32)
        c[:, C_COS + 32 * t:C_COS + 32 * (t + 1)] = np.cos(ang)
        c[:, C_SIN + 32 * t:C_SIN + 32 * (t + 1)] = np.sin(ang)
    sel = np.repeat(np.tile(np.eye(NE, dtype=np.float32), (3, 1)), SLOTS, axis=1)
    return c, sel.astype("bfloat16")


class Chain:

    def __init__(self, sem):
        self.sem, self.n = sem, 0

    def link(self, eng, ins):
        self.n += 1
        ins.then_inc(self.sem, 1)
        eng.wait_ge(self.sem, self.n)


def rep(ap, shape):
    return ap.unsqueeze(len(ap.shape)).broadcast_to(shape)


def rep1(ap, shape):
    return ap.unsqueeze(1).broadcast_to(shape)


def cols(t):
    return slice(t * P, t * P + ROWS[t])


def build(nc, x_prompt, x_sample, state_gdn, state_conv, cache_latent, cache_krope, page_table,
          cache_mem_k, cache_mem_v, mem_prompt, norm_mix, w_in, conv_w, a_log, dt_bias, gdn_norm,
          q_norm, w_uq, kv_norm, w_uk, w_uv, w_out, norm_x, mem_norm, w_xq, w_xk, w_xv, w_xo,
          norm_ffn, w_router, b_router, w_e1, b_e1, w_e2, b_e2, norm_final, const_f32, const_bf16,
          y_prompt, y_sample, gdn_prompt, conv_prompt, lat_prompt, kr_prompt, memk_prompt,
          memv_prompt, gdn_sample, conv_sample, lat_sample, kr_sample):
    ctx = ExitStack()

    recent = []

    def sem(name, lasting=False):
        s = nc.alloc_semaphore(name)
        if not lasting:
            recent.append(s)
        return s

    def clear_semaphores():
        nc.clear_and_free_semaphores(list(recent))
        nc.all_engine_barrier()
        recent.clear()

    def keep(name, shape, dt=F32):
        return nc.alloc_sbuf_tensor(name, shape, dt)

    cst = keep("cst", [P, C_ALL])
    vec = keep("vec", [P, V_ALL])
    res = keep("res", [P, NT, D])
    xnT = keep("xnT", [P, KD, TOK])
    W = keep("W", [P, 24576])
    small = keep("small", [P, 64])
    ps = nc.alloc_psum_tensor("ps", [P, 8, 512], F32)

    def c_(at, n=P, rows=P):
        return cst[0:rows, at:at + n]

    ident = c_(C_ID)
    dve_chain, act_chain, pool_chain = (Chain(sem(n, True)) for n in ("dve_steps", "act_steps", "pool_steps"))
    stored = sem("outputs_stored", True)
    n_stored = [0]

    def store(eng, dst, src):
        n_stored[0] += 16
        eng.dma_start(dst, src).then_inc(stored, 16)

    const_loaded, x_loaded, vec_loaded = sem("const_loaded"), sem("x_loaded", True), sem("vec_loaded")
    vec_turned = sem("vec_turned")
    w_in_loaded = sem("w_in_loaded")
    win = W[:, 0:KD * IN_COLS].rearrange("p (k n) -> p k n", k=KD)
    with ExitStack() as scope, nc.Block() as block:
        vrow = scope.enter_context(nc.sbuf_tensor("vrow", [V_ALL, P], F32))

        @block.sync
        def _(sp):
            sp.dma_start(res[:, 0:2, :], x_prompt[0].rearrange("(t p) d -> p t d", p=P)).then_inc(x_loaded, 16)
            sp.dma_start(res[0:DEC, 2, :], x_sample[:, 0, :]).then_inc(x_loaded, 16)
            for k in range(KD):
                sp.dma_start(win[:, k, :], w_in[0, k * P:(k + 1) * P, :]).then_inc(w_in_loaded, 16)

        @block.scalar
        def _(act):
            act.dma_start(cst[:, :], const_f32).then_inc(const_loaded, 16)
            for at, v, n in ((V_MIX, norm_mix, KD), (V_MEM, mem_norm, KD), (V_X, norm_x, KD),
                             (V_FFN, norm_ffn, KD), (V_Q, q_norm, 3), (V_GDN, gdn_norm, 1)):
                act.dma_start(vrow[at:at + n, :], v[0].rearrange("(k p) -> k p", p=P)).then_inc(vec_loaded, 16)
            act.dma_start(vrow[V_CONV:V_MIX, :], conv_w[0].rearrange("j (c p) -> (j c) p", p=P)).then_inc(vec_loaded, 16)

        @block.tensor
        def _(pe):
            pe.wait_ge(const_loaded, 16)
            pe.wait_ge(vec_loaded, 7 * 16)
            pe.transpose(ps[:, 0, 0:V_ALL], vrow[:, :], c_(C_ID, V_ALL, V_ALL)).then_inc(vec_turned, 1)

        @block.vector
        def _(dve):
            dve.memset(small[:, :], 0.0)
            dve.wait_ge(vec_turned, 1)
            dve.tensor_copy(vec[:, :], ps[:, 0, 0:V_ALL])

    def normed_transposed(tag, src, tiles, gain_at, ready, ready_at, kept=None):
        squared, varied, rooted, scaled = (sem(f"{tag}_{n}") for n in ("squared", "varied", "rooted", "scaled"))
        turned, emptied = sem(f"{tag}_turned"), sem(f"{tag}_emptied")
        with ExitStack() as scope, nc.Block() as block:
            junk = scope.enter_context(nc.sbuf_tensor(f"{tag}_junk", [P, D], F32))
            xs = scope.enter_context(nc.sbuf_tensor(f"{tag}_xs", [P, 2, D], F32)) if kept is None else kept
            n = len(tiles)
            place = [i % 2 if kept is None else i for i in range(n)]

            @block.scalar
            def _(act):
                act.wait_ge(ready, ready_at)
                for t in tiles:
                    act_chain.link(act, nc.scalar.activation(junk[0:ROWS[t], :], src[0:ROWS[t], t, :], ACT.Square,
                                                            accum_out=small[0:ROWS[t], t:t + 1]))
                nc.scalar.copy(small[:, 3:4], small[:, 3:4]).then_inc(squared, 1)
                act.wait_ge(varied, 1)
                nc.scalar.activation(small[:, 4:4 + n], small[:, 4:4 + n], ACT.Sqrt).then_inc(rooted, 1)

            @block.vector
            def _(dve):
                dve.wait_ge(squared, 1)
                nc.vector.tensor_scalar(small[:, 4:4 + n], small[:, 0:n], 1.0 / D, EPS, ALU.mult, ALU.add).then_inc(varied, 1)
                dve.wait_ge(rooted, 1)
                dve_chain.link(dve, nc.vector.reciprocal(small[:, 8:8 + n], small[:, 4:4 + n]))
                for i, t in enumerate(tiles):
                    r = ROWS[t]
                    if i >= 2 and kept is None:
                        dve.wait_ge(turned, 2 * (i - 1))
                    nc.vector.tensor_scalar(xs[0:r, place[i], :], src[0:r, t, :], small[0:r, 8 + t:9 + t], None, ALU.mult).then_inc(scaled, 1)
                    for j in range(2):
                        dve.wait_ge(turned, 2 * i + j + 1)
                        nc.vector.tensor_tensor(xnT[:, 4 * j:4 * j + 4, cols(t)],
                                                ps[:, (2 * i + j) % 8, :].rearrange("p (k n) -> p k n", k=4)[:, :, 0:r],
                                                rep(vec[:, gain_at + 4 * j:gain_at + 4 * j + 4], [P, 4, r]), ALU.mult).then_inc(emptied, 1)

            @block.tensor
            def _(pe):
                for i, t in enumerate(tiles):
                    r = ROWS[t]
                    pe.wait_ge(scaled, i + 1)
                    for j in range(2):
                        for k in range(4):
                            last = pe.transpose(ps[:, (2 * i + j) % 8, k * P:k * P + r],
                                                xs[0:r, place[i], (4 * j + k) * P:(4 * j + k + 1) * P], c_(C_ID, r, r))
                        last.then_inc(turned, 1)

    normed_transposed("mix", res, (0, 1, 2), V_MIX, x_loaded, 32)

    heads_scope = ExitStack()
    take = lambda name, shape, dt=F32: heads_scope.enter_context(nc.sbuf_tensor(name, shape, dt))
    qkv = take("qkv", [P, CB, TOK])
    rest = take("rest", [P, NT, REST])
    yT = take("yT", [P, 2 * H, TOK])
    REST_CUTS = ((0, 512), (512, 904), (904, REST))
    conv_proj, conv_moved = sem("conv_projected"), sem("conv_moved")
    rest_proj, rest_moved = sem("rest_projected"), sem("rest_moved")
    hist_loaded, hist_turned = sem("history_loaded"), sem("history_turned")
    hist_moved = sem("history_moved")
    rest_cleared = sem("rest_cleared")
    tail_turned, tail_moved = sem("tail_turned"), sem("tail_moved")
    conv_done, sig_done = sem("conv_done"), sem("conv_sigmoid_done")
    with ExitStack() as scope, nc.Block() as block:
        cp = scope.enter_context(nc.sbuf_tensor("cp", [P, CB, SEQ + TAPS - 1], F32))
        cs = scope.enter_context(nc.sbuf_tensor("cs", [P, CB, DEC, TAPS], F32))
        hist = scope.enter_context(nc.sbuf_tensor("hist", [DEC * 3, CONV], F32))
        tail = scope.enter_context(nc.sbuf_tensor("tail", [3 + DEC, CONV], F32))
        tmp = scope.enter_context(nc.sbuf_tensor("cs_tmp", [P, CB, DEC], F32))
        win_sig = W[:, 0:CB * TOK].rearrange("p (c n) -> p c n", c=CB)

        @block.sync
        def _(sp):
            sp.dma_start(hist[:, :], state_conv[0].rearrange("b j c -> (b j) c")).then_inc(hist_loaded, 16)
            store(sp, conv_sample[0, :, 0:2, :], state_conv[0, :, 1:3, :])
            sp.wait_ge(tail_moved, 3)
            store(sp, conv_prompt[0, 0], tail[0:3, :])
            store(sp, conv_sample[0, :, 2, :], tail[3:3 + DEC, :])

        @block.tensor
        def _(pe):
            pe.wait_ge(hist_loaded, 16)
            for c in range(CB):
                last = pe.transpose(ps[:, 7, c * 24:(c + 1) * 24], hist[:, c * P:(c + 1) * P], c_(C_ID, 24, 24))
            last.then_inc(hist_turned, 1)
            pe.wait_ge(w_in_loaded, 16 * KD)
            for c in range(CB):
                if c >= 4:
                    pe.wait_ge(conv_moved, c - 3)
                for k in range(KD):
                    last = pe.matmul(ps[:, c % 4, 0:TOK], win[:, k, c * P:(c + 1) * P], xnT[:, k, :],
                                     start=(k == 0), stop=(k == KD - 1))
                last.then_inc(conv_proj, 1)
            n = 0
            for t in range(NT):
                for a, b in REST_CUTS:
                    if n >= 3:
                        pe.wait_ge(rest_moved, n - 2)
                    for k in range(KD):
                        last = pe.matmul(ps[0:ROWS[t], 4 + n % 3, 0:b - a], xnT[:, k, cols(t)],
                                         win[:, k, CONV + a:CONV + b], start=(k == 0), stop=(k == KD - 1))
                    last.then_inc(rest_proj, 1)
                    n += 1
            pe.wait_ge(conv_moved, CB)
            for j in range(3):
                for c in range(4):
                    last = pe.transpose(ps[0:3 + DEC, j, c * P:(c + 1) * P], qkv[:, 4 * j + c, SEQ - 3:TOK], ident)
                last.then_inc(tail_turned, 1)

        @block.vector
        def _(dve):
            nc.vector.memset(rest[:, 2, :], 0.0).then_inc(rest_cleared, 1)
            dve_chain.link(dve, nc.vector.memset(cp[:, :, 0:TAPS - 1], 0.0))
            dve.wait_ge(hist_turned, 1)
            nc.vector.tensor_copy(cs[:, :, :, 0:3], ps[:, 7, 0:CB * 24].rearrange("p (c b j) -> p c b j", c=CB, j=3)).then_inc(hist_moved, 1)
            for c in range(CB):
                dve.wait_ge(conv_proj, c + 1)
                dve_chain.link(dve, nc.vector.tensor_copy(qkv[:, c, :], ps[:, c % 4, 0:TOK]))
                nc.vector.tensor_copy(cs[:, c, :, 3], qkv[:, c, SEQ:TOK])
                nc.vector.tensor_copy(cp[:, c, 3:3 + SEQ], qkv[:, c, 0:SEQ]).then_inc(conv_moved, 1)
            for j in range(3):
                dve.wait_ge(tail_turned, j + 1)
                nc.vector.tensor_copy(tail[:, 4 * P * j:4 * P * (j + 1)], ps[0:3 + DEC, j, :]).then_inc(tail_moved, 1)
            dve.wait_ge(conv_moved, CB)
            dve.wait_ge(hist_moved, 1)
            for j in range(TAPS):
                for c in range(CB):
                    w = vec[:, V_CONV + CB * j + c:V_CONV + CB * j + c + 1]
                    if j == 0:
                        last = nc.vector.tensor_scalar(qkv[:, c, 0:SEQ], cp[:, c, j:j + SEQ], w, None, ALU.mult)
                    else:
                        last = nc.vector.scalar_tensor_tensor(qkv[:, c, 0:SEQ], cp[:, c, j:j + SEQ], w, qkv[:, c, 0:SEQ], ALU.mult, ALU.add)
                w = rep(vec[:, V_CONV + CB * j:V_CONV + CB * (j + 1)], [P, CB, DEC])
                if j == 0:
                    dve_chain.link(dve, nc.vector.tensor_tensor(qkv[:, :, SEQ:TOK], cs[:, :, :, 0], w, ALU.mult))
                else:
                    dve_chain.link(dve, nc.vector.tensor_tensor(tmp[:, :, :], cs[:, :, :, j], w, ALU.mult))
                    dve_chain.link(dve, nc.vector.tensor_tensor(qkv[:, :, SEQ:TOK], qkv[:, :, SEQ:TOK], tmp[:, :, :], ALU.add))
            nc.vector.tensor_copy(small[:, 63:64], small[:, 62:63]).then_inc(conv_done, 1)
            dve.wait_ge(sig_done, 1)
            nc.vector.tensor_tensor(qkv[:, :, 0:TOK], qkv[:, :, 0:TOK], win_sig[:, :, :], ALU.mult)

        @block.scalar
        def _(act):
            act.wait_ge(rest_cleared, 1)
            n = 0
            for t in range(NT):
                for a, b in REST_CUTS:
                    act.wait_ge(rest_proj, n + 1)
                    nc.scalar.copy(rest[0:ROWS[t], t, a:b], ps[0:ROWS[t], 4 + n % 3, 0:b - a]).then_inc(rest_moved, 1)
                    n += 1
            act.wait_ge(conv_done, 1)
            nc.scalar.activation(win_sig[:, :, :], qkv[:, :, :], ACT.Sigmoid).then_inc(sig_done, 1)
    gdn_scope = ExitStack()
    gtake = lambda name, shape, dt=F32: gdn_scope.enter_context(nc.sbuf_tensor(name, shape, dt))
    S = gtake("S", [P, H, P])
    otok = gtake("otok", [P, NT, H, P])
    sq = gtake("sq", [P, 2 * H, TOK])
    gsb = gtake("gsb", [P, 104])
    eg = gtake("eg", [P, 104])
    gw = gtake("gw", [P, 8, NT * H])
    alog = gtake("alog", [P, H])
    dtb = gtake("dtb", [P, H])
    G_CUM, G_TOT, G_CH, G_SMP, G_BSMP, G_LEFT = 0, 8, 16, 32, 64, 96
    views = [W[:, i * 1024:(i + 1) * 1024].rearrange("p (t h n) -> p t h n", t=2, h=H) for i in range(14)]
    qTe, decT, LT, iT, kbe, kd, vb, X, XT, Y, CT, u, wT, vnew = views
    st = W[:, 14336:14336 + DEC * H * P].rearrange("p (s n) -> p s n", n=P)
    delta = W[0:DEC, 18432:18432 + H * DEC * P].rearrange("p (h b n) -> p h b n", h=H, b=DEC)
    g, beta = gw[:, 6, :].rearrange("p (t h) -> p t h", h=H), gw[:, 7, :].rearrange("p (t h) -> p t h", h=H)
    state_loaded = sem("state_loaded")
    decay_loaded = sem("decay_loaded")
    g1 = {n: sem("gdn_" + n) for n in (
        "squared", "summed", "added", "rooted", "normed", "neg_abs", "exp", "plus1", "ln", "gates", "sums", "sums_read",
        "exp_sums", "rows_exp", "row_min", "dec_exp", "turned", "turned_read", "products", "left", "rows_read", "rows_beta_read")}
    with nc.Block() as block:
        @block.sync
        def _(sp):
            sp.dma_start(alog[:, :], a_log[0].partition_broadcast(P)).then_inc(decay_loaded, 16)
            sp.dma_start(dtb[:, :], dt_bias[0].partition_broadcast(P)).then_inc(decay_loaded, 16)
            sp.dma_start(st[:, :, :], state_gdn[0].rearrange("b h k v -> k (b h) v")).then_inc(state_loaded, 16)

        @block.scalar
        def _(act):
            nc.scalar.activation(sq[:, :, :], qkv[:, 0:2 * H, :], ACT.Square).then_inc(g1["squared"], 1)
            act.wait_ge(g1["added"], 1)
            nc.scalar.activation(sq[:, :, :], sq[:, :, :], ACT.Sqrt).then_inc(g1["rooted"], 1)
            act.wait_ge(decay_loaded, 32)
            nc.scalar.activation(alog[:, :], alog[:, :], ACT.Exp)
            nc.scalar.activation(gw[:, 4, :].rearrange("p (t h) -> p t h", h=H), rest[:, :, B0:B0 + H], ACT.Exp, scale=-1.0)
            act.wait_ge(g1["neg_abs"], 1)
            nc.scalar.activation(gw[:, 2, :], gw[:, 1, :], ACT.Exp).then_inc(g1["exp"], 1)
            act.wait_ge(g1["plus1"], 1)
            nc.scalar.activation(gw[:, 3, :], gw[:, 2, :], ACT.Ln).then_inc(g1["ln"], 1)
            act.wait_ge(g1["sums"], 1)
            for t in range(2):
                nc.scalar.activation(qTe[:, t].rearrange("p h n -> p (h n)"), ps[:, 1 + t, :], ACT.Exp).then_inc(g1["rows_exp"], 1)
            act.wait_ge(g1["sums_read"], 1)
            nc.scalar.activation(eg[:, :], gsb[:, :], ACT.Exp).then_inc(g1["exp_sums"], 1)
            act.wait_ge(g1["row_min"], 1)
            nc.scalar.activation(decT[:, :, :, :], decT[:, :, :, :], ACT.Exp).then_inc(g1["dec_exp"], 1)

        @block.vector
        def _(dve):
            link = lambda ins: dve_chain.link(dve, ins)
            dve.wait_ge(g1["summed"], 1)
            nc.vector.tensor_scalar(sq[:, 0:H, :], ps[:, 0:H, 0:TOK], EPS, float(P), ALU.add, ALU.mult)
            nc.vector.tensor_scalar(sq[:, H:2 * H, :], ps[:, H:2 * H, 0:TOK], EPS, None, ALU.add).then_inc(g1["added"], 1)
            dve.wait_ge(decay_loaded, 32)
            a3 = gw[:, 0, :].rearrange("p (t h) -> p t h", h=H)
            link(nc.vector.tensor_tensor(a3, rest[:, :, A0:A0 + H], rep1(dtb[:, :], [P, NT, H]), ALU.add))
            link(nc.vector.tensor_scalar(gw[:, 1, :], gw[:, 0, :], -1.0, None, ALU.mult))
            nc.vector.tensor_tensor(gw[:, 1, :], gw[:, 1, :], gw[:, 0, :], ALU.min).then_inc(g1["neg_abs"], 1)
            dve.wait_ge(g1["exp"], 1)
            nc.vector.tensor_scalar(gw[:, 2, :], gw[:, 2, :], 1.0, None, ALU.add).then_inc(g1["plus1"], 1)
            link(nc.vector.tensor_scalar(gw[:, 4, :], gw[:, 4, :], 1.0, None, ALU.add))
            link(nc.vector.reciprocal(gw[:, 7, :], gw[:, 4, :]))
            dve.wait_ge(g1["ln"], 1)
            link(nc.vector.scalar_tensor_tensor(gw[:, 5, :], gw[:, 0, :], 0.0, gw[:, 3, :], ALU.max, ALU.add))
            nc.vector.scalar_tensor_tensor(g, gw[:, 5, :].rearrange("p (t h) -> p t h", h=H), -1.0,
                                           rep1(alog[:, :], [P, NT, H]), ALU.mult, ALU.mult).then_inc(g1["gates"], 1)
            dve.wait_ge(g1["rooted"], 1)
            link(nc.vector.reciprocal(sq[:, :, :], sq[:, :, :]))
            nc.vector.tensor_tensor(qkv[:, 0:2 * H, :], qkv[:, 0:2 * H, :], sq[:, :, :], ALU.mult).then_inc(g1["normed"], 1)
            dve.wait_ge(g1["sums"], 1)
            link(nc.vector.tensor_copy(gsb[:, 0:96], ps[:, 0, 0:96]))
            link(nc.vector.tensor_tensor(gsb[:, G_LEFT:G_LEFT + 8], gsb[:, G_TOT:G_TOT + 8], gsb[:, 0:8], ALU.subtract))
            nc.vector.tensor_copy(small[:, 62:63], gsb[:, 0:1]).then_inc(g1["sums_read"], 1)
            dve.wait_ge(g1["rows_exp"], 2)
            for t in range(2):
                link(nc.vector.tensor_tensor(decT[:, t], ps[:, 1 + t, :].rearrange("p (h n) -> p h n", h=H),
                                             rep(gsb[:, 4 * t:4 * t + 4], [P, H, P]), ALU.subtract))
            nc.vector.tensor_scalar(decT[:, :, :, :], decT[:, :, :, :], 0.0, None, ALU.min).then_inc(g1["row_min"], 1)
            dve.wait_ge(g1["normed"], 1)
            for t in range(2):
                nc.vector.tensor_tensor(qTe[:, t], qTe[:, t], qkv[:, 0:H, cols(t)], ALU.mult)
            dve.wait_ge(g1["exp_sums"], 1)
            link(nc.vector.tensor_tensor(gw[:, 0, 0:8], gw[:, 7, 0:8], eg[:, 0:8], ALU.mult))
            dve.wait_ge(g1["dec_exp"], 1)
            link(nc.vector.tensor_tensor(decT[:, :, :, :].rearrange("p t h n -> p (t h) n"), decT[:, :, :, :].rearrange("p t h n -> p (t h) n"),
                                         rep1(c_(C_TRI), [P, 2 * H, P]), ALU.mult))
            for t in range(2):
                link(nc.vector.tensor_tensor(LT[:, t], decT[:, t], ps[:, 3 + t, :].rearrange("p (h n) -> p h n", h=H), ALU.mult))
            nc.vector.tensor_copy(small[:, 62:63], gsb[:, 0:1]).then_inc(g1["rows_read"], 1)
            dve.wait_ge(g1["turned"], 1)
            for t in range(2):
                kt = ps[:, 5 + t, :].rearrange("p (h n) -> p h n", h=H)
                vt = ps[:, (7 + t) % 8, :].rearrange("p (h n) -> p h n", h=H)
                nc.vector.tensor_tensor(kbe[:, t], kt, rep(gw[:, 0, 4 * t:4 * t + 4], [P, H, P]), ALU.mult)
                nc.vector.tensor_tensor(kd[:, t], kt, rep(eg[:, G_LEFT + 4 * t:G_LEFT + 4 * t + 4], [P, H, P]), ALU.mult)
                nc.vector.tensor_tensor(vb[:, t], vt, rep(gw[:, 7, 4 * t:4 * t + 4], [P, H, P]), ALU.mult)
            dve.wait_ge(g1["products"], 1)
            for t in range(2):
                nc.vector.tensor_tensor(LT[:, t], LT[:, t], ps[:, 1 + t, :].rearrange("p (h n) -> p h n", h=H), ALU.mult)
                nc.vector.tensor_tensor(iT[:, t], decT[:, t], ps[:, 3 + t, :].rearrange("p (h n) -> p h n", h=H), ALU.mult)

        @block.tensor
        def _(pe):
            pe.wait_ge(g1["squared"], 1)
            for c in range(2 * H):
                last = pe.matmul(ps[:, c, 0:TOK], c_(C_ONE), sq[:, c, :], start=True, stop=True)
            last.then_inc(g1["summed"], 1)
            pe.wait_ge(g1["added"], 1)
            pe.wait_ge(g1["gates"], 1)
            for t in range(2):
                pe.matmul(ps[:, 0, 4 * t:4 * t + 4], c_(C_TRI), g[:, t, :], start=True, stop=True)
                pe.matmul(ps[:, 0, 8 + 4 * t:12 + 4 * t], c_(C_BLK), g[:, t, :], start=True, stop=True)
                for h in range(H):
                    gcol = g[:, t, h:h + 1].broadcast_to([P, P])
                    a = G_CH + 2 * (4 * t + h)
                    pe.matmul(ps[:, 0, a:a + 2], gcol, c_(C_CH2, 2), start=True, stop=True)
                    pe.matmul(ps[:, 1 + t, h * P:(h + 1) * P], gcol, c_(C_TRI), start=True, stop=True)
                    pe.matmul(ps[:, 3 + t, h * P:(h + 1) * P], beta[:, t, h:h + 1].broadcast_to([P, P]), ident, start=True, stop=True)
            for h in range(H):
                i8 = c_(C_ID, DEC, DEC)
                pe.matmul(ps[:, 0, G_SMP + 8 * h:G_SMP + 8 * h + 8], g[0:DEC, 2, h:h + 1].broadcast_to([DEC, P]), i8, start=True, stop=True)
                last = pe.matmul(ps[:, 0, G_BSMP + 8 * h:G_BSMP + 8 * h + 8], beta[0:DEC, 2, h:h + 1].broadcast_to([DEC, P]), i8, start=True, stop=True)
            last.then_inc(g1["sums"], 1)
            pe.wait_ge(g1["normed"], 1)
            pe.wait_ge(g1["sums_read"], 1)
            for t in range(2):
                for h in range(H):
                    pe.transpose(ps[:, 5 + t, h * P:(h + 1) * P], qkv[:, H + h, cols(t)], ident)
                    last = pe.transpose(ps[:, (7 + t) % 8, h * P:(h + 1) * P], qkv[:, 2 * H + h, cols(t)], ident)
            last.then_inc(g1["turned"], 1)
            pe.wait_ge(g1["rows_exp"], 2)
            pe.wait_ge(g1["rows_read"], 1)
            for t in range(2):
                for h in range(H):
                    pe.matmul(ps[:, 1 + t, h * P:(h + 1) * P], qkv[:, H + h, cols(t)], qkv[:, H + h, cols(t)], start=True, stop=True)
                    last = pe.matmul(ps[:, 3 + t, h * P:(h + 1) * P], qkv[:, H + h, cols(t)], qkv[:, h, cols(t)], start=True, stop=True)
            last.then_inc(g1["products"], 1)

    x0, x_turned, x_ready = sem("inv_first"), sem("inv_turned"), sem("inv_x_ready")
    c_ready, y_made, y_moved, z_made = sem("inv_c_ready"), sem("inv_y_made"), sem("inv_y_moved"), sem("inv_z_made")
    uw_made = sem("uw_made")
    with nc.Block() as block:
        def level(m):
            return rep1(c_(C_LVL + m * P), [P, H, P])

        @block.vector
        def _(dve):
            link = lambda ins: dve_chain.link(dve, ins)
            for t in range(2):
                link(nc.vector.tensor_tensor(CT[:, t], LT[:, t], level(0), ALU.mult))
                nc.vector.tensor_tensor(XT[:, t], rep1(ident, [P, H, P]), CT[:, t], ALU.subtract).then_inc(x0, 1)
            for t in range(2):
                dve.wait_ge(x_turned, t + 1)
                nc.vector.tensor_copy(X[:, t], ps[:, 6 + t, :].rearrange("p (h n) -> p h n", h=H)).then_inc(x_ready, 1)
            for m in range(1, LEVELS):
                for t in range(2):
                    if m > 1:
                        dve.wait_ge(y_made, 2 * (m - 2) + t + 1)
                    nc.vector.tensor_tensor(CT[:, t], LT[:, t], level(m), ALU.mult).then_inc(c_ready, 1)
                for t in range(2):
                    dve.wait_ge(z_made, 2 * (m - 1) + t + 1)
                    nc.vector.tensor_tensor(X[:, t], X[:, t], ps[:, 2 + t, :].rearrange("p (h n) -> p h n", h=H), ALU.subtract)
                    nc.vector.tensor_tensor(XT[:, t], XT[:, t], ps[:, 4 + t, :].rearrange("p (h n) -> p h n", h=H), ALU.subtract).then_inc(x_ready, 1)
            for t in range(2):
                dve.wait_ge(uw_made, t + 1)
                nc.vector.tensor_copy(u[:, t], ps[:, 6 + t, :].rearrange("p (h n) -> p h n", h=H))
                nc.vector.tensor_copy(wT[:, t], ps[:, t, :].rearrange("p (h n) -> p h n", h=H))

        @block.scalar
        def _(act):
            for m in range(1, LEVELS):
                for t in range(2):
                    act.wait_ge(y_made, 2 * (m - 1) + t + 1)
                    nc.scalar.copy(Y[:, t], ps[:, t, :].rearrange("p (h n) -> p h n", h=H)).then_inc(y_moved, 1)

        @block.tensor
        def _(pe):
            for t in range(2):
                pe.wait_ge(x0, t + 1)
                for h in range(H):
                    last = pe.transpose(ps[:, 6 + t, h * P:(h + 1) * P], XT[:, t, h, :], ident)
                last.then_inc(x_turned, 1)
            for m in range(1, LEVELS):
                for t in range(2):
                    pe.wait_ge(c_ready, 2 * (m - 1) + t + 1)
                    pe.wait_ge(x_ready, 2 * (m - 1) + t + 1)
                    for h in range(H):
                        last = pe.matmul(ps[:, t, h * P:(h + 1) * P], CT[:, t, h, :], X[:, t, h, :], start=True, stop=True)
                    last.then_inc(y_made, 1)
                for t in range(2):
                    pe.wait_ge(y_moved, 2 * (m - 1) + t + 1)
                    for h in range(H):
                        pe.matmul(ps[:, 2 + t, h * P:(h + 1) * P], XT[:, t, h, :], Y[:, t, h, :], start=True, stop=True)
                        last = pe.matmul(ps[:, 4 + t, h * P:(h + 1) * P], Y[:, t, h, :], XT[:, t, h, :], start=True, stop=True)
                    last.then_inc(z_made, 1)
            for t in range(2):
                pe.wait_ge(x_ready, 2 * (LEVELS - 1) + t + 1)
                for h in range(H):
                    pe.matmul(ps[:, 6 + t, h * P:(h + 1) * P], XT[:, t, h, :], vb[:, t, h, :], start=True, stop=True)
                    last = pe.matmul(ps[:, t, h * P:(h + 1) * P], kbe[:, t, h, :], XT[:, t, h, :], start=True, stop=True)
                last.then_inc(uw_made, 1)

    NC = SEQ // CHUNK
    seen, v_ready, add_made, s_ready, o_made = (sem(n) for n in ("scan_seen", "scan_v_ready", "scan_add_made", "scan_s_ready", "scan_o_made"))
    with nc.Block() as block:
        @block.vector
        def _(dve):
            for i in range(NC):
                t, r = i // 2, CHUNK * (i % 2)
                rows = slice(r, r + CHUNK)
                if i == 0:
                    nc.vector.tensor_copy(vnew[rows, t], u[rows, t]).then_inc(v_ready, 1)
                else:
                    dve.wait_ge(seen, i)
                    nc.vector.tensor_tensor(vnew[rows, t], u[rows, t], ps[rows, i % 2, :].rearrange("p (h n) -> p h n", h=H), ALU.subtract).then_inc(v_ready, 1)
                dve.wait_ge(add_made, i + 1)
                for h in range(H):
                    made = ps[:, 2 + i % 2, h * P:(h + 1) * P]
                    a = G_CH + 2 * (4 * t + h) + i % 2
                    if i == 0:
                        last = nc.vector.tensor_copy(S[:, h, :], made)
                    else:
                        last = nc.vector.scalar_tensor_tensor(S[:, h, :], S[:, h, :], eg[:, a:a + 1], made, ALU.mult, ALU.add)
                last.then_inc(s_ready, 1)
            for t in range(2):
                dve.wait_ge(o_made, t + 1)
                dve_chain.link(dve, nc.vector.tensor_copy(otok[:, t], ps[:, 6 + t, :].rearrange("p (h n) -> p h n", h=H)))
                rows = slice(CHUNK if t == 0 else 0, P)
                nc.vector.tensor_tensor(otok[rows, t], otok[rows, t], ps[rows, 4 + t, :].rearrange("p (h n) -> p h n", h=H), ALU.add)

        @block.tensor
        def _(pe):
            for i in range(NC):
                t, r = i // 2, CHUNK * (i % 2)
                rows = slice(r, r + CHUNK)
                if i > 0:
                    pe.wait_ge(s_ready, i)
                    for h in range(H):
                        last = pe.matmul(ps[rows, i % 2, h * P:(h + 1) * P], wT[:, t, h, rows], S[:, h, :], start=True, stop=True)
                    last.then_inc(seen, 1)
                    for h in range(H):
                        pe.matmul(ps[rows, 4 + t, h * P:(h + 1) * P], qTe[:, t, h, rows], S[:, h, :], start=True, stop=True)
                pe.wait_ge(v_ready, i + 1)
                for h in range(H):
                    last = pe.matmul(ps[:, 2 + i % 2, h * P:(h + 1) * P], kd[rows, t, h, :], vnew[rows, t, h, :], start=True, stop=True)
                last.then_inc(add_made, 1)
            for t in range(2):
                for h in range(H):
                    last = pe.matmul(ps[:, 6 + t, h * P:(h + 1) * P], iT[:, t, h, :], vnew[:, t, h, :], start=True, stop=True)
                last.then_inc(o_made, 1)

    sm = {n: sem("smp_" + n) for n in ("prod", "seen", "delta", "turned", "blocks", "outer", "updated", "o_ready", "moved")}
    kts = gtake("kts", [DEC, H, P])
    dts = gtake("dts", [DEC, H, P])
    dT = gtake("dT", [P, H, DEC])
    oT = gtake("oT", [P, H, DEC])
    pr = gtake("pr", [P, H, DEC])
    with nc.Block() as block:
        @block.sync
        def _(sp):
            store(sp, gdn_prompt[0, 0].rearrange("h k v -> k h v"), S[:, :, :])
            sp.wait_ge(sm["updated"], H)
            store(sp, gdn_sample[0].rearrange("b h k v -> k (b h) v"), st[:, :, :])

        @block.vector
        def _(dve):
            link = lambda ins: dve_chain.link(dve, ins)
            q_s, k_s, v_s = (qkv[:, i * H:(i + 1) * H, SEQ:TOK] for i in range(3))
            egs = eg[:, G_SMP:G_SMP + 32].rearrange("p (h b) -> p h b", h=H)
            bs = gsb[:, G_BSMP:G_BSMP + 32].rearrange("p (h b) -> p h b", h=H)
            nc.vector.memset(otok[:, 2], 0.0)
            nc.vector.tensor_tensor(pr[:, :, :], q_s, k_s, ALU.mult).then_inc(sm["prod"], 1)
            dve.wait_ge(sm["seen"], 1)
            sqk = ps[:, 0, 0:64].rearrange("p (h b j) -> p h b j", h=H, j=2)
            link(nc.vector.tensor_tensor(dT[:, :, :], sqk[:, :, :, 1], egs, ALU.mult))
            link(nc.vector.tensor_tensor(dT[:, :, :], v_s, dT[:, :, :], ALU.subtract))
            link(nc.vector.tensor_tensor(dT[:, :, :], dT[:, :, :], bs, ALU.mult))
            link(nc.vector.tensor_tensor(pr[:, :, :], dT[:, :, :], ps[:, 0, 64:96].rearrange("p (h b) -> p h b", h=H), ALU.mult))
            link(nc.vector.tensor_tensor(oT[:, :, :], sqk[:, :, :, 0], egs, ALU.mult))
            nc.vector.tensor_tensor(oT[:, :, :], oT[:, :, :], pr[:, :, :], ALU.add).then_inc(sm["delta"], 1)
            dve.wait_ge(sm["turned"], 1)
            nc.vector.tensor_copy(kts[:, :, :], ps[0:DEC, 1, :].rearrange("p (h n) -> p h n", h=H))
            link(nc.vector.tensor_copy(dts[:, :, :], ps[0:DEC, 2, :].rearrange("p (h n) -> p h n", h=H)))
            nc.vector.tensor_copy(otok[0:DEC, 2], ps[0:DEC, 3, :].rearrange("p (h n) -> p h n", h=H))
            for h in range(H):
                nc.vector.tensor_tensor(delta[:, h], rep1(dts[:, h, :], [DEC, DEC, P]), rep(c_(C_ID, DEC, DEC), [DEC, DEC, P]), ALU.mult).then_inc(sm["blocks"], 1)
            for h in range(H):
                dve.wait_ge(sm["outer"], h + 1)
                for b in range(DEC):
                    s = st[:, b * H + h, :]
                    last = nc.vector.scalar_tensor_tensor(s, s, eg[:, G_SMP + 8 * h + b:G_SMP + 8 * h + b + 1],
                                                          ps[:, 4 + 2 * (h % 2) + b // 4, (b % 4) * P:(b % 4 + 1) * P], ALU.mult, ALU.add)
                last.then_inc(sm["updated"], 1)

        @block.tensor
        def _(pe):
            pe.wait_ge(state_loaded, 16)
            for h in range(H):
                for b in range(DEC):
                    a = 2 * (h * DEC + b)
                    pe.matmul(ps[:, 0, a:a + 2], st[:, b * H + h, :], qkv[:, h:h + 5:4, SEQ + b], start=True, stop=True)
            pe.wait_ge(sm["prod"], 1)
            pe.matmul(ps[:, 0, 64:96], c_(C_ONE), pr[:, :, :], start=True, stop=True).then_inc(sm["seen"], 1)
            pe.wait_ge(sm["delta"], 1)
            for h in range(H):
                pe.transpose(ps[0:DEC, 1, h * P:(h + 1) * P], qkv[:, H + h, SEQ:TOK], ident)
                pe.transpose(ps[0:DEC, 2, h * P:(h + 1) * P], dT[:, h, :], ident)
                last = pe.transpose(ps[0:DEC, 3, h * P:(h + 1) * P], oT[:, h, :], ident)
            last.then_inc(sm["turned"], 1)
            for h in range(H):
                pe.wait_ge(sm["blocks"], h + 1)
                if h >= 2:
                    pe.wait_ge(sm["updated"], h - 1)
                for j in range(2):
                    last = pe.matmul(ps[:, 4 + 2 * (h % 2) + j, :], kts[:, h, :], delta[:, h, 4 * j:4 * j + 4, :], start=True, stop=True)
                last.then_inc(sm["outer"], 1)

    gn = {n: sem("gnorm_" + n) for n in ("sig", "sq", "var", "root", "ready", "turned")}
    with ExitStack() as scope, nc.Block() as block:
        sig = scope.enter_context(nc.sbuf_tensor("gate", [P, NT, H * P], F32))
        osq = W[:, 0:NT * H * P].rearrange("p (a n) -> p a n", n=P)
        o3 = otok[:, :, :, :].rearrange("p t h n -> p (t h) n")

        @block.scalar
        def _(act):
            nc.scalar.activation(sig[:, :, :], rest[:, :, Z0:Z0 + H * P], ACT.Sigmoid).then_inc(gn["sig"], 1)
            act.wait_ge(gn["var"], 1)
            nc.scalar.activation(gw[:, 1, :], gw[:, 1, :], ACT.Sqrt).then_inc(gn["root"], 1)

        @block.vector
        def _(dve):
            link = lambda ins: dve_chain.link(dve, ins)
            link(nc.vector.tensor_tensor(osq, o3, o3, ALU.mult))
            link(nc.vector.tensor_reduce(gw[:, 0, :], osq, AX, ALU.add))
            nc.vector.tensor_scalar(gw[:, 1, :], gw[:, 0, :], 1.0 / P, EPS, ALU.mult, ALU.add).then_inc(gn["var"], 1)
            dve.wait_ge(gn["sig"], 1)
            link(nc.vector.tensor_tensor(sig[:, :, :], sig[:, :, :], rest[:, :, Z0:Z0 + H * P], ALU.mult))
            link(nc.vector.tensor_tensor(o3, o3, sig[:, :, :].rearrange("p t (h n) -> p (t h) n", n=P), ALU.mult))
            dve.wait_ge(gn["root"], 1)
            link(nc.vector.reciprocal(gw[:, 1, :], gw[:, 1, :]))
            nc.vector.tensor_tensor(o3, o3, rep(gw[:, 1, :], [P, NT * H, P]), ALU.mult).then_inc(gn["ready"], 1)
            for t in range(NT):
                dve.wait_ge(gn["turned"], t + 1)
                nc.vector.tensor_scalar(yT[:, 0:H, cols(t)], ps[:, t, :].rearrange("p (h n) -> p h n", h=H)[:, :, 0:ROWS[t]],
                                        vec[:, V_GDN:V_GDN + 1], None, ALU.mult)

        @block.tensor
        def _(pe):
            pe.wait_ge(gn["ready"], 1)
            for t in range(NT):
                for h in range(H):
                    r = ROWS[t]
                    last = pe.transpose(ps[:, t, h * P:h * P + r], otok[0:r, t, h, :], c_(C_ID, r, r))
                last.then_inc(gn["turned"], 1)
    gdn_scope.close()
    clear_semaphores()
    mla_scope = ExitStack()
    mtake = lambda name, shape, dt=F32: mla_scope.enter_context(nc.sbuf_tensor(name, shape, dt))
    latT = mtake("latT", [P, 2, TOK])
    krT = mtake("krT", [P, TOK])
    qnT = mtake("qnT", [P, H, TOK])
    qrT = mtake("qrT", [P, H, TOK])
    kvn = mtake("kvn", [P, KVR])
    prompt_scope = ExitStack()
    ptake = lambda name, shape, dt=F32: prompt_scope.enter_context(nc.sbuf_tensor(name, shape, dt))
    cqT = ptake("cqT", [P, 3, TOK])
    knT = ptake("knT", [P, H, SEQ])
    vtok = ptake("vtok", [P, 2, H * P])
    qr = ptake("qr", [P, NT, H * ROPE])
    kr = ptake("kr", [P, NT, ROPE])
    rt = ptake("rope_tmp", [P, NT, H, 32])
    qkv_flat = qkv[:, :, :].rearrange("p c n -> p (c n)")
    uq = qkv_flat[:, 0:3 * H * QK].rearrange("p (k h n) -> p k h n", k=3, h=H)
    uk = W[:, 20480:21504].rearrange("p (r h n) -> p r h n", r=2, h=H)
    uv = W[:, 21504:22528].rearrange("p (r h n) -> p r h n", r=2, h=H)
    ml = {n: sem("mla_" + n) for n in ("w_loaded", "kvn_loaded", "squared", "var", "root", "lat_ready", "kr_ready", "turned",
                                       "moved", "proj", "proj_moved", "qr_made", "qr_ready", "qr_turned", "k_made", "k_moved")}

    def rope(dve, dst, src, tmp, cos, sin):
        half = ROPE // 2
        x1, x2 = (src[..., 0:half], src[..., half:ROPE])
        o1, o2 = (dst[..., 0:half], dst[..., half:ROPE])
        nc.vector.tensor_tensor(o1, x1, cos, ALU.mult)
        dve_chain.link(dve, nc.vector.tensor_tensor(tmp, x2, sin, ALU.mult))
        nc.vector.tensor_tensor(o1, o1, tmp, ALU.subtract)
        dve_chain.link(dve, nc.vector.tensor_tensor(o2, x2, cos, ALU.mult))
        dve_chain.link(dve, nc.vector.tensor_tensor(tmp, x1, sin, ALU.mult))
        return nc.vector.tensor_tensor(o2, o2, tmp, ALU.add)

    cos3 = cst[:, C_COS:C_COS + NT * 32].rearrange("p (t n) -> p t n", t=NT)
    sin3 = cst[:, C_SIN:C_SIN + NT * 32].rearrange("p (t n) -> p t n", t=NT)
    with nc.Block() as block:
        @block.sync
        def _(sp):
            sp.dma_start(kvn[:, :], kv_norm[0].partition_broadcast(P)).then_inc(ml["kvn_loaded"], 16)
            sp.dma_start(uq, w_uq[0].rearrange("(k p) h n -> p k h n", p=P)).then_inc(ml["w_loaded"], 16)
            sp.dma_start(uk, w_uk[0].rearrange("(k p) h n -> p k h n", p=P)).then_inc(ml["w_loaded"], 16)
            sp.dma_start(uv, w_uv[0].rearrange("(k p) h n -> p k h n", p=P)).then_inc(ml["w_loaded"], 16)
            sp.wait_ge(ml["lat_ready"], 1)
            store(sp, lat_prompt[0, 0].rearrange("(t p) n -> p t n", p=P), rest[:, 0:2, CKV0:CKV0 + KVR])
            store(sp, lat_sample[:, 0, 0, :], rest[0:DEC, 2, CKV0:CKV0 + KVR])
            sp.wait_ge(ml["kr_ready"], 1)
            store(sp, kr_prompt[0, 0].rearrange("(t p) n -> p t n", p=P), kr[:, 0:2, :])
            store(sp, kr_sample[:, 0, 0, :], kr[0:DEC, 2, :])

        @block.scalar
        def _(act):
            junk = qr[:, :, :].rearrange("p t n -> p (t n)")
            for t in range(NT):
                act_chain.link(act, nc.scalar.activation(junk[:, 0:QR], rest[:, t, CQ0:CQ0 + QR], ACT.Square, accum_out=small[:, 12 + t:13 + t]))
                act_chain.link(act, nc.scalar.activation(junk[:, 0:KVR], rest[:, t, CKV0:CKV0 + KVR], ACT.Square, accum_out=small[:, 15 + t:16 + t]))
            nc.scalar.copy(small[:, 60:61], small[:, 12:13]).then_inc(ml["squared"], 1)
            act.wait_ge(ml["var"], 1)
            nc.scalar.activation(small[:, 18:24], small[:, 18:24], ACT.Sqrt).then_inc(ml["root"], 1)
            for h in range(H):
                act.wait_ge(ml["proj"], h + 1)
                nc.scalar.copy(qnT[:, h, :], ps[:, h, 0:TOK]).then_inc(ml["proj_moved"], 1)
            for h in range(H):
                act.wait_ge(ml["k_made"], h + 1)
                nc.scalar.copy(knT[:, h, :], ps[:, h, 0:SEQ]).then_inc(ml["k_moved"], 1)
            for t in range(2):
                act.wait_ge(ml["k_made"], H + t + 1)
                nc.scalar.copy(vtok[:, t, :], ps[:, 7 * t, :])

        @block.vector
        def _(dve):
            link = lambda ins: dve_chain.link(dve, ins)
            nc.vector.memset(krT[:, :], 0.0)
            link(nc.vector.memset(qrT[:, :, :], 0.0))
            link(rope(dve, kr[:, :, :], rest[:, :, KR0:KR0 + ROPE], rt[:, :, 0, :], cos3, sin3))
            nc.vector.tensor_copy(small[:, 61:62], small[:, 62:63]).then_inc(ml["kr_ready"], 1)
            dve.wait_ge(ml["squared"], 1)
            nc.vector.tensor_scalar(small[:, 18:21], small[:, 12:15], 1.0 / QR, EPS, ALU.mult, ALU.add)
            nc.vector.tensor_scalar(small[:, 21:24], small[:, 15:18], 1.0 / KVR, EPS, ALU.mult, ALU.add).then_inc(ml["var"], 1)
            dve.wait_ge(ml["root"], 1)
            link(nc.vector.reciprocal(small[:, 24:30], small[:, 18:24]))
            dve.wait_ge(ml["kvn_loaded"], 16)
            for t in range(NT):
                cq = rest[:, t, CQ0:CQ0 + QR]
                ck = rest[:, t, CKV0:CKV0 + KVR]
                nc.vector.tensor_scalar(cq, cq, small[:, 24 + t:25 + t], None, ALU.mult)
                last = nc.vector.scalar_tensor_tensor(ck, ck, small[:, 27 + t:28 + t], kvn[:, :], ALU.mult, ALU.mult)
            last.then_inc(ml["lat_ready"], 1)
            for t in range(NT):
                r = ROWS[t]
                dve.wait_ge(ml["turned"], t + 1)
                nc.vector.tensor_tensor(cqT[:, :, cols(t)], ps[:, 2 * t, 0:3 * P].rearrange("p (k n) -> p k n", k=3)[:, :, 0:r],
                                        rep(vec[:, V_Q:V_Q + 3], [P, 3, r]), ALU.mult)
                nc.vector.tensor_copy(latT[:, :, cols(t)], ps[:, 2 * t + 1, 0:2 * P].rearrange("p (k n) -> p k n", k=2)[:, :, 0:r])
                nc.vector.tensor_copy(krT[0:ROPE, cols(t)], ps[0:ROPE, 2 * t + 1, 2 * P:2 * P + r]).then_inc(ml["moved"], 1)
            link(nc.vector.memset(qr[:, 2, :], 0.0))
            for t in range(NT):
                dve.wait_ge(ml["qr_made"], t + 1)
                r = ROWS[t]
                src = ps[0:r, 4 + t, 0:H * ROPE].rearrange("p (h n) -> p h n", h=H)
                link(rope(dve, qr[0:r, t, :].rearrange("p (h n) -> p h n", h=H), src, rt[0:r, t], rep1(cos3[0:r, t, :], [r, H, 32]),
                          rep1(sin3[0:r, t, :], [r, H, 32])))
            nc.vector.tensor_copy(small[:, 61:62], small[:, 62:63]).then_inc(ml["qr_ready"], 1)
            for t in range(NT):
                r = ROWS[t]
                dve.wait_ge(ml["qr_turned"], t + 1)
                nc.vector.tensor_copy(qrT[0:ROPE, :, cols(t)], ps[0:ROPE, 4 + t, :].rearrange("p (h n) -> p h n", h=H)[:, :, 0:r])

        @block.tensor
        def _(pe):
            pe.wait_ge(ml["lat_ready"], 1)
            pe.wait_ge(ml["kr_ready"], 1)
            for t in range(NT):
                r = ROWS[t]
                i = c_(C_ID, r, r)
                for k in range(3):
                    pe.transpose(ps[:, 2 * t, k * P:k * P + r], rest[0:r, t, CQ0 + k * P:CQ0 + (k + 1) * P], i)
                for k in range(2):
                    pe.transpose(ps[:, 2 * t + 1, k * P:k * P + r], rest[0:r, t, CKV0 + k * P:CKV0 + (k + 1) * P], i)
                pe.transpose(ps[0:ROPE, 2 * t + 1, 2 * P:2 * P + r], kr[0:r, t, :], i).then_inc(ml["turned"], 1)
            pe.wait_ge(ml["w_loaded"], 48)
            pe.wait_ge(ml["moved"], NT)
            for t in range(NT):
                for k in range(3):
                    last = pe.matmul(ps[0:ROWS[t], 4 + t, 0:H * ROPE], cqT[:, k, cols(t)], uq[:, k, :, NOPE:QK], start=(k == 0), stop=(k == 2))
                last.then_inc(ml["qr_made"], 1)
            for h in range(H):
                for k in range(3):
                    last = pe.matmul(ps[:, h, 0:TOK], uq[:, k, h, 0:NOPE], cqT[:, k, :], start=(k == 0), stop=(k == 2))
                last.then_inc(ml["proj"], 1)
            for h in range(H):
                pe.wait_ge(ml["proj_moved"], h + 1)
                for k in range(2):
                    last = pe.matmul(ps[:, h, 0:SEQ], uk[:, k, h, :], latT[:, k, 0:SEQ], start=(k == 0), stop=(k == 1))
                last.then_inc(ml["k_made"], 1)
            pe.wait_ge(ml["qr_ready"], 1)
            for t in range(NT):
                r = ROWS[t]
                for h in range(H):
                    last = pe.transpose(ps[0:ROPE, 4 + t, h * P:h * P + r], qr[0:r, t, h * ROPE:(h + 1) * ROPE], c_(C_ID, r, r))
                last.then_inc(ml["qr_turned"], 1)
            for t in range(2):
                if t == 0:
                    pe.wait_ge(ml["k_moved"], 1)
                for k in range(2):
                    last = pe.matmul(ps[:, 7 * t, :], latT[:, k, cols(t)], uv[:, k, :, :], start=(k == 0), stop=(k == 1))
                last.then_inc(ml["k_made"], 1)

    sc = W[:, 0:H * 384].rearrange("p (h n) -> p h n", h=H)
    pT = W[:, 2048:2048 + H * 384].rearrange("p (h n) -> p h n", h=H)
    mx = small[:, 30:38]
    ap = {n: sem("att_" + n) for n in ("scored", "max", "exp", "probs", "turned", "pt_ready", "out")}
    with nc.Block() as block:
        @block.tensor
        def _(pe):
            for h in range(H):
                for a, n, q in ((0, P, 0), (P, SEQ, P)):
                    pe.matmul(ps[:, h, a:a + n], qnT[:, h, q:q + P], knT[:, h, 0:n], start=True, stop=False)
                    last = pe.matmul(ps[:, h, a:a + n], qrT[:, h, q:q + P], krT[:, 0:n], start=False, stop=True)
            last.then_inc(ap["scored"], 1)
            pe.wait_ge(ap["probs"], 1)
            for h in range(H):
                for j in range(3):
                    last = pe.transpose(ps[:, 4 + h, j * P:(j + 1) * P], sc[:, h, j * P:(j + 1) * P], ident)
                last.then_inc(ap["turned"], 1)
            for h in range(H):
                pe.wait_ge(ap["pt_ready"], h + 1)
                pe.matmul(ps[:, h, 0:P], vtok[:, 0, h * P:(h + 1) * P], pT[:, h, 0:P], start=True, stop=True)
                pe.matmul(ps[:, h, P:SEQ], vtok[:, 0, h * P:(h + 1) * P], pT[:, h, P:SEQ], start=True, stop=False)
                pe.matmul(ps[:, h, P:SEQ], vtok[:, 1, h * P:(h + 1) * P], pT[:, h, SEQ:384], start=False, stop=True).then_inc(ap["out"], 1)

        @block.vector
        def _(dve):
            link = lambda ins: dve_chain.link(dve, ins)
            dve.wait_ge(ap["scored"], 1)
            for a in (0, SEQ):
                nc.vector.tensor_tensor(sc[:, :, a:a + P], ps[:, 0:H, a:a + P], rep1(c_(C_CAUS), [P, H, P]), ALU.add)
            link(nc.vector.tensor_copy(sc[:, :, P:SEQ], ps[:, 0:H, P:SEQ]))
            nc.vector.tensor_reduce(mx[:, 0:H], sc[:, :, 0:P], AX, ALU.max)
            link(nc.vector.tensor_reduce(mx[:, H:2 * H], sc[:, :, P:384], AX, ALU.max))
            nc.vector.tensor_scalar(mx, mx, -MLA_SCALE, None, ALU.mult).then_inc(ap["max"], 1)
            dve.wait_ge(ap["exp"], 1)
            link(nc.vector.reciprocal(small[:, 38:46], small[:, 38:46]))
            nc.vector.tensor_tensor(sc[:, :, 0:P], sc[:, :, 0:P], rep(small[:, 38:42], [P, H, P]), ALU.mult)
            nc.vector.tensor_tensor(sc[:, :, P:384], sc[:, :, P:384], rep(small[:, 42:46], [P, H, SEQ]), ALU.mult).then_inc(ap["probs"], 1)
            for h in range(H):
                dve.wait_ge(ap["turned"], h + 1)
                nc.vector.tensor_copy(pT[:, h, :], ps[:, 4 + h, 0:384]).then_inc(ap["pt_ready"], 1)
            for h in range(H):
                dve.wait_ge(ap["out"], h + 1)
                nc.vector.tensor_copy(yT[:, H + h, 0:SEQ], ps[:, h, 0:SEQ])

        @block.scalar
        def _(act):
            act.wait_ge(ap["max"], 1)
            for h in range(H):
                for j, (a, b) in enumerate(((0, P), (P, 384))):
                    i = j * H + h
                    act_chain.link(act, nc.scalar.activation(sc[:, h, a:b], sc[:, h, a:b], ACT.Exp, bias=mx[:, i:i + 1], scale=MLA_SCALE,
                                                             accum_out=small[:, 38 + i:39 + i]))
            nc.scalar.copy(small[:, 60:61], small[:, 38:39]).then_inc(ap["exp"], 1)
    prompt_scope.close()

    G = 4
    lat = W[:, 0:16384].rearrange("p (b j n) -> p b j n", b=G, j=NPAGE)
    krc = W[:, 16384:20480].rearrange("p (b j n) -> p b j n", b=G, j=NPAGE)
    ukT = W[:, 22528:23552].rearrange("p (h n) -> p h n", h=H)
    kT = qkv_flat[:, 0:3072].rearrange("p (i k n) -> p i k n", i=2, k=12)
    Ssc = mtake("Ssc", [P, PAST + 1])
    PT = mtake("PT", [P, NPAGE, P])
    qlp = mtake("qlp", [P, 2, DEC, 32])
    qrp = mtake("qrp", [P, DEC, 32])
    oLT = mtake("oLT", [P, 2, DEC, 32])
    olat = mtake("olat", [P, KVR])
    lnew = mtake("lnew", [P, KVR])
    pages = mtake("pages", [1, DEC * NPAGE], I32)
    page_loaded = [sem(f"page{j}_loaded") for j in range(NPAGE)]
    sa = {n: sem("smla_" + n) for n in ("pages", "uk_turned", "uk_moved", "ql_made", "ql_ready", "new_made", "new_moved", "turned", "moved_act",
                                        "moved_dve", "scored", "scores_moved", "max", "exp", "p_turned", "pt_moved", "pv_done", "o_ready",
                                        "o_turned", "o_moved", "out")}
    with nc.Block() as block:
        @block.sync
        def _(sp):
            sp.dma_start(pages[:, :], page_table.rearrange("(a b) j -> a (b j)", a=1)).then_inc(sa["pages"], 16)
            sp.wait_ge(sa["pages"], 16)
            for g in range(2):
                if g:
                    sp.wait_ge(sa["pv_done"], g)
                for j in range(NPAGE):
                    for b in range(G):
                        i = (g * G + b) * NPAGE + j
                        page = sp.value_load(pages[0:1, i:i + 1], min_val=0, max_val=cache_latent.shape[0] - 1)
                        sp.dma_start(lat[:, b, j, :], cache_latent[bass.ds(page, 1), 0, :, :].rearrange("a s n -> (a s) n")).then_inc(page_loaded[j], 16)
                        sp.dma_start(krc[:, b, j, :], cache_krope[bass.ds(page, 1), 0, :, :].rearrange("a s n -> (a s) n")).then_inc(page_loaded[j], 16)

        @block.tensor
        def _(pe):
            for h in range(H):
                for k in range(2):
                    last = pe.transpose(ps[:, h // 2, (2 * (h % 2) + k) * P:(2 * (h % 2) + k + 1) * P], uk[:, k, h, :], ident)
            last.then_inc(sa["uk_turned"], 1)
            pe.wait_ge(sa["uk_moved"], 1)
            for h in range(H):
                for k in range(2):
                    a = (k * H + h) * DEC
                    last = pe.matmul(ps[:, 2, a:a + DEC], ukT[:, h, k * P:(k + 1) * P], qnT[:, h, SEQ:TOK], start=True, stop=True)
            last.then_inc(sa["ql_made"], 1)
            pe.wait_ge(sa["ql_ready"], 1)
            for g in range(2):
                for b in range(G):
                    s, rows = g * G + b, slice(32 * b, 32 * b + 32)
                    for k in range(2):
                        pe.matmul(ps[rows, 1, 0:1], qlp[:, k, s, :], latT[:, k, SEQ + s:SEQ + s + 1], start=(k == 0), stop=False, tile_position=(0, 32 * b))
                    last = pe.matmul(ps[rows, 1, 0:1], qrp[:, s, :], krT[:, SEQ + s:SEQ + s + 1], start=False, stop=True, tile_position=(0, 32 * b))
                last.then_inc(sa["new_made"], 1)
                pe.wait_ge(sa["new_moved"], g + 1)

                def turn(j):
                    n = g * NPAGE + j
                    pe.wait_ge(page_loaded[j], 128 * (g + 1))
                    if n >= 2:
                        pe.wait_ge(sa["moved_act"], n - 1)
                        pe.wait_ge(sa["moved_dve"], n - 1)
                    bank = 2 + 3 * (n % 2)
                    for b in range(G):
                        for k in range(2):
                            pe.transpose(ps[:, bank + b // 2, (2 * (b % 2) + k) * P:(2 * (b % 2) + k + 1) * P], lat[:, b, j, k * P:(k + 1) * P], ident)
                        last = pe.transpose(ps[0:ROPE, bank + 2, b * P:(b + 1) * P], krc[:, b, j, :], ident)
                    last.then_inc(sa["turned"], 1)

                def score(j):
                    n = g * NPAGE + j
                    pe.wait_ge(sa["moved_act"], n + 1)
                    pe.wait_ge(sa["moved_dve"], n + 1)
                    m = g * 4 + j // 4
                    if j % 4 == 0 and m >= 2:
                        pe.wait_ge(sa["scores_moved"], m - 1)
                    for k in range(3):
                        for b in range(G):
                            s = g * G + b
                            lhs = qlp[:, k, s, :] if k < 2 else qrp[:, s, :]
                            last = pe.matmul(ps[32 * b:32 * b + 32, m % 2, (j % 4) * P:(j % 4 + 1) * P], lhs, kT[:, n % 2, 2 * b + k if k < 2 else 8 + b, :],
                                             start=(k == 0), stop=(k == 2), tile_position=(0, 32 * b))
                    last.then_inc(sa["scored"], 1)

                turn(0)
                for j in range(NPAGE):
                    if j + 1 < NPAGE:
                        turn(j + 1)
                    score(j)
                pe.wait_ge(sa["exp"], g + 1)
                for j in range(NPAGE):
                    last = pe.transpose(ps[:, 4 + j // 4, (j % 4) * P:(j % 4 + 1) * P], Ssc[:, j * P:(j + 1) * P], ident)
                    if j % 4 == 3:
                        last.then_inc(sa["p_turned"], 1)
                for j in range(NPAGE):
                    if j % 4 == 0:
                        pe.wait_ge(sa["pt_moved"], 4 * g + j // 4 + 1)
                    for b in range(G):
                        pe.matmul(ps[32 * b:32 * b + 32, 2, 0:KVR], PT[:, j, 32 * b:32 * b + 32], lat[:, b, j, :],
                                  start=(j == 0), stop=(j == NPAGE - 1), tile_position=(0, 32 * b))
                pe.matmul(ps[:, 3, 0:KVR], c_(C_SEQ + g * P, P, DEC), rest[0:DEC, 2, CKV0:CKV0 + KVR], start=True, stop=True).then_inc(sa["pv_done"], 1)
                pe.wait_ge(sa["o_ready"], g + 1)
                for k in range(2):
                    last = pe.transpose(ps[:, 4, k * P:(k + 1) * P], olat[:, k * P:(k + 1) * P], ident)
                last.then_inc(sa["o_turned"], 1)
                pe.wait_ge(sa["o_moved"], g + 1)
            for h in range(H):
                for k in range(2):
                    last = pe.matmul(ps[:, 0, h * DEC:(h + 1) * DEC], uv[:, k, h, :], oLT[:, k, :, h], start=(k == 0), stop=(k == 1))
            last.then_inc(sa["out"], 1)

        @block.scalar
        def _(act):
            for g in range(2):
                for j in range(NPAGE):
                    n = g * NPAGE + j
                    act.wait_ge(sa["turned"], n + 1)
                    if n >= 2:
                        act.wait_ge(sa["scored"], n - 1)
                    bank = 2 + 3 * (n % 2)
                    nc.scalar.copy(kT[:, n % 2, 0:4, :].rearrange("p k n -> p (k n)"), ps[:, bank, :]).then_inc(sa["moved_act"], 1)
                act.wait_ge(sa["max"], g + 1)
                nc.scalar.activation(Ssc[:, :], Ssc[:, :], ACT.Exp, bias=small[:, 46:47], scale=MLA_SCALE,
                                     accum_out=small[:, 47:48]).then_inc(sa["exp"], 1)

        @block.vector
        def _(dve):
            link = lambda ins: dve_chain.link(dve, ins)
            nc.vector.memset(qlp[:, :, :, :], 0.0)
            nc.vector.memset(qrp[:, :, :], 0.0)
            nc.vector.memset(kT[:, :, 8:12, :], 0.0)
            dve.wait_ge(sa["uk_turned"], 1)
            nc.vector.tensor_copy(ukT[:, :, :], ps[:, 0:2, :].rearrange("p a (h n) -> p (a h) n", h=2)).then_inc(sa["uk_moved"], 1)
            dve.wait_ge(sa["ql_made"], 1)
            for k in range(2):
                nc.vector.tensor_copy(qlp[:, k, :, 0:H].rearrange("p b h -> p h b"), ps[:, 2, k * 32:k * 32 + 32].rearrange("p (h b) -> p h b", h=H))
            nc.vector.tensor_copy(qrp[:, :, 0:H].rearrange("p b h -> p h b"), qrT[:, :, SEQ:TOK]).then_inc(sa["ql_ready"], 1)
            for g in range(2):
                dve.wait_ge(sa["new_made"], g + 1)
                nc.vector.tensor_copy(Ssc[:, PAST:PAST + 1], ps[:, 1, 0:1]).then_inc(sa["new_moved"], 1)
                for j in range(NPAGE):
                    n = g * NPAGE + j
                    dve.wait_ge(sa["turned"], n + 1)
                    if n >= 2:
                        dve.wait_ge(sa["scored"], n - 1)
                    bank = 2 + 3 * (n % 2)
                    nc.vector.tensor_copy(kT[:, n % 2, 4:8, :].rearrange("p k n -> p (k n)"), ps[:, bank + 1, :])
                    nc.vector.tensor_copy(kT[0:ROPE, n % 2, 8:12, :].rearrange("p k n -> p (k n)"), ps[0:ROPE, bank + 2, :]).then_inc(sa["moved_dve"], 1)
                    if j % 4 == 3:
                        m = g * 4 + j // 4
                        dve.wait_ge(sa["scored"], n + 1)
                        nc.vector.tensor_copy(Ssc[:, (j - 3) * P:(j + 1) * P], ps[:, m % 2, :]).then_inc(sa["scores_moved"], 1)
                dve.wait_ge(sa["scores_moved"], 4 * g + 4)
                link(nc.vector.tensor_reduce(small[:, 46:47], Ssc[:, :], AX, ALU.max))
                nc.vector.tensor_scalar(small[:, 46:47], small[:, 46:47], -MLA_SCALE, None, ALU.mult).then_inc(sa["max"], 1)
                dve.wait_ge(sa["exp"], g + 1)
                nc.vector.reciprocal(small[:, 48:49], small[:, 47:48])
                for m in range(4):
                    dve.wait_ge(sa["p_turned"], 4 * g + m + 1)
                    nc.vector.tensor_copy(PT[:, 4 * m:4 * m + 4, :].rearrange("p j n -> p (j n)"), ps[:, 4 + m, :]).then_inc(sa["pt_moved"], 1)
                dve.wait_ge(sa["pv_done"], g + 1)
                link(nc.vector.tensor_copy(lnew[:, :], ps[:, 3, 0:KVR]))
                link(nc.vector.scalar_tensor_tensor(olat[:, :], lnew[:, :], Ssc[:, PAST:PAST + 1], ps[:, 2, 0:KVR], ALU.mult, ALU.add))
                nc.vector.tensor_scalar(olat[:, :], olat[:, :], small[:, 48:49], None, ALU.mult).then_inc(sa["o_ready"], 1)
                dve.wait_ge(sa["o_turned"], g + 1)
                nc.vector.tensor_copy(oLT[:, :, g * G:(g + 1) * G, :], ps[:, 4, 0:2 * P].rearrange("p (k b n) -> p k b n", k=2, b=G)).then_inc(sa["o_moved"], 1)
            dve.wait_ge(sa["out"], 1)
            nc.vector.tensor_copy(yT[:, H:2 * H, SEQ:TOK], ps[:, 0, 0:H * DEC].rearrange("p (h b) -> p h b", h=H))
    mla_scope.close()
    clear_semaphores()
    heads_free = sem("heads_free")
    wkv = W[:, 0:16384].rearrange("p (w k n) -> p w k n", w=2, k=KD)
    wout = W[:, 16384:24576].rearrange("p (k n) -> p k n", k=KD)
    wxq = W[:, 0:8192].rearrange("p (k n) -> p k n", k=KD)
    wxo = W[:, 8192:16384].rearrange("p (k n) -> p k n", k=KD)
    mem_loaded, wkv_loaded, wout_loaded, wx_loaded = (sem(n) for n in ("mem_loaded", "wkv_loaded", "wout_loaded", "wx_loaded"))
    with nc.Block() as block:
        @block.sync
        def _(sp):
            sp.dma_start(wout, w_out[0].rearrange("(k p) n -> p k n", p=P)).then_inc(wout_loaded, 16)
            sp.dma_start(wkv[:, 0], w_xk[0].rearrange("(k p) n -> p k n", p=P)).then_inc(wkv_loaded, 16)
            sp.dma_start(wkv[:, 1], w_xv[0].rearrange("(k p) n -> p k n", p=P)).then_inc(wkv_loaded, 16)

    def add_projection(tag, src, w, loaded, at):
        made = sem(f"{tag}_made")
        with nc.Block() as block:
            @block.tensor
            def _(pe):
                pe.wait_ge(loaded, at)
                for t in range(NT):
                    for n in range(2):
                        for k in range(KD):
                            last = pe.matmul(ps[0:ROWS[t], 2 * t + n, :], src[:, k, cols(t)], w[:, k, n * 512:(n + 1) * 512],
                                             start=(k == 0), stop=(k == KD - 1))
                        last.then_inc(made, 1)

            @block.vector
            def _(dve):
                for t in range(NT):
                    for n in range(2):
                        dve.wait_ge(made, 2 * t + n + 1)
                        r = res[0:ROWS[t], t, n * 512:(n + 1) * 512]
                        nc.vector.tensor_tensor(r, r, ps[0:ROWS[t], 2 * t + n, :], ALU.add)

    add_projection("mix_out", yT, wout, wout_loaded, 16)
    heads_scope.close()

    x_scope = ExitStack()
    xtake = lambda name, shape, dt=F32: x_scope.enter_context(nc.sbuf_tensor(name, shape, dt))
    mkT = xtake("mkT", [P, KD, MEM])
    mv = xtake("mv", [P, 2, D])
    qxT = xtake("qxT", [P, KD, TOK])
    oxT = xtake("oxT", [P, KD, TOK])
    big = xtake("big", [P, 4096])
    qpad = xtake("qpad", [P, KD, DEC, 32])
    memt = big[:, 0:2 * D].rearrange("p (t n) -> p t n", t=2)
    mk = big[:, 2 * D:4 * D].rearrange("p (t n) -> p t n", t=2)
    with nc.Block() as block:
        @block.sync
        def _(sp):
            sp.dma_start(memt, mem_prompt[0].rearrange("(t p) d -> p t d", p=P)).then_inc(mem_loaded, 16)
    normed_transposed("mem", memt, (0, 1), V_MEM, mem_loaded, 16)

    kv_made, kv_moved, mk_turned = sem("kv_made"), sem("kv_moved"), sem("mk_turned")
    with nc.Block() as block:
        @block.sync
        def _(sp):
            sp.wait_ge(kv_moved, 8)
            store(sp, memk_prompt[0, 0].rearrange("(t p) h n -> p t (h n)", p=P), mk)
            store(sp, memv_prompt[0, 0].rearrange("(t p) h n -> p t (h n)", p=P), mv[:, :, :])
            sp.dma_start(wxq, w_xq[0].rearrange("(k p) n -> p k n", p=P)).then_inc(wx_loaded, 16)
            sp.dma_start(wxo, w_xo[0].rearrange("(k p) n -> p k n", p=P)).then_inc(wx_loaded, 16)

        @block.tensor
        def _(pe):
            pe.wait_ge(wkv_loaded, 32)
            i = 0
            for w in range(2):
                for t in range(2):
                    for n in range(2):
                        for k in range(KD):
                            last = pe.matmul(ps[:, i, :], xnT[:, k, cols(t)], wkv[:, w, k, n * 512:(n + 1) * 512], start=(k == 0), stop=(k == KD - 1))
                        last.then_inc(kv_made, 1)
                        i += 1
            pe.wait_ge(kv_moved, 4)
            for j in range(4):
                for k in range(2):
                    for t in range(2):
                        b = 2 * j + k
                        last = pe.transpose(ps[:, j, (2 * k + t) * P:(2 * k + t + 1) * P], mk[:, t, b * P:(b + 1) * P], ident)
                last.then_inc(mk_turned, 1)

        @block.vector
        def _(dve):
            for i in range(8):
                dve.wait_ge(kv_made, i + 1)
                dst = (mk if i < 4 else mv)[:, (i // 2) % 2, (i % 2) * 512:(i % 2 + 1) * 512]
                nc.vector.tensor_copy(dst, ps[:, i, :]).then_inc(kv_moved, 1)
            for j in range(4):
                dve.wait_ge(mk_turned, j + 1)
                nc.vector.tensor_copy(mkT[:, 2 * j:2 * j + 2, :].rearrange("p k n -> p (k n)"), ps[:, j, :])

    normed_transposed("x", res, (0, 1, 2), V_X, x_loaded, 32)

    scx = big[:, 0:2048].rearrange("p (i n) -> p i n", i=8)
    pTx = big[:, 2048:4096].rearrange("p (h s n) -> p h s n", h=H, s=2)
    X_SCALE = XD ** -0.5
    cx = {n: sem("cross_" + n) for n in ("q_made", "q_moved", "scored", "max", "exp", "probs", "turned", "pt_ready", "out", "out_moved")}
    with nc.Block() as block:
        @block.tensor
        def _(pe):
            pe.wait_ge(wx_loaded, 32)
            for c in range(KD):
                if c >= 4:
                    pe.wait_ge(cx["q_moved"], c - 3)
                for k in range(KD):
                    last = pe.matmul(ps[:, c % 4, 0:TOK], wxq[:, k, c * P:(c + 1) * P], xnT[:, k, :], start=(k == 0), stop=(k == KD - 1))
                last.then_inc(cx["q_made"], 1)
            pe.wait_ge(cx["q_moved"], KD)
            for h in range(H):
                for q in range(2):
                    for k in range(2):
                        last = pe.matmul(ps[:, 4 + h, q * MEM:(q + 1) * MEM], qxT[:, 2 * h + k, q * P:(q + 1) * P], mkT[:, 2 * h + k, :], start=(k == 0), stop=(k == 1))
            last.then_inc(cx["scored"], 1)
            pe.wait_ge(cx["probs"], 1)
            for h in range(H):
                for q in range(2):
                    for s in range(2):
                        last = pe.transpose(ps[:, h, s * SEQ + q * P:s * SEQ + (q + 1) * P], scx[:, 2 * h + q, s * P:(s + 1) * P], ident)
                last.then_inc(cx["turned"], 1)
            for k in range(KD):
                pe.wait_ge(cx["pt_ready"], k // 2 + 1)
                if k >= 4:
                    pe.wait_ge(cx["out_moved"], k - 3)
                for s in range(2):
                    last = pe.matmul(ps[:, 4 + k % 4, 0:SEQ], mv[:, s, k * P:(k + 1) * P], pTx[:, k // 2, s, :], start=(s == 0), stop=(s == 1))
                last.then_inc(cx["out"], 1)

        @block.scalar
        def _(act):
            for c in range(KD):
                act.wait_ge(cx["q_made"], c + 1)
                nc.scalar.copy(qxT[:, c, :], ps[:, c % 4, 0:TOK]).then_inc(cx["q_moved"], 1)
            act.wait_ge(cx["max"], 1)
            for i in range(8):
                act_chain.link(act, nc.scalar.activation(scx[:, i, :], ps[:, 4 + i // 2, (i % 2) * MEM:(i % 2 + 1) * MEM], ACT.Exp,
                                                         bias=small[:, 30 + i:31 + i], scale=X_SCALE, accum_out=small[:, 38 + i:39 + i]))
            nc.scalar.copy(small[:, 60:61], small[:, 38:39]).then_inc(cx["exp"], 1)

        @block.vector
        def _(dve):
            link = lambda ins: dve_chain.link(dve, ins)
            dve.wait_ge(cx["scored"], 1)
            link(nc.vector.tensor_reduce(small[:, 30:38], ps[:, 4:8, :].rearrange("p h (q n) -> p (h q) n", q=2), AX, ALU.max))
            nc.vector.tensor_scalar(small[:, 30:38], small[:, 30:38], -X_SCALE, None, ALU.mult).then_inc(cx["max"], 1)
            dve.wait_ge(cx["exp"], 1)
            link(nc.vector.reciprocal(small[:, 38:46], small[:, 38:46]))
            nc.vector.tensor_tensor(scx, scx, rep(small[:, 38:46], [P, 8, MEM]), ALU.mult).then_inc(cx["probs"], 1)
            for h in range(H):
                dve.wait_ge(cx["turned"], h + 1)
                nc.vector.tensor_copy(pTx[:, h, :, :].rearrange("p s n -> p (s n)"), ps[:, h, :]).then_inc(cx["pt_ready"], 1)
            for k in range(KD):
                dve.wait_ge(cx["out"], k + 1)
                nc.vector.tensor_copy(oxT[:, k, 0:SEQ], ps[:, 4 + k % 4, 0:SEQ]).then_inc(cx["out_moved"], 1)

    KTx = big[:, :].rearrange("p (i k n) -> p i k n", i=2, k=KD)
    Vx = W[:, 0:8192].rearrange("p (b s n) -> p b s n", b=G, s=2)
    Kx = W[:, 16384:24576].rearrange("p (b s n) -> p b s n", b=G, s=2)
    pS = xtake("pS", [P, MEM])
    pST = xtake("pST", [P, 2, P])
    oS = xtake("oS", [P, D])
    kx_loaded = [sem(f"xkey{b}_loaded") for b in range(G)]
    vx_loaded = sem("xvalue_loaded")
    sx = {n: sem("scross_" + n) for n in ("q_ready", "turned", "moved_act", "moved_dve", "scored", "max", "exp", "probs", "p_turned", "pt_ready",
                                          "out", "o_moved", "o_turned", "o_done")}
    with nc.Block() as block:
        @block.sync
        def _(sp):
            for g in range(2):
                for b in range(G):
                    if g:
                        sp.wait_ge(sx["scored"], b + 1)
                    sp.dma_start(Kx[:, b], cache_mem_k[0, g * G + b].rearrange("(s p) h n -> p s (h n)", p=P)).then_inc(kx_loaded[b], 16)
                if g:
                    sp.wait_ge(sx["out"], g)
                sp.dma_start(Vx, cache_mem_v[0, g * G:(g + 1) * G].rearrange("b (s p) h n -> p b s (h n)", p=P)).then_inc(vx_loaded, 16)

        @block.tensor
        def _(pe):
            pe.wait_ge(sx["q_ready"], 1)
            for g in range(2):
                for b in range(G):
                    n = g * G + b
                    pe.wait_ge(kx_loaded[b], 16 * (g + 1))
                    for s in range(2):
                        m = 2 * n + s
                        if m >= 2:
                            pe.wait_ge(sx["moved_act"], m - 1)
                            pe.wait_ge(sx["moved_dve"], m - 1)
                        if g and b == 0:
                            pe.wait_ge(sx["o_done"], g)
                        for k in range(KD):
                            last = pe.transpose(ps[:, 2 * (m % 2) + k // 4, (k % 4) * P:(k % 4 + 1) * P], Kx[:, b, s, k * P:(k + 1) * P], ident)
                        last.then_inc(sx["turned"], 1)
                    pe.wait_ge(sx["moved_act"], 2 * n + 2)
                    pe.wait_ge(sx["moved_dve"], 2 * n + 2)
                    for k in range(KD):
                        last = pe.matmul(ps[32 * b:32 * b + 32, 4, 0:MEM], qpad[:, k, n, :], KTx[:, n % 2, k, :],
                                         start=(k == 0), stop=(k == KD - 1), tile_position=(0, 32 * b))
                    last.then_inc(sx["scored"], 1)
                pe.wait_ge(sx["probs"], g + 1)
                for s in range(2):
                    last = pe.transpose(ps[:, 5, s * P:(s + 1) * P], pS[:, s * P:(s + 1) * P], ident)
                last.then_inc(sx["p_turned"], 1)
                pe.wait_ge(sx["pt_ready"], g + 1)
                pe.wait_ge(vx_loaded, 16 * (g + 1))
                for j in range(2):
                    for s in range(2):
                        for b in range(G):
                            last = pe.matmul(ps[32 * b:32 * b + 32, 6 + j, :], pST[:, s, 32 * b:32 * b + 32], Vx[:, b, s, j * 512:(j + 1) * 512],
                                             start=(s == 0), stop=(s == 1), tile_position=(0, 32 * b))
                last.then_inc(sx["out"], 1)
                pe.wait_ge(sx["o_moved"], g + 1)
                for k in range(KD):
                    last = pe.transpose(ps[:, 2 + k // 4, (k % 4) * P:(k % 4 + 1) * P], oS[:, k * P:(k + 1) * P], ident)
                last.then_inc(sx["o_turned"], 1)

        @block.scalar
        def _(act):
            for g in range(2):
                for m in range(2 * G * g, 2 * G * (g + 1)):
                    act.wait_ge(sx["turned"], m + 1)
                    n = m // 2
                    if n >= 2:
                        act.wait_ge(sx["scored"], n - 1)
                    nc.scalar.copy(KTx[:, n % 2, 0:4, (m % 2) * P:(m % 2 + 1) * P], ps[:, 2 * (m % 2), :].rearrange("p (k n) -> p k n", k=4)).then_inc(sx["moved_act"], 1)
                act.wait_ge(sx["max"], g + 1)
                nc.scalar.activation(pS[:, :], ps[:, 4, 0:MEM], ACT.Exp, bias=small[:, 46:47], scale=X_SCALE, accum_out=small[:, 47:48]).then_inc(sx["exp"], 1)
                act.wait_ge(sx["out"], g + 1)
                nc.scalar.copy(oS[:, :].rearrange("p (a n) -> p a n", a=2), ps[:, 6:8, :]).then_inc(sx["o_moved"], 1)

        @block.vector
        def _(dve):
            link = lambda ins: dve_chain.link(dve, ins)
            link(nc.vector.memset(qpad[:, :, :, :], 0.0))
            for h in range(H):
                last = nc.vector.tensor_copy(qpad[:, 2 * h:2 * h + 2, :, h], qxT[:, 2 * h:2 * h + 2, SEQ:TOK])
            last.then_inc(sx["q_ready"], 1)
            for g in range(2):
                for m in range(2 * G * g, 2 * G * (g + 1)):
                    dve.wait_ge(sx["turned"], m + 1)
                    n = m // 2
                    if n >= 2:
                        dve.wait_ge(sx["scored"], n - 1)
                    nc.vector.tensor_copy(KTx[:, n % 2, 4:8, (m % 2) * P:(m % 2 + 1) * P], ps[:, 2 * (m % 2) + 1, :].rearrange("p (k n) -> p k n", k=4)).then_inc(sx["moved_dve"], 1)
                dve.wait_ge(sx["scored"], G * (g + 1))
                link(nc.vector.tensor_reduce(small[:, 46:47], ps[:, 4, 0:MEM], AX, ALU.max))
                nc.vector.tensor_scalar(small[:, 46:47], small[:, 46:47], -X_SCALE, None, ALU.mult).then_inc(sx["max"], 1)
                dve.wait_ge(sx["exp"], g + 1)
                link(nc.vector.reciprocal(small[:, 48:49], small[:, 47:48]))
                nc.vector.tensor_scalar(pS[:, :], pS[:, :], small[:, 48:49], None, ALU.mult).then_inc(sx["probs"], 1)
                dve.wait_ge(sx["p_turned"], g + 1)
                nc.vector.tensor_copy(pST[:, :, :].rearrange("p s n -> p (s n)"), ps[:, 5, 0:2 * P]).then_inc(sx["pt_ready"], 1)
                dve.wait_ge(sx["o_turned"], g + 1)
                for h in range(H):
                    src = ps[:, 2 + h // 2, :].rearrange("p (k b n) -> p k b n", k=4, b=G)[:, 2 * (h % 2):2 * (h % 2) + 2, :, h]
                    last = nc.vector.tensor_copy(oxT[:, 2 * h:2 * h + 2, SEQ + g * G:SEQ + (g + 1) * G], src)
                last.then_inc(sx["o_done"], 1)

    add_projection("cross_out", oxT, wxo, wx_loaded, 32)
    x_scope.close()
    clear_semaphores()
    e_scope = ExitStack()
    etake = lambda name, shape, dt=F32: e_scope.enter_context(nc.sbuf_tensor(name, shape, dt))
    xh = etake("xh", [P, NT, D])
    wr = etake("wr", [P, KD, NE])
    br = etake("br", [P, NE])
    LG = etake("LG", [P, NT, NE + 8])
    LR = etake("LR", [P, NT, NE + 8])
    top = etake("top", [P, NT, 8])
    sel = etake("sel", [P, NT, NE])
    gate = etake("gate_w", [P, NT, NE])
    slot = etake("slot", [P, NT, NE])
    cnt = etake("cnt", [P, 8])
    rounds = etake("rounds", [P, 2], I32)
    b1 = etake("b1", [3 * NE, 3 * D], BF16)
    pick = etake("pick", [3 * NE, NE * SLOTS], BF16)
    RING = 12
    ring = W[:, :].rearrange("p (s n) -> p s n", s=RING)
    full = [sem(f"ring{s}_full") for s in range(RING)]
    free = [sem(f"ring{s}_free") for s in range(RING)]
    FILLS = 24

    def fill(sp, n, e):
        s, x = n % RING, n % 2
        if n < 16:
            k = n // 2
            src = w_e1[0, bass.ds(e + x, 1), k * P:(k + 1) * P, :].rearrange("a p n -> (a p) n")
            sp.dma_start(ring[:, s, :], src).then_inc(full[s], 16)
        else:
            k = 2 * ((n - 16) // 2)
            src = w_e2[0, bass.ds(e + x, 1), k * P:(k + 2) * P, :].rearrange("a (k p) n -> p (a k) n", p=P)
            sp.dma_start(ring[:, s, :].rearrange("p (k n) -> p k n", k=2), src).then_inc(full[s], 16)

    bs_scope = ExitStack()
    bias = bs_scope.enter_context(nc.sbuf_tensor("bias", [NE, 3 * D], F32))
    part = bs_scope.enter_context(nc.sbuf_tensor("part", [NE, 3 * D], BF16))
    mo = {n: sem("moe_" + n) for n in ("r_loaded", "b_loaded", "pick_loaded", "logits", "top", "exp", "sel", "pos", "rounds")}
    with nc.Block() as block:
        @block.sync
        def _(sp):
            sp.dma_start(wr[:, :, :], w_router[0].rearrange("(k p) n -> p k n", p=P)).then_inc(mo["r_loaded"], 16)
            sp.dma_start(br[:, :], b_router[0].partition_broadcast(P)).then_inc(mo["r_loaded"], 16)
            sp.dma_start(bias[:, 0:2 * D], b_e1[0]).then_inc(mo["b_loaded"], 16)
            sp.dma_start(bias[:, 2 * D:3 * D], b_e2[0]).then_inc(mo["b_loaded"], 16)
            sp.dma_start(pick[:, :], const_bf16).then_inc(mo["pick_loaded"], 16)
            for n in range(RING):
                fill(sp, n, 0)

        @block.vector
        def _(dve):
            dve.wait_ge(mo["b_loaded"], 32)
            for i in range(3):
                dve_chain.link(dve, nc.vector.tensor_copy(b1[i * NE:(i + 1) * NE, :], bias[:, :]))
                if i < 2:
                    dve_chain.link(dve, nc.vector.tensor_copy(part[:, :], bias[:, :]))
                    dve_chain.link(dve, nc.vector.tensor_tensor(bias[:, :], bias[:, :], part[:, :], ALU.subtract))
    bs_scope.close()

    normed_transposed("ffn", res, (0, 1, 2), V_FFN, x_loaded, 32, xh)

    with nc.Block() as block:
        @block.tensor
        def _(pe):
            pe.wait_ge(mo["r_loaded"], 32)
            for t in range(NT):
                for k in range(KD):
                    last = pe.matmul(ps[0:ROWS[t], t, 0:NE], xnT[:, k, cols(t)], wr[:, k, :], start=(k == 0), stop=(k == KD - 1))
            last.then_inc(mo["logits"], 1)
            pe.wait_ge(mo["sel"], 1)
            for t in range(NT):
                r = ROWS[t]
                for j in range(t):
                    pe.matmul(ps[0:r, 4 + t, 0:NE], c_(C_ONE, r), sel[:, j, :], start=(j == 0), stop=False)
                pe.matmul(ps[0:r, 4 + t, 0:NE], c_(C_BEF, r, r), sel[0:r, t, :], start=(t == 0), stop=True)
            for t in range(NT):
                last = pe.matmul(ps[:, 7, 0:NE], c_(C_ONE), sel[:, t, :], start=(t == 0), stop=(t == NT - 1))
            last.then_inc(mo["pos"], 1)

        @block.scalar
        def _(act):
            act.wait_ge(mo["top"], NT)
            for t in range(NT):
                r = ROWS[t]
                last = nc.scalar.activation(gate[0:r, t, :], LG[0:r, t, 0:NE], ACT.Exp, bias=cnt[0:r, t:t + 1])
            last.then_inc(mo["exp"], 1)

        @block.vector
        def _(dve):
            link = lambda ins: dve_chain.link(dve, ins)
            nc.vector.memset(LG[:, :, NE:NE + 8], 3 * NEG)
            nc.vector.memset(sel[:, :, :], 0.0)
            link(nc.vector.memset(gate[:, :, :], 0.0))
            dve.wait_ge(mo["logits"], 1)
            for t in range(NT):
                r = ROWS[t]
                link(nc.vector.tensor_tensor(LG[0:r, t, 0:NE], ps[0:r, t, 0:NE], br[0:r, :], ALU.add))
                link(nc.vector.max(top[0:r, t, :], LG[0:r, t, :]))
                nc.vector.tensor_scalar(cnt[0:r, t:t + 1], top[0:r, t, 0:1], -1.0, None, ALU.mult).then_inc(mo["top"], 1)
                link(nc.vector.memset(top[0:r, t, TOPK:8], 3 * NEG))
                link(nc.vector.match_replace(LR[0:r, t, :], top[0:r, t, :], LG[0:r, t, :], 4 * NEG))
                link(nc.vector.tensor_tensor(sel[0:r, t, :], LR[0:r, t, 0:NE], LG[0:r, t, 0:NE], ALU.not_equal))
            nc.vector.tensor_copy(small[:, 61:62], small[:, 62:63]).then_inc(mo["sel"], 1)
            dve.wait_ge(mo["exp"], 1)
            link(nc.vector.tensor_tensor(gate[:, :, :], gate[:, :, :], sel[:, :, :], ALU.mult))
            link(nc.vector.tensor_reduce(cnt[:, 3:6], gate[:, :, :], AX, ALU.add))
            link(nc.vector.tensor_scalar(cnt[:, 3:6], cnt[:, 3:6], 1e-30, None, ALU.max))
            link(nc.vector.reciprocal(cnt[:, 3:6], cnt[:, 3:6]))
            nc.vector.tensor_tensor(gate[:, :, :], gate[:, :, :], rep(cnt[:, 3:6], [P, NT, NE]), ALU.mult)
            dve.wait_ge(mo["pos"], 1)
            for t in range(NT):
                r = ROWS[t]
                link(nc.vector.scalar_tensor_tensor(slot[0:r, t, :], ps[0:r, 4 + t, 0:NE], 1.0, sel[0:r, t, :], ALU.add, ALU.mult))
                link(nc.vector.tensor_scalar(slot[0:r, t, :], slot[0:r, t, :], -1.0, None, ALU.add))
            link(nc.vector.tensor_reduce(cnt[:, 6:7], ps[:, 7, 0:NE], AX, ALU.max))
            link(nc.vector.memset(cnt[:, 7:8], 1.0))
            for i in range(1, -(-TOK // SLOTS)):
                link(nc.vector.scalar_tensor_tensor(cnt[:, 7:8], cnt[:, 6:7], float(SLOTS * i), cnt[:, 7:8], ALU.is_gt, ALU.add))
            link(nc.vector.tensor_scalar(cnt[:, 6:7], cnt[:, 7:8], float(NE), -1.0, ALU.mult, ALU.add))
            nc.vector.tensor_copy(rounds[:, 0:1], cnt[:, 7:8])
            nc.vector.tensor_copy(rounds[:, 1:2], cnt[:, 6:7]).then_inc(mo["rounds"], 1)

    PAIRS = NE // 2
    MAXR = -(-TOK // SLOTS)
    picked = etake("picked", [P, NT, P])
    gated = etake("gated", [P, NT, P])
    gT = etake("gT", [P, NT, P])
    xe = etake("xe", [P, KD, P])
    glu = etake("glu", [P, D])
    lin = etake("lin", [P, D])
    sg = etake("sg", [P, D])
    aT = etake("aT", [P, KD, P])
    ye = etake("ye", [P, D])
    lp = {n: sem("pair_" + n) for n in ("picked", "gathered", "xe_ready", "gt_turned", "gt_ready", "glu", "clipped", "joined", "sig", "act", "shifted", "a_turned",
                                        "a_act", "a_dve", "y_act", "y_dve", "combined", "added")}

    def wait_hidden(eng, it):
        eng.wait_ge(free[15 % RING], it * 2 + 2)

    def wait_y(eng, it):
        eng.wait_ge(free[23 % RING], it * 2 + 2)

    def n_rounds(eng):
        return eng.value_load(rounds[0:1, 0:1], min_val=1, max_val=MAXR)

    with nc.Block() as block:
        @block.sync
        def _(sp):
            nr = n_rounds(sp)
            with sp.Fori(0, nr * PAIRS - 1) as it:
                e = sp.snap((it % PAIRS) * 2)
                after = sp.snap(((it + 1) % PAIRS) * 2)
                for n in range(RING, FILLS):
                    sp.wait_ge(free[n % RING], it * 2 + 1)
                    fill(sp, n, e)
                for n in range(RING):
                    sp.wait_ge(free[n % RING], it * 2 + 2)
                    fill(sp, n, after)
            last = sp.value_load(rounds[0:1, 1:2], min_val=NE - 1, max_val=MAXR * NE - 1)
            for n in range(RING, FILLS):
                sp.wait_ge(free[n % RING], last)
                fill(sp, n, NE - 2)

        @block.tensor
        def _(pe):
            pe.wait_ge(mo["pick_loaded"], 16)
            nr = n_rounds(pe)
            with pe.Fori(0, nr) as r:
                with pe.Fori(0, PAIRS) as p:
                    it = pe.snap(r * PAIRS + p)
                    one = pe.snap(it + 1)
                    pe.wait_ge(lp["picked"], one)
                    pe.wait_ge(lp["added"], it * 6 + 1)
                    for k in range(KD):
                        for t in range(NT):
                            last = pe.matmul(ps[:, 6 + k // 4, (k % 4) * P:(k % 4 + 1) * P], xh[0:ROWS[t], t, k * P:(k + 1) * P],
                                             picked[0:ROWS[t], t, :], start=(t == 0), stop=(t == NT - 1))
                    last.then_inc(lp["gathered"], 1)
                    for t in range(NT):
                        last = pe.transpose(ps[:, 4, t * P:t * P + ROWS[t]], gated[0:ROWS[t], t, :], c_(C_ID, ROWS[t], ROWS[t]))
                    last.then_inc(lp["gt_turned"], 1)
                    mine = pick[:, bass.ds(p * P, P)]
                    for c in range(4):
                        pe.matmul(ps[:, c, :], mine, b1[:, c * 512:(c + 1) * 512], start=True, stop=True)
                    pe.wait_ge(lp["xe_ready"], one)
                    for n in range(0, 16, 2):
                        k = n // 2
                        for x in range(2):
                            pe.wait_ge(full[(n + x) % RING], (it * 2 + (n + x) // RING + 1) * 16)
                        for c in range(4):
                            for x in range(2):
                                last = pe.matmul(ps[64 * x:64 * x + 64, c, :], xe[:, k, 64 * x:64 * x + 64], ring[:, (n + x) % RING, c * 512:(c + 1) * 512],
                                                 start=False, stop=(k == KD - 1), skip_group_check=True)
                                if c == 3:
                                    last.then_inc(free[(n + x) % RING], 1)
                    pe.wait_ge(lp["act"], one)
                    for k in range(KD):
                        last = pe.transpose(ps[:, 6 + k // 4, (k % 4) * P:(k % 4 + 1) * P], lin[:, k * P:(k + 1) * P], ident)
                    last.then_inc(lp["a_turned"], 1)
                    pe.wait_ge(lp["gt_ready"], it + 2)
                    for c in range(2):
                        pe.matmul(ps[:, 4 + c, :], mine, b1[:, (4 + c) * 512:(5 + c) * 512], start=True, stop=True)
                    pe.wait_ge(lp["a_act"], one)
                    pe.wait_ge(lp["a_dve"], one)
                    for n in range(16, FILLS, 2):
                        for x in range(2):
                            pe.wait_ge(full[(n + x) % RING], (it * 2 + (n + x) // RING + 1) * 16)
                        for j in range(2):
                            k = n - 16 + j
                            for c in range(2):
                                for x in range(2):
                                    last = pe.matmul(ps[64 * x:64 * x + 64, 4 + c, :], aT[:, k, 64 * x:64 * x + 64],
                                                     ring[:, (n + x) % RING, j * D + c * 512:j * D + (c + 1) * 512],
                                                     start=False, stop=(k == KD - 1), skip_group_check=True)
                                    if c == 1 and j == 1:
                                        last.then_inc(free[(n + x) % RING], 1)
                    pe.wait_ge(lp["y_act"], one)
                    pe.wait_ge(lp["y_dve"], one)
                    for t in range(NT):
                        for c in range(2):
                            bank = (0, 1, 2, 3, 6, 7)[2 * t + c]
                            pe.matmul(ps[0:ROWS[t], bank, :], gT[:, t, 0:ROWS[t]], ye[:, c * 512:(c + 1) * 512], start=True, stop=True).then_inc(lp["combined"], 1)

        @block.scalar
        def _(act):
            nr = n_rounds(act)
            act.sem_inc(lp["gt_ready"], 1)
            with act.Fori(0, nr) as r:
                with act.Fori(0, PAIRS) as p:
                    it = act.snap(r * PAIRS + p)
                    one = act.snap(it + 1)
                    act.wait_ge(lp["gt_turned"], one)
                    nc.scalar.copy(gT[:, 0:2, :], ps[:, 4, 0:2 * P].rearrange("p (t n) -> p t n", t=2))
                    nc.scalar.copy(gT[:, 2, 0:DEC], ps[:, 4, 2 * P:2 * P + DEC]).then_inc(lp["gt_ready"], 1)
                    act.wait_ge(lp["glu"], one)
                    nc.scalar.activation(sg[:, :], glu[:, :], ACT.Sigmoid, scale=1.702).then_inc(lp["sig"], 1)
                    act.wait_ge(lp["a_turned"], one)
                    nc.scalar.copy(aT[:, 0:4, :].rearrange("p k n -> p (k n)"), ps[:, 6, :]).then_inc(lp["a_act"], 1)
                    wait_y(act, it)
                    nc.scalar.copy(ye[:, 0:512], ps[:, 4, :]).then_inc(lp["y_act"], 1)

        @block.vector
        def _(dve):
            nr = n_rounds(dve)
            dve.sem_inc(lp["added"], 1)
            with dve.Fori(0, nr) as r:
                with dve.Fori(0, PAIRS) as p:
                    it = dve.snap(r * PAIRS + p)
                    one = dve.snap(it + 1)
                    dve.wait_ge(lp["gt_ready"], one)
                    for x in range(2):
                        for t in range(NT):
                            q, mine = ROWS[t], bass.ds(p * 2 + x, 1)
                            io = c_(C_IOTA, SLOTS, q)
                            nc.vector.tensor_scalar(picked[0:q, t, 64 * x:64 * x + 64], io, slot[0:q, t, mine], None, ALU.is_equal)
                            last = nc.vector.tensor_scalar(gated[0:q, t, 64 * x:64 * x + 64], io, slot[0:q, t, mine], gate[0:q, t, mine], ALU.is_equal, ALU.mult)
                    last.then_inc(lp["picked"], 1)
                    dve.wait_ge(lp["gathered"], one)
                    for j in range(2):
                        last = nc.vector.tensor_tensor(xe[:, 4 * j:4 * j + 4, :], ps[:, 6 + j, :].rearrange("p (k n) -> p k n", k=4),
                                                       rep(vec[:, V_FFN + 4 * j:V_FFN + 4 * j + 4], [P, 4, P]), ALU.mult)
                    last.then_inc(lp["xe_ready"], 1)
                    wait_hidden(dve, it)
                    hid = ps[:, 0:4, :].rearrange("p c (n j) -> p c n j", j=2)
                    nc.vector.tensor_scalar(glu[:, :].rearrange("p (c n) -> p c n", c=4), hid[:, :, :, 0], 7.0, None, ALU.min).then_inc(lp["glu"], 1)
                    nc.vector.tensor_scalar(lin[:, :].rearrange("p (c n) -> p c n", c=4), hid[:, :, :, 1], 7.0, -7.0, ALU.min, ALU.max).then_inc(lp["clipped"], 1)
                    dve.wait_ge(lp["clipped"], one)
                    nc.vector.scalar_tensor_tensor(lin[:, :], lin[:, :], 1.0, glu[:, :], ALU.add, ALU.mult).then_inc(lp["joined"], 1)
                    dve.wait_ge(lp["joined"], one)
                    dve.wait_ge(lp["sig"], one)
                    nc.vector.tensor_tensor(lin[:, :], lin[:, :], sg[:, :], ALU.mult).then_inc(lp["act"], 1)
                    dve.wait_ge(lp["a_turned"], one)
                    nc.vector.tensor_copy(aT[:, 4:8, :].rearrange("p k n -> p (k n)"), ps[:, 7, :]).then_inc(lp["a_dve"], 1)
                    wait_y(dve, it)
                    nc.vector.tensor_copy(ye[:, 512:D], ps[:, 5, :]).then_inc(lp["y_dve"], 1)
                    for t in range(NT):
                        for c in range(2):
                            i = 2 * t + c
                            dve.wait_ge(lp["combined"], it * 6 + (i + 1))
                            a = res[0:ROWS[t], t, c * 512:(c + 1) * 512]
                            nc.vector.tensor_tensor(a, a, ps[0:ROWS[t], (0, 1, 2, 3, 6, 7)[i], :], ALU.add).then_inc(lp["added"], 1)
                for t in range(NT):
                    last = nc.vector.tensor_scalar(slot[0:ROWS[t], t, :], slot[0:ROWS[t], t, :], -float(SLOTS), None, ALU.add)
                last.then_inc(lp["shifted"], 1)
                dve.wait_ge(lp["shifted"], r + 1)
    e_scope.close()

    fn = {n: sem("final_" + n) for n in ("gain", "sq", "var", "root", "done")}
    with ExitStack() as scope, nc.Block() as block:
        nf = scope.enter_context(nc.sbuf_tensor("nf", [P, D], F32))
        junk = scope.enter_context(nc.sbuf_tensor("fjunk", [P, D], F32))

        @block.sync
        def _(sp):
            sp.dma_start(nf[:, :], norm_final.partition_broadcast(P)).then_inc(fn["gain"], 16)
            sp.wait_ge(fn["done"], 1)
            store(sp, y_prompt[0, 0:P, :], res[:, 0, :])
            sp.wait_ge(fn["done"], 2)
            store(sp, y_prompt[0, P:SEQ, :], res[:, 1, :])
            sp.wait_ge(fn["done"], 3)
            store(sp, y_sample[:, 0, :], res[0:DEC, 2, :])
            sp.wait_ge(stored, n_stored[0])

        @block.scalar
        def _(act):
            for t in range(NT):
                act_chain.link(act, nc.scalar.activation(junk[0:ROWS[t], :], res[0:ROWS[t], t, :], ACT.Square, accum_out=small[0:ROWS[t], t:t + 1]))
            nc.scalar.copy(small[:, 3:4], small[:, 3:4]).then_inc(fn["sq"], 1)
            act.wait_ge(fn["var"], 1)
            nc.scalar.activation(small[:, 4:7], small[:, 4:7], ACT.Sqrt).then_inc(fn["root"], 1)

        @block.vector
        def _(dve):
            dve.wait_ge(fn["sq"], 1)
            nc.vector.tensor_scalar(small[:, 4:7], small[:, 0:3], 1.0 / D, EPS, ALU.mult, ALU.add).then_inc(fn["var"], 1)
            dve.wait_ge(fn["root"], 1)
            dve_chain.link(dve, nc.vector.reciprocal(small[:, 8:11], small[:, 4:7]))
            dve.wait_ge(fn["gain"], 16)
            for t in range(NT):
                a = res[0:ROWS[t], t, :]
                nc.vector.scalar_tensor_tensor(a, a, small[0:ROWS[t], 8 + t:9 + t], nf[0:ROWS[t], :], ALU.mult, ALU.mult).then_inc(fn["done"], 1)

INPUTS = ("x_prompt", "x_sample", "state_gdn", "state_conv", "cache_latent", "cache_krope", "page_table",
          "cache_mem_k", "cache_mem_v", "mem_prompt", "norm_mix", "w_in", "conv_w", "a_log", "dt_bias", "gdn_norm",
          "q_norm", "w_uq", "kv_norm", "w_uk", "w_uv", "w_out", "norm_x", "mem_norm", "w_xq", "w_xk", "w_xv", "w_xo",
          "norm_ffn", "w_router", "b_router", "w_e1", "b_e1", "w_e2", "b_e2", "norm_final")
OUTPUTS = ((1, SEQ, D), (DEC, 1, D), (1, 1, H, P, P), (1, 1, 3, CONV), (1, 1, SEQ, KVR), (1, 1, SEQ, ROPE),
           (1, 1, MEM, H, XD), (1, 1, MEM, H, XD), (1, DEC, H, P, P), (1, DEC, 3, CONV), (DEC, 1, 1, KVR),
           (DEC, 1, 1, ROPE))


def kernel(**inputs):
    import concourse.bacc as bacc
    from concourse.bass_utils import run_bass_kernel_spmd

    nc = bacc.Bacc("TRN2", target_bir_lowering=False, num_devices=1)
    arrays = {name: np.ascontiguousarray(inputs[name]) for name in INPUTS}
    arrays["const_f32"], arrays["const_bf16"] = constants()
    args = [nc.dram_tensor(f"in_{n}", a.shape, mybir.dt.from_np(a.dtype), kind="ExternalInput").ap()
            for n, a in arrays.items()]
    args += [nc.dram_tensor(f"out_{i}", s, F32, kind="ExternalOutput").ap() for i, s in enumerate(OUTPUTS)]
    build(nc, *args)
    ran = run_bass_kernel_spmd(nc, [{f"in_{n}": a for n, a in arrays.items()}], core_ids=[0])
    return tuple(ran.results[0][f"out_{i}"] for i in range(len(OUTPUTS)))
```

```python
from contextlib import ExitStack

import numpy as np

import concourse.bass as bass
from concourse import mybir

F32 = mybir.dt.float32
BF16 = mybir.dt.bfloat16
I32 = mybir.dt.int32
ALU = mybir.AluOpType
ACT = mybir.ActivationFunctionType
AX = mybir.AxisListType.X

P = 128
D = 1024
KD = D // P
SEQ, DEC = 256, 8
TOK = SEQ + DEC
NT = 3
ROWS = (P, P, DEC)
H = 4
CHUNK = 64
CONV = 1536
CB = CONV // P
TAPS = 4
REST = 1224
Z0, B0, A0, CQ0, CKV0, KR0 = 0, 512, 516, 520, 904, 1160
IN_COLS = CONV + REST
QR, KVR, ROPE, NOPE = 384, 256, 64, 128
QK = NOPE + ROPE
PAST, PAGE = 2048, 128
NPAGE = PAST // PAGE
MLA_SCALE = QK ** -0.5
XD = 256
MEM = 256
NE, TOPK = 32, 4
SLOTS = 64
EPS = 1e-6
NEG = -1e30
LEVELS = 6

C_ID, C_ONE, C_TRI, C_BLK, C_LVL = 0, 128, 256, 384, 512
C_BEF = C_LVL + LEVELS * P
C_CAUS = C_BEF + P
C_IOTA = C_CAUS + P
C_CH2 = C_IOTA + SLOTS
C_SEQ = C_CH2 + 2
C_COS = C_SEQ + 2 * P
C_SIN = C_COS + NT * 32
C_PAGE = C_SIN + NT * 32
C_SUB = C_PAGE + P
C_HEAD = C_SUB + 1
C_ALL = C_HEAD + H

ARENA = 45680
CACHED = (PAST // P) * (KVR + ROPE)
AT_WIN, AT_HEADS, AT_HIST = 0, 22528, 44032

V_CONV, V_MIX, V_MEM, V_X, V_FFN, V_Q, V_GDN, V_ALL = 0, 48, 56, 64, 72, 80, 83, 84


def constants():
    r = np.arange(P)
    row, col = r[:, None], r[None, :]
    c = np.zeros((P, C_ALL), np.float32)
    c[:, C_ID:C_ID + P] = row == col
    c[:, C_ONE:C_ONE + P] = 1.0
    same = row // CHUNK == col // CHUNK
    c[:, C_TRI:C_TRI + P] = (row <= col) & same
    c[:, C_BLK:C_BLK + P] = same
    for m in range(LEVELS):
        c[:, C_LVL + m * P:C_LVL + (m + 1) * P] = (row < col) & ((row ^ col) >> m == 1)
    c[:, C_BEF:C_BEF + P] = row < col
    c[:, C_CAUS:C_CAUS + P] = np.where(col <= row, 0.0, NEG)
    c[:, C_IOTA:C_IOTA + SLOTS] = np.arange(SLOTS)[None, :]
    c[:, C_CH2:C_CH2 + 2] = row // CHUNK == np.arange(2)[None, :]
    for g in range(2):
        c[:, C_SEQ + g * P:C_SEQ + (g + 1) * P] = row == 4 * g + col // 32
    half = ROPE // 2
    freq = (1.0 / (np.float32(10000.0) ** (np.arange(half, dtype=np.float32) / np.float32(half)))).astype(np.float32)
    for t in range(NT):
        pos = (t * P + r if t < 2 else np.full(P, PAST)).astype(np.float32)
        ang = (pos[:, None] * freq[None, :]).astype(np.float32)
        c[:, C_COS + 32 * t:C_COS + 32 * (t + 1)] = np.cos(ang)
        c[:, C_SIN + 32 * t:C_SIN + 32 * (t + 1)] = np.sin(ang)
    c[:, C_PAGE:C_PAGE + P] = row == col // (P // NPAGE)
    c[:, C_SUB] = r % (P // NPAGE)
    c[:, C_HEAD:C_HEAD + H] = row % 32 == np.arange(H)[None, :]
    sel = np.repeat(np.tile(np.eye(NE, dtype=np.float32), (3, 1)), SLOTS, axis=1)
    return c, sel.astype("bfloat16")


class Chain:

    def __init__(self, sem):
        self.sem, self.n = sem, 0

    def link(self, eng, ins):
        self.n += 1
        ins.then_inc(self.sem, 1)
        eng.wait_ge(self.sem, self.n)


class Arena:

    def __init__(self, tensor, at):
        self.tensor, self.at = tensor, at

    def take(self, shape, dt=F32):
        n = int(np.prod(shape[1:])) * (2 if dt is BF16 else 4) // 4
        ap = self.tensor[0:shape[0], self.at:self.at + n]
        self.at += n
        assert self.at <= self.tensor.shape[1], self.at
        if dt is not F32:
            ap = ap.bitcast(dt)
        if len(shape) > 2:
            names = "abcd"[:len(shape) - 1]
            ap = ap.rearrange(f"p ({' '.join(names)}) -> p {' '.join(names)}", **{k: n for k, n in zip(names, shape[1:])})
        return ap


def rep(ap, shape):
    return ap.unsqueeze(len(ap.shape)).broadcast_to(shape)


def rep1(ap, shape):
    return ap.unsqueeze(1).broadcast_to(shape)


def cols(t):
    return slice(t * P, t * P + ROWS[t])


def build(nc, x_prompt, x_sample, state_gdn, state_conv, cache_latent, cache_krope, page_table,
          cache_mem_k, cache_mem_v, mem_prompt, norm_mix, w_in, conv_w, a_log, dt_bias, gdn_norm,
          q_norm, w_uq, kv_norm, w_uk, w_uv, w_out, norm_x, mem_norm, w_xq, w_xk, w_xv, w_xo,
          norm_ffn, w_router, b_router, w_e1, b_e1, w_e2, b_e2, norm_final, const_f32, const_bf16,
          y_prompt, y_sample, gdn_prompt, conv_prompt, lat_prompt, kr_prompt, memk_prompt,
          memv_prompt, gdn_sample, conv_sample, lat_sample, kr_sample):
    ctx = ExitStack()

    recent = []

    def sem(name, lasting=False):
        s = nc.alloc_semaphore(name)
        if not lasting:
            recent.append(s)
        return s

    def clear_semaphores():
        nc.clear_and_free_semaphores(list(recent))
        nc.all_engine_barrier()
        recent.clear()

    def keep(name, shape, dt=F32):
        return nc.alloc_sbuf_tensor(name, shape, dt)

    cst = keep("cst", [P, C_ALL])
    vec = keep("vec", [P, V_ALL])
    res = keep("res", [P, NT, D])
    xnT = keep("xnT", [P, KD, TOK])
    arena = keep("arena", [P, ARENA])
    small = keep("small", [P, 64])
    ps = nc.alloc_psum_tensor("ps", [P, 8, 512], F32)

    def c_(at, n=P, rows=P):
        return cst[0:rows, at:at + n]

    ident = c_(C_ID)
    dve_chain, act_chain, pool_chain = (Chain(sem(n, True)) for n in ("dve_steps", "act_steps", "pool_steps"))
    stored = sem("outputs_stored", True)
    n_stored = [0]

    def store(eng, dst, src):
        n_stored[0] += 16
        eng.dma_start(dst, src).then_inc(stored, 16)

    const_loaded, x_loaded, vec_loaded = sem("const_loaded"), sem("x_loaded", True), sem("vec_loaded")
    vec_turned = sem("vec_turned")
    w_in_loaded = [sem(f"w_in{k}_loaded") for k in range(KD)]
    hist_loaded = sem("history_loaded")
    hist = Arena(arena, AT_HIST).take([DEC * 3, CONV])
    win = Arena(arena, AT_WIN).take([P, KD, IN_COLS])
    with nc.Block() as block:
        vrow = Arena(arena, AT_HEADS).take([V_ALL, P])

        @block.sync
        def _(sp):
            sp.dma_start(res[:, 0:2, :], x_prompt[0].rearrange("(t p) d -> p t d", p=P)).then_inc(x_loaded, 16)
            sp.dma_start(res[0:DEC, 2, :], x_sample[:, 0, :]).then_inc(x_loaded, 16)
            sp.dma_start(hist, state_conv[0].rearrange("b j c -> (b j) c")).then_inc(hist_loaded, 16)
            sp.wait_ge(const_loaded, 16)
            sp.wait_ge(vec_loaded, 7 * 16)
            for k in range(KD):
                sp.dma_start(win[:, k, :], w_in[0, k * P:(k + 1) * P, :]).then_inc(w_in_loaded[k], 16)

        @block.scalar
        def _(act):
            act.dma_start(cst[:, :], const_f32).then_inc(const_loaded, 16)
            for at, v, n in ((V_MIX, norm_mix, KD), (V_MEM, mem_norm, KD), (V_X, norm_x, KD),
                             (V_FFN, norm_ffn, KD), (V_Q, q_norm, 3), (V_GDN, gdn_norm, 1)):
                act.dma_start(vrow[at:at + n, :], v[0].rearrange("(k p) -> k p", p=P)).then_inc(vec_loaded, 16)
            act.dma_start(vrow[V_CONV:V_MIX, :], conv_w[0].rearrange("j (c p) -> (j c) p", p=P)).then_inc(vec_loaded, 16)

        @block.tensor
        def _(pe):
            pe.wait_ge(const_loaded, 16)
            pe.wait_ge(vec_loaded, 7 * 16)
            pe.transpose(ps[:, 0, 0:V_ALL], vrow[:, :], c_(C_ID, V_ALL, V_ALL)).then_inc(vec_turned, 1)

        @block.vector
        def _(dve):
            dve.memset(small[:, :], 0.0)
            dve.wait_ge(vec_turned, 1)
            dve.tensor_copy(vec[:, :], ps[:, 0, 0:V_ALL])

    def normed_transposed(tag, src, tiles, gain_at, ready, ready_at, at, kept=None):
        squared, varied, rooted, scaled = (sem(f"{tag}_{n}") for n in ("squared", "varied", "rooted", "scaled"))
        turned, emptied = sem(f"{tag}_turned"), sem(f"{tag}_emptied")
        with nc.Block() as block:
            place_of = Arena(arena, at)
            junk = place_of.take([P, D])
            xs = place_of.take([P, 2, D]) if kept is None else kept
            n = len(tiles)
            place = [i % 2 if kept is None else i for i in range(n)]

            @block.scalar
            def _(act):
                act.wait_ge(ready, ready_at)
                for t in tiles:
                    act_chain.link(act, nc.scalar.activation(junk[0:ROWS[t], :], src[0:ROWS[t], t, :], ACT.Square,
                                                            accum_out=small[0:ROWS[t], t:t + 1]))
                nc.scalar.copy(small[:, 3:4], small[:, 3:4]).then_inc(squared, 1)
                act.wait_ge(varied, 1)
                nc.scalar.activation(small[:, 4:4 + n], small[:, 4:4 + n], ACT.Sqrt).then_inc(rooted, 1)

            @block.vector
            def _(dve):
                dve.wait_ge(squared, 1)
                nc.vector.tensor_scalar(small[:, 4:4 + n], small[:, 0:n], 1.0 / D, EPS, ALU.mult, ALU.add).then_inc(varied, 1)
                dve.wait_ge(rooted, 1)
                dve_chain.link(dve, nc.vector.reciprocal(small[:, 8:8 + n], small[:, 4:4 + n]))
                for i, t in enumerate(tiles):
                    r = ROWS[t]
                    if i >= 2 and kept is None:
                        dve.wait_ge(turned, 2 * (i - 1))
                    nc.vector.tensor_scalar(xs[0:r, place[i], :], src[0:r, t, :], small[0:r, 8 + t:9 + t], None, ALU.mult).then_inc(scaled, 1)
                    for j in range(2):
                        dve.wait_ge(turned, 2 * i + j + 1)
                        nc.vector.tensor_tensor(xnT[:, 4 * j:4 * j + 4, cols(t)],
                                                ps[:, (2 * i + j) % 8, :].rearrange("p (k n) -> p k n", k=4)[:, :, 0:r],
                                                rep(vec[:, gain_at + 4 * j:gain_at + 4 * j + 4], [P, 4, r]), ALU.mult).then_inc(emptied, 1)

            @block.tensor
            def _(pe):
                for i, t in enumerate(tiles):
                    r = ROWS[t]
                    pe.wait_ge(scaled, i + 1)
                    for j in range(2):
                        for k in range(4):
                            last = pe.transpose(ps[:, (2 * i + j) % 8, k * P:k * P + r],
                                                xs[0:r, place[i], (4 * j + k) * P:(4 * j + k + 1) * P], c_(C_ID, r, r))
                        last.then_inc(turned, 1)

    normed_transposed("mix", res, (0, 1, 2), V_MIX, x_loaded, 32, AT_HEADS)

    heads = Arena(arena, AT_HEADS)
    qkv = heads.take([P, CB, TOK])
    rest = heads.take([P, NT, REST])
    AT_STATES = heads.at
    cp = heads.take([P, CB, SEQ + TAPS - 1])
    cs = heads.take([P, CB, DEC, TAPS])
    tail = heads.take([3 + DEC, CONV])
    tmp = heads.take([P, CB, DEC])
    raw = heads.take([P, CB, 3 + DEC])
    sig = heads.take([P, CB, TOK])
    yT = xnT
    REST_CUTS = ((0, 512), (512, 904), (904, REST))
    QUARTER = REST // 4
    conv_proj, conv_moved = sem("conv_projected"), sem("conv_moved")
    rest_proj, rest_moved = sem("rest_projected"), sem("rest_moved")
    hist_turned = sem("history_turned")
    hist_moved, raw_moved = sem("history_moved"), sem("raw_moved")
    rest_cleared = sem("rest_cleared")
    tail_turned, tail_moved = sem("tail_turned"), sem("tail_moved")
    conv_done, sig_done = sem("conv_done"), sem("conv_sigmoid_done")
    with nc.Block() as block:
        @block.sync
        def _(sp):
            store(sp, conv_sample[0, :, 0:2, :], state_conv[0, :, 1:3, :])
            sp.wait_ge(tail_moved, 3)
            store(sp, conv_prompt[0, 0], tail[0:3, :])
            store(sp, conv_sample[0, :, 2, :], tail[3:3 + DEC, :])
            sp.wait_ge(stored, n_stored[0])

        @block.tensor
        def _(pe):
            pe.wait_ge(hist_loaded, 16)
            for c in range(CB):
                last = pe.transpose(ps[:, 7, c * 24:(c + 1) * 24], hist[:, c * P:(c + 1) * P], c_(C_ID, 24, 24))
            last.then_inc(hist_turned, 1)
            pe.wait_ge(hist_moved, 1)
            for k in range(KD):
                pe.wait_ge(w_in_loaded[k], 16)
                for c in range(8):
                    last = pe.matmul(ps[:, c, 0:TOK], win[:, k, c * P:(c + 1) * P], xnT[:, k, :],
                                     start=(k == 0), stop=(k == KD - 1))
                    if k == KD - 1:
                        last.then_inc(conv_proj, 1)
            for c in range(8, CB):
                pe.wait_ge(conv_moved, c - 7)
                for k in range(KD):
                    last = pe.matmul(ps[:, c % 8, 0:TOK], win[:, k, c * P:(c + 1) * P], xnT[:, k, :],
                                     start=(k == 0), stop=(k == KD - 1))
                last.then_inc(conv_proj, 1)
            n = 0
            for t in range(2):
                for a, b in REST_CUTS:
                    if n < 3:
                        pe.wait_ge(conv_moved, 5 + n)
                    else:
                        pe.wait_ge(rest_moved, n - 2)
                    for k in range(KD):
                        last = pe.matmul(ps[:, 4 + n % 3, 0:b - a], xnT[:, k, cols(t)],
                                         win[:, k, CONV + a:CONV + b], start=(k == 0), stop=(k == KD - 1))
                    last.then_inc(rest_proj, 1)
                    n += 1
            pe.wait_ge(conv_moved, 8)
            for k in range(KD):
                for j in range(4):
                    a = CONV + QUARTER * j
                    last = pe.matmul(ps[32 * j:32 * j + DEC, 7, 0:QUARTER], xnT[:, k, cols(2)], win[:, k, a:a + QUARTER],
                                     start=(k == 0), stop=(k == KD - 1), tile_position=(0, 32 * j))
            last.then_inc(rest_proj, 1)
            pe.wait_ge(raw_moved, 1)
            for j in range(3):
                for c in range(4):
                    last = pe.transpose(ps[0:3 + DEC, j, c * P:(c + 1) * P], raw[:, 4 * j + c, :], ident)
                last.then_inc(tail_turned, 1)

        @block.vector
        def _(dve):
            link = lambda ins: dve_chain.link(dve, ins)
            nc.vector.memset(rest[:, 2, :], 0.0).then_inc(rest_cleared, 1)
            link(nc.vector.memset(cp[:, :, 0:TAPS - 1], 0.0))
            dve.wait_ge(hist_turned, 1)
            nc.vector.tensor_copy(cs[:, :, :, 0:3], ps[:, 7, 0:CB * 24].rearrange("p (c b j) -> p c b j", c=CB, j=3)).then_inc(hist_moved, 1)
            for c in range(CB):
                dve.wait_ge(conv_proj, c + 1)
                nc.vector.tensor_copy(cs[:, c, :, 3], ps[:, c % 8, SEQ:TOK])
                nc.vector.tensor_copy(raw[:, c, :], ps[:, c % 8, SEQ - 3:TOK])
                link(nc.vector.tensor_copy(cp[:, c, 3:3 + SEQ], ps[:, c % 8, 0:SEQ]))
                nc.vector.tensor_copy(small[:, 63:64], small[:, 62:63]).then_inc(conv_moved, 1)
                for j in range(TAPS):
                    w = vec[:, V_CONV + CB * j + c:V_CONV + CB * j + c + 1]
                    if j == 0:
                        link(nc.vector.tensor_scalar(qkv[:, c, 0:SEQ], cp[:, c, j:j + SEQ], w, None, ALU.mult))
                    else:
                        link(nc.vector.scalar_tensor_tensor(qkv[:, c, 0:SEQ], cp[:, c, j:j + SEQ], w, qkv[:, c, 0:SEQ], ALU.mult, ALU.add))
            nc.vector.tensor_copy(small[:, 63:64], small[:, 62:63]).then_inc(raw_moved, 1)
            for j in range(TAPS):
                w = rep(vec[:, V_CONV + CB * j:V_CONV + CB * (j + 1)], [P, CB, DEC])
                if j == 0:
                    link(nc.vector.tensor_tensor(qkv[:, :, SEQ:TOK], cs[:, :, :, 0], w, ALU.mult))
                else:
                    link(nc.vector.tensor_tensor(tmp, cs[:, :, :, j], w, ALU.mult))
                    link(nc.vector.tensor_tensor(qkv[:, :, SEQ:TOK], qkv[:, :, SEQ:TOK], tmp, ALU.add))
            nc.vector.tensor_copy(small[:, 63:64], small[:, 62:63]).then_inc(conv_done, 1)
            dve.wait_ge(sig_done, 1)
            nc.vector.tensor_tensor(qkv[:, :, 0:TOK], qkv[:, :, 0:TOK], sig, ALU.mult)
            for j in range(3):
                dve.wait_ge(tail_turned, j + 1)
                nc.vector.tensor_copy(tail[:, 4 * P * j:4 * P * (j + 1)], ps[0:3 + DEC, j, :]).then_inc(tail_moved, 1)

        @block.scalar
        def _(act):
            act.wait_ge(rest_cleared, 1)
            n = 0
            for t in range(2):
                for a, b in REST_CUTS:
                    act.wait_ge(rest_proj, n + 1)
                    nc.scalar.copy(rest[:, t, a:b], ps[:, 4 + n % 3, 0:b - a]).then_inc(rest_moved, 1)
                    n += 1
            act.wait_ge(rest_proj, n + 1)
            for j in range(4):
                nc.scalar.copy(rest[0:DEC, 2, QUARTER * j:QUARTER * (j + 1)], ps[32 * j:32 * j + DEC, 7, 0:QUARTER])
            act.wait_ge(conv_done, 1)
            nc.scalar.activation(sig, qkv[:, :, :], ACT.Sigmoid).then_inc(sig_done, 1)
    AT_SLOTS = 2 * CACHED
    keepers = Arena(arena, AT_STATES)
    st = keepers.take([P, DEC * H, P])
    otok = keepers.take([P, NT, H, P])
    S = keepers.take([P, H, P])
    gsb = keepers.take([P, 104])
    eg = keepers.take([P, 104])
    gw = keepers.take([P, 8, NT * H])
    alog = keepers.take([P, H])
    dtb = keepers.take([P, H])
    kts, dts = keepers.take([DEC, H, P]), keepers.take([DEC, H, P])
    dT, oT, pr = (keepers.take([P, H, DEC]) for _ in range(3))
    mtake = lambda name, shape, dt=F32: keepers.take(shape, dt)
    AT_LATENT = keepers.at
    latT = mtake("latT", [P, 2, TOK])
    krT = mtake("krT", [P, TOK])
    qnT = mtake("qnT", [P, H, TOK])
    qrT = mtake("qrT", [P, H, TOK])
    kvn = mtake("kvn", [P, KVR])
    ukT = keepers.take([P, H, KVR])
    assert keepers.at - AT_LATENT >= PAST // P * KVR
    brief = Arena(arena, AT_SLOTS)
    ptake = lambda name, shape, dt=F32: brief.take(shape, dt)
    cqT = ptake("cqT", [P, 3, TOK])
    knT = ptake("knT", [P, H, SEQ])
    vtok = ptake("vtok", [P, 2, H * P])
    qr = ptake("qr", [P, NT, H * ROPE])
    kr = ptake("kr", [P, NT, ROPE])
    rt = ptake("rope_tmp", [P, NT, H, 32])
    uq = brief.take([P, 3, H, QK])
    sc = brief.take([P, H, 384])
    pT = brief.take([P, H, 384])
    upper = Arena(arena, AT_SLOTS + 10 * 1024)
    uk, uv = upper.take([P, 2, H, NOPE]), upper.take([P, 2, H, P])
    qlp = keepers.take([P, 2, DEC, 32])
    qrp = keepers.take([P, 2, DEC, 32])
    KT = keepers.take([P, 2, 2, 640])
    snew = keepers.take([DEC, DEC, H])
    idx = keepers.take([P, DEC], I32)
    idxf = keepers.take([P, DEC])
    pgi = keepers.take([NPAGE, DEC], I32)
    pgf = keepers.take([NPAGE, DEC])
    lmax, nmax, lsum = (keepers.take([P, DEC]) for _ in range(3))
    early = res[:, :, :].rearrange("p t n -> p (t n)")
    Pb = early[:, 0:512]
    PT = early[:, 512:1024].rearrange("p (m n) -> p m n", m=4)
    acc = early[:, 1024:1024 + DEC * KVR].rearrange("p (b n) -> p b n", b=DEC)
    ml = {n: sem("mla_" + n) for n in ("w_loaded", "kvn_loaded", "squared", "var", "root", "lat_ready", "kr_ready", "turned",
                                       "moved", "proj", "proj_moved", "qr_made", "qr_ready", "qr_turned", "k_made", "k_moved", "pages", "pages_f", "pages_spread", "idx", "uk_turned", "uk_moved", "ql_made", "ql_ready", "snew")}

    def rope(dve, dst, src, tmp, cos, sin):
        half = ROPE // 2
        x1, x2 = (src[..., 0:half], src[..., half:ROPE])
        o1, o2 = (dst[..., 0:half], dst[..., half:ROPE])
        nc.vector.tensor_tensor(o1, x1, cos, ALU.mult)
        dve_chain.link(dve, nc.vector.tensor_tensor(tmp, x2, sin, ALU.mult))
        nc.vector.tensor_tensor(o1, o1, tmp, ALU.subtract)
        dve_chain.link(dve, nc.vector.tensor_tensor(o2, x2, cos, ALU.mult))
        dve_chain.link(dve, nc.vector.tensor_tensor(tmp, x1, sin, ALU.mult))
        return nc.vector.tensor_tensor(o2, o2, tmp, ALU.add)

    TILES = PAST // P
    cached = Arena(arena, 0)
    lat_slots, kr_slots = [], []
    for _ in range(2):
        lat_slots.append(cached.take([P, TILES, KVR]))
        kr_slots.append(cached.take([P, TILES, ROPE]))
    lat_slots.append(Arena(arena, AT_LATENT).take([P, TILES, KVR]))
    kr_slots.append(Arena(arena, AT_SLOTS + 10 * 1024).take([P, TILES, ROPE]))
    NSLOT = len(lat_slots)
    seq_loaded = [sem(f"sequence_slot{i}_loaded", True) for i in range(NSLOT)]
    lat_rows = cache_latent.rearrange("n l (r s) d -> (n l r) (s d)", r=P // NPAGE)
    kr_rows = cache_krope.rearrange("n l (r s) d -> (n l r) (s d)", r=P // NPAGE)

    def load_sequence(pool, b):
        for slots, rows in ((lat_slots, lat_rows), (kr_slots, kr_rows)):
            pool.indirect_dma_start(slots[b % NSLOT].rearrange("p i n -> p (i n)"), None, rows,
                                    bass.IndirectOffsetOnAxis(ap=idx[:, b:b + 1].bitcast(mybir.dt.uint32), axis=0)).then_inc(seq_loaded[b % NSLOT], 16)

    cos3 = cst[:, C_COS:C_COS + NT * 32].rearrange("p (t n) -> p t n", t=NT)
    sin3 = cst[:, C_SIN:C_SIN + NT * 32].rearrange("p (t n) -> p t n", t=NT)
    with nc.Block() as block:
        @block.sync
        def _(sp):
            sp.dma_start(pgi, page_table.rearrange("b j -> j b"), allow_slow_non_contiguous=True).then_inc(ml["pages"], 16)
            sp.dma_start(kvn[:, :], kv_norm[0].partition_broadcast(P)).then_inc(ml["kvn_loaded"], 16)
            sp.dma_start(uq, w_uq[0].rearrange("(k p) h n -> p k h n", p=P)).then_inc(ml["w_loaded"], 16)
            sp.dma_start(uk, w_uk[0].rearrange("(k p) h n -> p k h n", p=P)).then_inc(ml["w_loaded"], 16)
            sp.dma_start(uv, w_uv[0].rearrange("(k p) h n -> p k h n", p=P)).then_inc(ml["w_loaded"], 16)
            sp.wait_ge(ml["lat_ready"], 1)
            store(sp, lat_prompt[0, 0].rearrange("(t p) n -> p t n", p=P), rest[:, 0:2, CKV0:CKV0 + KVR])
            store(sp, lat_sample[:, 0, 0, :], rest[0:DEC, 2, CKV0:CKV0 + KVR])
            sp.wait_ge(ml["kr_ready"], 1)
            store(sp, kr_prompt[0, 0].rearrange("(t p) n -> p t n", p=P), kr[:, 0:2, :])
            store(sp, kr_sample[:, 0, 0, :], kr[0:DEC, 2, :])
            sp.wait_ge(stored, n_stored[0])

        @block.gpsimd
        def _(pool):
            pool.wait_ge(ml["idx"], 1)
            for b in range(2):
                load_sequence(pool, b)

        @block.scalar
        def _(act):
            junk = qr[:, :, :].rearrange("p t n -> p (t n)")
            for t in range(NT):
                act_chain.link(act, nc.scalar.activation(junk[:, 0:QR], rest[:, t, CQ0:CQ0 + QR], ACT.Square, accum_out=small[:, 12 + t:13 + t]))
                act_chain.link(act, nc.scalar.activation(junk[:, 0:KVR], rest[:, t, CKV0:CKV0 + KVR], ACT.Square, accum_out=small[:, 15 + t:16 + t]))
            nc.scalar.copy(small[:, 60:61], small[:, 12:13]).then_inc(ml["squared"], 1)
            act.wait_ge(ml["var"], 1)
            nc.scalar.activation(small[:, 18:24], small[:, 18:24], ACT.Sqrt).then_inc(ml["root"], 1)
            for h in range(H):
                act.wait_ge(ml["proj"], h + 1)
                nc.scalar.copy(qnT[:, h, :], ps[:, h, 0:TOK]).then_inc(ml["proj_moved"], 1)
            for h in range(H):
                act.wait_ge(ml["k_made"], h + 1)
                nc.scalar.copy(knT[:, h, :], ps[:, h, 0:SEQ]).then_inc(ml["k_moved"], 1)
            for t in range(2):
                act.wait_ge(ml["k_made"], H + t + 1)
                nc.scalar.copy(vtok[:, t, :], ps[:, 7 * t, :])

        @block.vector
        def _(dve):
            link = lambda ins: dve_chain.link(dve, ins)
            nc.vector.memset(krT[:, :], 0.0)
            dve.wait_ge(ml["pages"], 16)
            nc.vector.tensor_copy(pgf, pgi).then_inc(ml["pages_f"], 1)
            link(nc.vector.memset(qrT[:, :, :], 0.0))
            link(rope(dve, kr[:, :, :], rest[:, :, KR0:KR0 + ROPE], rt[:, :, 0, :], cos3, sin3))
            nc.vector.tensor_copy(small[:, 61:62], small[:, 62:63]).then_inc(ml["kr_ready"], 1)
            dve.wait_ge(ml["squared"], 1)
            nc.vector.tensor_scalar(small[:, 18:21], small[:, 12:15], 1.0 / QR, EPS, ALU.mult, ALU.add)
            nc.vector.tensor_scalar(small[:, 21:24], small[:, 15:18], 1.0 / KVR, EPS, ALU.mult, ALU.add).then_inc(ml["var"], 1)
            dve.wait_ge(ml["root"], 1)
            link(nc.vector.reciprocal(small[:, 24:30], small[:, 18:24]))
            dve.wait_ge(ml["kvn_loaded"], 16)
            for t in range(NT):
                cq = rest[:, t, CQ0:CQ0 + QR]
                ck = rest[:, t, CKV0:CKV0 + KVR]
                nc.vector.tensor_scalar(cq, cq, small[:, 24 + t:25 + t], None, ALU.mult)
                last = nc.vector.scalar_tensor_tensor(ck, ck, small[:, 27 + t:28 + t], kvn[:, :], ALU.mult, ALU.mult)
            last.then_inc(ml["lat_ready"], 1)
            dve.wait_ge(ml["pages_spread"], 1)
            link(nc.vector.tensor_copy(idxf, ps[:, 7, 0:DEC]))
            nc.vector.tensor_scalar(idx, idxf, float(P // NPAGE), c_(C_SUB, 1), ALU.mult, ALU.add).then_inc(ml["idx"], 1)
            for t in range(NT):
                r = ROWS[t]
                dve.wait_ge(ml["turned"], t + 1)
                nc.vector.tensor_tensor(cqT[:, :, cols(t)], ps[:, 2 * t, 0:3 * P].rearrange("p (k n) -> p k n", k=3)[:, :, 0:r],
                                        rep(vec[:, V_Q:V_Q + 3], [P, 3, r]), ALU.mult)
                nc.vector.tensor_copy(latT[:, :, cols(t)], ps[:, 2 * t + 1, 0:2 * P].rearrange("p (k n) -> p k n", k=2)[:, :, 0:r])
                nc.vector.tensor_copy(krT[0:ROPE, cols(t)], ps[0:ROPE, 2 * t + 1, 2 * P:2 * P + r]).then_inc(ml["moved"], 1)
            link(nc.vector.memset(qr[:, 2, :], 0.0))
            for t in range(NT):
                dve.wait_ge(ml["qr_made"], t + 1)
                r = ROWS[t]
                src = ps[0:r, 4 + t, 0:H * ROPE].rearrange("p (h n) -> p h n", h=H)
                link(rope(dve, qr[0:r, t, :].rearrange("p (h n) -> p h n", h=H), src, rt[0:r, t], rep1(cos3[0:r, t, :], [r, H, 32]),
                          rep1(sin3[0:r, t, :], [r, H, 32])))
            nc.vector.tensor_copy(small[:, 61:62], small[:, 62:63]).then_inc(ml["qr_ready"], 1)
            for t in range(NT):
                r = ROWS[t]
                dve.wait_ge(ml["qr_turned"], t + 1)
                nc.vector.tensor_copy(qrT[0:ROPE, :, cols(t)], ps[0:ROPE, 4 + t, :].rearrange("p (h n) -> p h n", h=H)[:, :, 0:r])

        @block.tensor
        def _(pe):
            pe.wait_ge(ml["pages_f"], 1)
            pe.matmul(ps[:, 7, 0:DEC], c_(C_PAGE, P, NPAGE), pgf, start=True, stop=True).then_inc(ml["pages_spread"], 1)
            pe.wait_ge(ml["lat_ready"], 1)
            pe.wait_ge(ml["kr_ready"], 1)
            for t in range(NT):
                r = ROWS[t]
                i = c_(C_ID, r, r)
                for k in range(3):
                    pe.transpose(ps[:, 2 * t, k * P:k * P + r], rest[0:r, t, CQ0 + k * P:CQ0 + (k + 1) * P], i)
                for k in range(2):
                    pe.transpose(ps[:, 2 * t + 1, k * P:k * P + r], rest[0:r, t, CKV0 + k * P:CKV0 + (k + 1) * P], i)
                pe.transpose(ps[0:ROPE, 2 * t + 1, 2 * P:2 * P + r], kr[0:r, t, :], i).then_inc(ml["turned"], 1)
            pe.wait_ge(ml["w_loaded"], 48)
            pe.wait_ge(ml["moved"], NT)
            for t in range(NT):
                for k in range(3):
                    last = pe.matmul(ps[0:ROWS[t], 4 + t, 0:H * ROPE], cqT[:, k, cols(t)], uq[:, k, :, NOPE:QK], start=(k == 0), stop=(k == 2))
                last.then_inc(ml["qr_made"], 1)
            for h in range(H):
                for k in range(3):
                    last = pe.matmul(ps[:, h, 0:TOK], uq[:, k, h, 0:NOPE], cqT[:, k, :], start=(k == 0), stop=(k == 2))
                last.then_inc(ml["proj"], 1)
            for h in range(H):
                pe.wait_ge(ml["proj_moved"], h + 1)
                for k in range(2):
                    last = pe.matmul(ps[:, h, 0:SEQ], uk[:, k, h, :], latT[:, k, 0:SEQ], start=(k == 0), stop=(k == 1))
                last.then_inc(ml["k_made"], 1)
            pe.wait_ge(ml["qr_ready"], 1)
            for t in range(NT):
                r = ROWS[t]
                for h in range(H):
                    last = pe.transpose(ps[0:ROPE, 4 + t, h * P:h * P + r], qr[0:r, t, h * ROPE:(h + 1) * ROPE], c_(C_ID, r, r))
                last.then_inc(ml["qr_turned"], 1)
            for t in range(2):
                if t == 0:
                    pe.wait_ge(ml["k_moved"], 1)
                for k in range(2):
                    last = pe.matmul(ps[:, 7 * t, :], latT[:, k, cols(t)], uv[:, k, :, :], start=(k == 0), stop=(k == 1))
                last.then_inc(ml["k_made"], 1)

    mx = small[:, 30:38]
    ap = {n: sem("att_" + n) for n in ("scored", "max", "exp", "probs", "turned", "pt_ready", "out")}
    with nc.Block() as block:
        @block.tensor
        def _(pe):
            for h in range(H):
                for a, n, q in ((0, P, 0), (P, SEQ, P)):
                    pe.matmul(ps[:, h, a:a + n], qnT[:, h, q:q + P], knT[:, h, 0:n], start=True, stop=False)
                    last = pe.matmul(ps[:, h, a:a + n], qrT[:, h, q:q + P], krT[:, 0:n], start=False, stop=True)
            last.then_inc(ap["scored"], 1)
            for h in range(H):
                for k in range(2):
                    last = pe.transpose(ps[:, 4 + h // 2, (2 * (h % 2) + k) * P:(2 * (h % 2) + k + 1) * P], uk[:, k, h, :], ident)
            last.then_inc(ml["uk_turned"], 1)
            pe.wait_ge(ml["uk_moved"], 1)
            for h in range(H):
                for k in range(2):
                    a = (k * H + h) * DEC
                    last = pe.matmul(ps[:, 6, a:a + DEC], ukT[:, h, k * P:(k + 1) * P], qnT[:, h, SEQ:TOK], start=True, stop=True)
            last.then_inc(ml["ql_made"], 1)
            pe.wait_ge(ml["ql_ready"], 1)
            for k in range(2):
                pe.matmul(ps[0:DEC, 7, 0:DEC * H], latT[:, k, SEQ:TOK], qlp[:, k, :, 0:H], start=(k == 0), stop=False)
            pe.matmul(ps[0:DEC, 7, 0:DEC * H], krT[:, SEQ:TOK], qrp[:, 0, :, 0:H], start=False, stop=True).then_inc(ml["snew"], 1)
            pe.wait_ge(ap["probs"], 1)
            for h in range(H):
                for j in range(3):
                    last = pe.transpose(ps[:, h, j * P:(j + 1) * P], sc[:, h, j * P:(j + 1) * P], ident)
                last.then_inc(ap["turned"], 1)
            for h in range(H):
                pe.wait_ge(ap["pt_ready"], h + 1)
                pe.matmul(ps[:, h, 0:P], vtok[:, 0, h * P:(h + 1) * P], pT[:, h, 0:P], start=True, stop=True)
                pe.matmul(ps[:, h, P:SEQ], vtok[:, 0, h * P:(h + 1) * P], pT[:, h, P:SEQ], start=True, stop=False)
                pe.matmul(ps[:, h, P:SEQ], vtok[:, 1, h * P:(h + 1) * P], pT[:, h, SEQ:384], start=False, stop=True).then_inc(ap["out"], 1)

        @block.vector
        def _(dve):
            link = lambda ins: dve_chain.link(dve, ins)
            nc.vector.memset(qlp, 0.0)
            link(nc.vector.memset(qrp, 0.0))
            nc.vector.tensor_copy(qrp[0:ROPE, 0, :, 0:H].rearrange("p b h -> p h b"), qrT[0:ROPE, :, SEQ:TOK])
            nc.vector.tensor_copy(qrp[ROPE:P, 1, :, 0:H].rearrange("p b h -> p h b"), qrT[0:ROPE, :, SEQ:TOK])
            dve.wait_ge(ml["uk_turned"], 1)
            nc.vector.tensor_copy(ukT, ps[:, 4:6, :].rearrange("p a (h n) -> p (a h) n", h=2)).then_inc(ml["uk_moved"], 1)
            dve.wait_ge(ap["scored"], 1)
            for a in (0, SEQ):
                nc.vector.tensor_tensor(sc[:, :, a:a + P], ps[:, 0:H, a:a + P], rep1(c_(C_CAUS), [P, H, P]), ALU.add)
            link(nc.vector.tensor_copy(sc[:, :, P:SEQ], ps[:, 0:H, P:SEQ]))
            nc.vector.tensor_reduce(mx[:, 0:H], sc[:, :, 0:P], AX, ALU.max)
            link(nc.vector.tensor_reduce(mx[:, H:2 * H], sc[:, :, P:384], AX, ALU.max))
            nc.vector.tensor_scalar(mx, mx, -MLA_SCALE, None, ALU.mult).then_inc(ap["max"], 1)
            dve.wait_ge(ml["ql_made"], 1)
            for k in range(2):
                last = nc.vector.tensor_copy(qlp[:, k, :, 0:H].rearrange("p b h -> p h b"), ps[:, 6, k * 32:k * 32 + 32].rearrange("p (h b) -> p h b", h=H))
            last.then_inc(ml["ql_ready"], 1)
            dve.wait_ge(ml["snew"], 1)
            nc.vector.tensor_tensor(snew, ps[0:DEC, 7, 0:DEC * H].rearrange("p (b h) -> p b h", b=DEC), rep(c_(C_ID, DEC, DEC), [DEC, DEC, H]), ALU.mult)
            dve.wait_ge(ap["exp"], 1)
            link(nc.vector.reciprocal(small[:, 38:46], small[:, 38:46]))
            nc.vector.tensor_tensor(sc[:, :, 0:P], sc[:, :, 0:P], rep(small[:, 38:42], [P, H, P]), ALU.mult)
            nc.vector.tensor_tensor(sc[:, :, P:384], sc[:, :, P:384], rep(small[:, 42:46], [P, H, SEQ]), ALU.mult).then_inc(ap["probs"], 1)
            for h in range(H):
                dve.wait_ge(ap["turned"], h + 1)
                nc.vector.tensor_copy(pT[:, h, :], ps[:, h, 0:384]).then_inc(ap["pt_ready"], 1)
            for h in range(H):
                dve.wait_ge(ap["out"], h + 1)
                nc.vector.tensor_copy(yT[:, H + h, 0:SEQ], ps[:, h, 0:SEQ])

        @block.scalar
        def _(act):
            act.wait_ge(ap["max"], 1)
            for h in range(H):
                for j, (a, b) in enumerate(((0, P), (P, 384))):
                    i = j * H + h
                    act_chain.link(act, nc.scalar.activation(sc[:, h, a:b], sc[:, h, a:b], ACT.Exp, bias=mx[:, i:i + 1], scale=MLA_SCALE,
                                                             accum_out=small[:, 38 + i:39 + i]))
            nc.scalar.copy(small[:, 60:61], small[:, 38:39]).then_inc(ap["exp"], 1)
    clear_semaphores()

    G_CUM, G_TOT, G_CH, G_SMP, G_BSMP, G_LEFT = 0, 8, 16, 32, 64, 96
    slots = Arena(arena, AT_SLOTS)
    decT, X, CT, qTe, iT, kd, LT, kbe, vb, XT = (slots.take([P, 2, H, P]) for _ in range(10))
    Y, u, vnew, wT = decT, decT, X, CT
    delta = Arena(arena, AT_SLOTS + 6 * 1024).take([DEC, H, DEC, P])
    sq = Arena(arena, AT_STATES).take([P, 2 * H, TOK])
    rk = small[:, 30:54]
    g, beta = gw[:, 6, :].rearrange("p (t h) -> p t h", h=H), gw[:, 7, :].rearrange("p (t h) -> p t h", h=H)
    state_loaded = sem("state_loaded")
    decay_loaded = sem("decay_loaded")
    g1 = {n: sem("gdn_" + n) for n in (
        "squared", "rows_made", "summed", "added", "rooted", "inverted", "normed", "neg_abs", "exp", "plus1", "ln", "gates", "sums", "sums_read",
        "exp_sums", "rows_exp", "row_min", "dec_exp", "turned", "turned_read", "products", "left", "rows_read", "rows_beta_read")}
    with nc.Block() as block:
        @block.sync
        def _(sp):
            sp.dma_start(alog[:, :], a_log[0].partition_broadcast(P)).then_inc(decay_loaded, 16)
            sp.dma_start(dtb[:, :], dt_bias[0].partition_broadcast(P)).then_inc(decay_loaded, 16)
            sp.wait_ge(g1["rows_made"], 1)
            sp.dma_start(st[:, :, :], state_gdn[0].rearrange("b h k v -> k (b h) v")).then_inc(state_loaded, 16)

        @block.gpsimd
        def _(pool):
            load_sequence(pool, 2)

        @block.scalar
        def _(act):
            nc.scalar.activation(sq[:, :, :], qkv[:, 0:2 * H, :], ACT.Square).then_inc(g1["squared"], 1)
            act.wait_ge(g1["added"], 1)
            nc.scalar.activation(rk, rk, ACT.Sqrt).then_inc(g1["rooted"], 1)
            act.wait_ge(decay_loaded, 32)
            nc.scalar.activation(alog[:, :], alog[:, :], ACT.Exp)
            nc.scalar.activation(gw[:, 4, :].rearrange("p (t h) -> p t h", h=H), rest[:, :, B0:B0 + H], ACT.Exp, scale=-1.0)
            act.wait_ge(g1["neg_abs"], 1)
            nc.scalar.activation(gw[:, 2, :], gw[:, 1, :], ACT.Exp).then_inc(g1["exp"], 1)
            act.wait_ge(g1["plus1"], 1)
            nc.scalar.activation(gw[:, 3, :], gw[:, 2, :], ACT.Ln).then_inc(g1["ln"], 1)
            act.wait_ge(g1["sums"], 1)
            for t in range(2):
                nc.scalar.activation(qTe[:, t].rearrange("p h n -> p (h n)"), ps[:, 1 + t, :], ACT.Exp).then_inc(g1["rows_exp"], 1)
            act.wait_ge(g1["sums_read"], 1)
            nc.scalar.activation(eg[:, :], gsb[:, :], ACT.Exp).then_inc(g1["exp_sums"], 1)
            act.wait_ge(g1["row_min"], 1)
            nc.scalar.activation(decT[:, :, :, :], decT[:, :, :, :], ACT.Exp).then_inc(g1["dec_exp"], 1)

        @block.vector
        def _(dve):
            link = lambda ins: dve_chain.link(dve, ins)
            dve.wait_ge(g1["summed"], 1)
            link(nc.vector.memset(rk, 1.0))
            for t in range(NT):
                r = ROWS[t]
                nc.vector.tensor_scalar(rk[0:r, 8 * t:8 * t + H], ps[0:r, 0, 8 * t:8 * t + H], EPS, float(P), ALU.add, ALU.mult)
                last = nc.vector.tensor_scalar(rk[0:r, 8 * t + H:8 * t + 2 * H], ps[0:r, 0, 8 * t + H:8 * t + 2 * H], EPS, None, ALU.add)
            last.then_inc(g1["added"], 1)
            dve.wait_ge(g1["rooted"], 1)
            nc.vector.reciprocal(rk, rk).then_inc(g1["inverted"], 1)
            dve.wait_ge(decay_loaded, 32)
            a3 = gw[:, 0, :].rearrange("p (t h) -> p t h", h=H)
            link(nc.vector.tensor_tensor(a3, rest[:, :, A0:A0 + H], rep1(dtb[:, :], [P, NT, H]), ALU.add))
            link(nc.vector.tensor_scalar(gw[:, 1, :], gw[:, 0, :], -1.0, None, ALU.mult))
            nc.vector.tensor_tensor(gw[:, 1, :], gw[:, 1, :], gw[:, 0, :], ALU.min).then_inc(g1["neg_abs"], 1)
            dve.wait_ge(g1["exp"], 1)
            nc.vector.tensor_scalar(gw[:, 2, :], gw[:, 2, :], 1.0, None, ALU.add).then_inc(g1["plus1"], 1)
            link(nc.vector.tensor_scalar(gw[:, 4, :], gw[:, 4, :], 1.0, None, ALU.add))
            link(nc.vector.reciprocal(gw[:, 7, :], gw[:, 4, :]))
            dve.wait_ge(g1["ln"], 1)
            link(nc.vector.scalar_tensor_tensor(gw[:, 5, :], gw[:, 0, :], 0.0, gw[:, 3, :], ALU.max, ALU.add))
            nc.vector.scalar_tensor_tensor(g, gw[:, 5, :].rearrange("p (t h) -> p t h", h=H), -1.0,
                                           rep1(alog[:, :], [P, NT, H]), ALU.mult, ALU.mult).then_inc(g1["gates"], 1)
            dve.wait_ge(g1["rows_made"], 1)
            nc.vector.tensor_tensor(qkv[:, 0:2 * H, :], qkv[:, 0:2 * H, :], ps[:, :, 0:TOK], ALU.mult).then_inc(g1["normed"], 1)
            dve.wait_ge(g1["sums"], 1)
            link(nc.vector.tensor_copy(gsb[:, 0:96], ps[:, 0, 0:96]))
            link(nc.vector.tensor_tensor(gsb[:, G_LEFT:G_LEFT + 8], gsb[:, G_TOT:G_TOT + 8], gsb[:, 0:8], ALU.subtract))
            nc.vector.tensor_copy(small[:, 62:63], gsb[:, 0:1]).then_inc(g1["sums_read"], 1)
            dve.wait_ge(g1["rows_exp"], 2)
            for t in range(2):
                link(nc.vector.tensor_tensor(decT[:, t], ps[:, 1 + t, :].rearrange("p (h n) -> p h n", h=H),
                                             rep(gsb[:, 4 * t:4 * t + 4], [P, H, P]), ALU.subtract))
            nc.vector.tensor_scalar(decT[:, :, :, :], decT[:, :, :, :], 0.0, None, ALU.min).then_inc(g1["row_min"], 1)
            dve.wait_ge(g1["normed"], 1)
            for t in range(2):
                nc.vector.tensor_tensor(qTe[:, t], qTe[:, t], qkv[:, 0:H, cols(t)], ALU.mult)
            dve.wait_ge(g1["exp_sums"], 1)
            link(nc.vector.tensor_tensor(gw[:, 0, 0:8], gw[:, 7, 0:8], eg[:, 0:8], ALU.mult))
            dve.wait_ge(g1["dec_exp"], 1)
            link(nc.vector.tensor_tensor(decT[:, :, :, :].rearrange("p t h n -> p (t h) n"), decT[:, :, :, :].rearrange("p t h n -> p (t h) n"),
                                         rep1(c_(C_TRI), [P, 2 * H, P]), ALU.mult))
            for t in range(2):
                link(nc.vector.tensor_tensor(LT[:, t], decT[:, t], ps[:, 3 + t, :].rearrange("p (h n) -> p h n", h=H), ALU.mult))
            nc.vector.tensor_copy(small[:, 62:63], gsb[:, 0:1]).then_inc(g1["rows_read"], 1)
            dve.wait_ge(g1["turned"], 1)
            for t in range(2):
                kt = ps[:, 5 + t, :].rearrange("p (h n) -> p h n", h=H)
                vt = ps[:, (7 + t) % 8, :].rearrange("p (h n) -> p h n", h=H)
                nc.vector.tensor_tensor(kbe[:, t], kt, rep(gw[:, 0, 4 * t:4 * t + 4], [P, H, P]), ALU.mult)
                nc.vector.tensor_tensor(kd[:, t], kt, rep(eg[:, G_LEFT + 4 * t:G_LEFT + 4 * t + 4], [P, H, P]), ALU.mult)
                nc.vector.tensor_tensor(vb[:, t], vt, rep(gw[:, 7, 4 * t:4 * t + 4], [P, H, P]), ALU.mult)
            dve.wait_ge(g1["products"], 1)
            for t in range(2):
                nc.vector.tensor_tensor(LT[:, t], LT[:, t], ps[:, 1 + t, :].rearrange("p (h n) -> p h n", h=H), ALU.mult)
                nc.vector.tensor_tensor(iT[:, t], decT[:, t], ps[:, 3 + t, :].rearrange("p (h n) -> p h n", h=H), ALU.mult)

        @block.tensor
        def _(pe):
            pe.wait_ge(g1["squared"], 1)
            for t in range(NT):
                for c in range(2 * H):
                    last = pe.matmul(ps[0:ROWS[t], 0, 8 * t + c:8 * t + c + 1], sq[:, c, cols(t)], c_(C_ONE, 1), start=True, stop=True)
            last.then_inc(g1["summed"], 1)
            pe.wait_ge(g1["inverted"], 1)
            for t in range(NT):
                for c in range(2 * H):
                    r = ROWS[t]
                    last = pe.matmul(ps[:, c, cols(t)], rk[0:r, 8 * t + c:8 * t + c + 1].broadcast_to([r, P]), c_(C_ID, r, r), start=True, stop=True)
            last.then_inc(g1["rows_made"], 1)
            pe.wait_ge(g1["normed"], 1)
            pe.wait_ge(g1["gates"], 1)
            for t in range(2):
                pe.matmul(ps[:, 0, 4 * t:4 * t + 4], c_(C_TRI), g[:, t, :], start=True, stop=True)
                pe.matmul(ps[:, 0, 8 + 4 * t:12 + 4 * t], c_(C_BLK), g[:, t, :], start=True, stop=True)
                for h in range(H):
                    gcol = g[:, t, h:h + 1].broadcast_to([P, P])
                    a = G_CH + 2 * (4 * t + h)
                    pe.matmul(ps[:, 0, a:a + 2], gcol, c_(C_CH2, 2), start=True, stop=True)
                    pe.matmul(ps[:, 1 + t, h * P:(h + 1) * P], gcol, c_(C_TRI), start=True, stop=True)
                    pe.matmul(ps[:, 3 + t, h * P:(h + 1) * P], beta[:, t, h:h + 1].broadcast_to([P, P]), ident, start=True, stop=True)
            for h in range(H):
                i8 = c_(C_ID, DEC, DEC)
                pe.matmul(ps[:, 0, G_SMP + 8 * h:G_SMP + 8 * h + 8], g[0:DEC, 2, h:h + 1].broadcast_to([DEC, P]), i8, start=True, stop=True)
                last = pe.matmul(ps[:, 0, G_BSMP + 8 * h:G_BSMP + 8 * h + 8], beta[0:DEC, 2, h:h + 1].broadcast_to([DEC, P]), i8, start=True, stop=True)
            last.then_inc(g1["sums"], 1)
            pe.wait_ge(g1["sums_read"], 1)
            for t in range(2):
                for h in range(H):
                    pe.transpose(ps[:, 5 + t, h * P:(h + 1) * P], qkv[:, H + h, cols(t)], ident)
                    last = pe.transpose(ps[:, (7 + t) % 8, h * P:(h + 1) * P], qkv[:, 2 * H + h, cols(t)], ident)
            last.then_inc(g1["turned"], 1)
            pe.wait_ge(g1["rows_exp"], 2)
            pe.wait_ge(g1["rows_read"], 1)
            for t in range(2):
                for h in range(H):
                    pe.matmul(ps[:, 1 + t, h * P:(h + 1) * P], qkv[:, H + h, cols(t)], qkv[:, H + h, cols(t)], start=True, stop=True)
                    last = pe.matmul(ps[:, 3 + t, h * P:(h + 1) * P], qkv[:, H + h, cols(t)], qkv[:, h, cols(t)], start=True, stop=True)
            last.then_inc(g1["products"], 1)

    STEPS = 4 * DEC + 4
    sa = {n: sem("smla_" + n, True) for n in ("even_turned", "odd_turned", "even_moved", "odd_moved", "scored", "max", "exp",
                                              "p_turned", "pt_moved", "pv_done", "acc_moved")}

    def sampled_pe(pe, k):
        b, m = k // 4, k % 4
        if b < DEC:
            if m == 0:
                pe.wait_ge(seq_loaded[b % NSLOT], 32 * (b // NSLOT + 1))
            for p in range(2):
                n, tile = 2 * k + p, 4 * m + 2 * p
                lat, krc = lat_slots[b % NSLOT], kr_slots[b % NSLOT]
                if n > 0:
                    pe.wait_ge(sa["even_moved"], n)
                for j in range(2):
                    pe.transpose(ps[:, 5, j * P:(j + 1) * P], lat[:, tile, j * P:(j + 1) * P], ident)
                pe.transpose(ps[:, 5, 2 * P:3 * P], krc[:, tile:tile + 2, :].rearrange("p i n -> p (i n)"), ident).then_inc(sa["even_turned"], 1)
                if n > 0:
                    pe.wait_ge(sa["odd_moved"], n)
                for j in range(2):
                    last = pe.transpose(ps[:, 6, j * P:(j + 1) * P], lat[:, tile + 1, j * P:(j + 1) * P], ident)
                last.then_inc(sa["odd_turned"], 1)
        if b > 0 and m == 1:
            pe.wait_ge(sa["exp"], b)
            if b > 1:
                pe.wait_ge(sa["acc_moved"], b - 1)
            for j in range(4):
                last = pe.transpose(ps[:, 4, j * P:(j + 1) * P], Pb[:, j * P:(j + 1) * P], ident)
            last.then_inc(sa["p_turned"], 1)
        if b > 0 and m == 2:
            pe.wait_ge(sa["pt_moved"], b)
            for j in range(4):
                for i in range(4):
                    last = pe.matmul(ps[32 * i:32 * i + 32, 4, 0:KVR], PT[:, j, 32 * i:32 * i + 32], lat_slots[(b - 1) % NSLOT][:, 4 * j + i, :],
                                     start=(j == 0), stop=(j == 3), tile_position=(0, 32 * i))
            last.then_inc(sa["pv_done"], 1)
        if 0 < k <= 4 * DEC:
            sb, sm_ = (k - 1) // 4, (k - 1) % 4
            pe.wait_ge(sa["even_moved"], 2 * k)
            pe.wait_ge(sa["odd_moved"], 2 * k)
            if sm_ == 0 and sb > 0:
                pe.wait_ge(sa["exp"], sb)
            for j in range(3):
                for i in range(4):
                    keys = KT[:, (k - 1) % 2, i // 2, :]
                    a = (0, P, 2 * P)[j] if i % 2 == 0 else (3 * P, 4 * P, 2 * P)[j]
                    lhs = qlp[:, j, sb, :] if j < 2 else qrp[:, i % 2, sb, :]
                    last = pe.matmul(ps[32 * i:32 * i + 32, 7, sm_ * P:(sm_ + 1) * P], lhs, keys[:, a:a + P],
                                     start=(j == 0), stop=(j == 2), tile_position=(0, 32 * i))
            last.then_inc(sa["scored"], 1)

    def sampled_dve(dve, k):
        b, m = k // 4, k % 4
        if b > 0 and m == 1:
            dve.wait_ge(sa["scored"], 4 * b)
            dve_chain.link(dve, nc.vector.tensor_reduce(lmax[:, b - 1:b], ps[:, 7, :], AX, ALU.max))
            nc.vector.tensor_scalar(nmax[:, b - 1:b], lmax[:, b - 1:b], -MLA_SCALE, None, ALU.mult).then_inc(sa["max"], 1)
        for p in range(2 if b < DEC else 0):
            dve.wait_ge(sa["odd_turned"], 2 * k + p + 1)
            if k >= 2:
                dve.wait_ge(sa["scored"], k - 1)
            nc.vector.tensor_copy(KT[:, k % 2, p, 3 * P:5 * P], ps[:, 6, 0:2 * P]).then_inc(sa["odd_moved"], 1)
        if b > 0 and m == 1:
            dve.wait_ge(sa["p_turned"], b)
            nc.vector.tensor_copy(PT[:, :, :], ps[:, 4, :].rearrange("p (m n) -> p m n", m=4)).then_inc(sa["pt_moved"], 1)

    def sampled_act(act, k):
        b, m = k // 4, k % 4

        def even(p):
            act.wait_ge(sa["even_turned"], 2 * k + p + 1)
            if k >= 2:
                act.wait_ge(sa["scored"], k - 1)
            nc.scalar.copy(KT[:, k % 2, p, 0:3 * P], ps[:, 5, 0:3 * P]).then_inc(sa["even_moved"], 1)

        if b < DEC:
            even(0)
        if b > 0 and m == 1:
            act.wait_ge(sa["max"], b)
            if b > 1:
                act.wait_ge(sa["p_turned"], b - 1)
            nc.scalar.activation(Pb[:, :], ps[:, 7, :], ACT.Exp, bias=nmax[:, b - 1:b], scale=MLA_SCALE,
                                 accum_out=lsum[:, b - 1:b]).then_inc(sa["exp"], 1)
        if b < DEC:
            even(1)
        if b > 0 and m == 3:
            act.wait_ge(sa["pv_done"], b)
            nc.scalar.copy(acc[:, b - 1, :], ps[:, 4, 0:KVR]).then_inc(sa["acc_moved"], 1)

    def sampled_pool(pool, k):
        b, m = k // 4, k % 4
        if 0 < b <= DEC - NSLOT and m == 2:
            pool.wait_ge(sa["pv_done"], b)
            load_sequence(pool, b - 1 + NSLOT)

    AFTER_Y, AFTER_Z = 1, 2
    STEP_SCAN = (AFTER_Y + AFTER_Z) * (LEVELS - 1)
    PER_CHUNK = 2
    STEP_HEAD = STEP_SCAN + 2 * PER_CHUNK * (SEQ // CHUNK)
    STEP_REST = STEP_HEAD + H

    def level_steps(m, after_z):
        k = (AFTER_Y + AFTER_Z) * (m - 1)
        return range(k + AFTER_Y, k + AFTER_Y + AFTER_Z) if after_z else range(k, k + AFTER_Y)

    def chunk_steps(i, second):
        k = STEP_SCAN + PER_CHUNK * (2 * i + second)
        return range(k, k + PER_CHUNK)

    x0, x_turned, x_ready = sem("inv_first"), sem("inv_turned"), sem("inv_x_ready")
    c_ready, y_made, y_moved, z_made = sem("inv_c_ready"), sem("inv_y_made"), sem("inv_y_moved"), sem("inv_z_made")
    uw_made = sem("uw_made")
    with nc.Block() as block:
        def level(m):
            return rep1(c_(C_LVL + m * P), [P, H, P])

        @block.vector
        def _(dve):
            link = lambda ins: dve_chain.link(dve, ins)
            for t in range(2):
                link(nc.vector.tensor_tensor(CT[:, t], LT[:, t], level(0), ALU.mult))
                nc.vector.tensor_tensor(XT[:, t], rep1(ident, [P, H, P]), CT[:, t], ALU.subtract).then_inc(x0, 1)
            for t in range(2):
                dve_chain.link(dve, nc.vector.tensor_tensor(CT[:, t], LT[:, t], level(1), ALU.mult))
                dve.wait_ge(x_turned, t + 1)
                nc.vector.tensor_copy(X[:, t], ps[:, 2 + t, :].rearrange("p (h n) -> p h n", h=H)).then_inc(x_ready, 1)
            for m in range(1, LEVELS):
                if m + 1 < LEVELS:
                    for t in range(2):
                        dve.wait_ge(y_made, 2 * (m - 1) + t + 1)
                        nc.vector.tensor_tensor(CT[:, t], LT[:, t], level(m + 1), ALU.mult).then_inc(c_ready, 1)
                for k in level_steps(m, False):
                    sampled_dve(dve, k)
                for t in range(2):
                    dve.wait_ge(z_made, 2 * (m - 1) + t + 1)
                    nc.vector.tensor_tensor(X[:, t], X[:, t], ps[:, t, :].rearrange("p (h n) -> p h n", h=H), ALU.subtract)
                    nc.vector.tensor_tensor(XT[:, t], XT[:, t], ps[:, 2 + t, :].rearrange("p (h n) -> p h n", h=H), ALU.subtract).then_inc(x_ready, 1)
                for k in level_steps(m, True):
                    sampled_dve(dve, k)
            for t in range(2):
                dve.wait_ge(uw_made, t + 1)
                nc.vector.tensor_copy(u[:, t], ps[:, t, :].rearrange("p (h n) -> p h n", h=H))
                nc.vector.tensor_copy(wT[:, t], ps[:, 2 + t, :].rearrange("p (h n) -> p h n", h=H))

        @block.scalar
        def _(act):
            for m in range(1, LEVELS):
                for t in range(2):
                    act.wait_ge(y_made, 2 * (m - 1) + t + 1)
                    if m > 1:
                        act.wait_ge(z_made, 2 * (m - 2) + t + 1)
                    nc.scalar.copy(Y[:, t], ps[:, t, :].rearrange("p (h n) -> p h n", h=H)).then_inc(y_moved, 1)
                for after_z in (False, True):
                    for k in level_steps(m, after_z):
                        sampled_act(act, k)

        @block.gpsimd
        def _(pool):
            for k in range(STEP_SCAN):
                sampled_pool(pool, k)

        @block.tensor
        def _(pe):
            for t in range(2):
                pe.wait_ge(x0, t + 1)
                for h in range(H):
                    last = pe.transpose(ps[:, 2 + t, h * P:(h + 1) * P], XT[:, t, h, :], ident)
                last.then_inc(x_turned, 1)
            for m in range(1, LEVELS):
                for t in range(2):
                    if m > 1:
                        pe.wait_ge(c_ready, 2 * (m - 2) + t + 1)
                    pe.wait_ge(x_ready, 2 * (m - 1) + t + 1)
                    for h in range(H):
                        last = pe.matmul(ps[:, t, h * P:(h + 1) * P], CT[:, t, h, :], X[:, t, h, :], start=True, stop=True)
                    last.then_inc(y_made, 1)
                for k in level_steps(m, False):
                    sampled_pe(pe, k)
                for t in range(2):
                    pe.wait_ge(y_moved, 2 * (m - 1) + t + 1)
                    for h in range(H):
                        pe.matmul(ps[:, t, h * P:(h + 1) * P], XT[:, t, h, :], Y[:, t, h, :], start=True, stop=True)
                        last = pe.matmul(ps[:, 2 + t, h * P:(h + 1) * P], Y[:, t, h, :], XT[:, t, h, :], start=True, stop=True)
                    last.then_inc(z_made, 1)
                for k in level_steps(m, True):
                    sampled_pe(pe, k)
            for t in range(2):
                pe.wait_ge(x_ready, 2 * (LEVELS - 1) + t + 1)
                for h in range(H):
                    pe.matmul(ps[:, t, h * P:(h + 1) * P], XT[:, t, h, :], vb[:, t, h, :], start=True, stop=True)
                    last = pe.matmul(ps[:, 2 + t, h * P:(h + 1) * P], kbe[:, t, h, :], XT[:, t, h, :], start=True, stop=True)
                last.then_inc(uw_made, 1)

    NC = SEQ // CHUNK
    seen, v_ready, add_made, s_ready, o_made = (sem(n) for n in ("scan_seen", "scan_v_ready", "scan_add_made", "scan_s_ready", "scan_o_made"))
    with nc.Block() as block:
        @block.scalar
        def _(act):
            for k in range(STEP_SCAN, STEP_HEAD):
                sampled_act(act, k)

        @block.gpsimd
        def _(pool):
            for k in range(STEP_SCAN, STEP_HEAD):
                sampled_pool(pool, k)

        @block.vector
        def _(dve):
            for i in range(NC):
                t, r = i // 2, CHUNK * (i % 2)
                rows = slice(r, r + CHUNK)
                if i == 0:
                    nc.vector.tensor_copy(vnew[rows, t], u[rows, t]).then_inc(v_ready, 1)
                else:
                    dve.wait_ge(seen, i)
                    nc.vector.tensor_tensor(vnew[rows, t], u[rows, t], ps[rows, 0, :].rearrange("p (h n) -> p h n", h=H), ALU.subtract).then_inc(v_ready, 1)
                for k in chunk_steps(i, 0):
                    sampled_dve(dve, k)
                dve.wait_ge(add_made, i + 1)
                for h in range(H):
                    made = ps[:, 1, h * P:(h + 1) * P]
                    a = G_CH + 2 * (4 * t + h) + i % 2
                    if i == 0:
                        last = nc.vector.tensor_copy(S[:, h, :], made)
                    else:
                        last = nc.vector.scalar_tensor_tensor(S[:, h, :], S[:, h, :], eg[:, a:a + 1], made, ALU.mult, ALU.add)
                last.then_inc(s_ready, 1)
                for k in chunk_steps(i, 1):
                    sampled_dve(dve, k)
            for t in range(2):
                dve.wait_ge(o_made, t + 1)
                dve_chain.link(dve, nc.vector.tensor_copy(otok[:, t], ps[:, t, :].rearrange("p (h n) -> p h n", h=H)))
                rows = slice(CHUNK if t == 0 else 0, P)
                nc.vector.tensor_tensor(otok[rows, t], otok[rows, t], ps[rows, 2 + t, :].rearrange("p (h n) -> p h n", h=H), ALU.add)

        @block.tensor
        def _(pe):
            for i in range(NC):
                t, r = i // 2, CHUNK * (i % 2)
                rows = slice(r, r + CHUNK)
                if i > 0:
                    pe.wait_ge(s_ready, i)
                    for h in range(H):
                        last = pe.matmul(ps[rows, 0, h * P:(h + 1) * P], wT[:, t, h, rows], S[:, h, :], start=True, stop=True)
                    last.then_inc(seen, 1)
                    for h in range(H):
                        pe.matmul(ps[rows, 2 + t, h * P:(h + 1) * P], qTe[:, t, h, rows], S[:, h, :], start=True, stop=True)
                for k in chunk_steps(i, 0):
                    sampled_pe(pe, k)
                pe.wait_ge(v_ready, i + 1)
                for h in range(H):
                    last = pe.matmul(ps[:, 1, h * P:(h + 1) * P], kd[rows, t, h, :], vnew[rows, t, h, :], start=True, stop=True)
                last.then_inc(add_made, 1)
                for k in chunk_steps(i, 1):
                    sampled_pe(pe, k)
            pe.wait_ge(s_ready, NC)
            for t in range(2):
                for h in range(H):
                    last = pe.matmul(ps[:, t, h * P:(h + 1) * P], iT[:, t, h, :], vnew[:, t, h, :], start=True, stop=True)
                last.then_inc(o_made, 1)

    sm = {n: sem("smp_" + n) for n in ("prod", "seen", "delta", "turned", "blocks", "outer", "updated", "o_ready", "moved")}
    with nc.Block() as block:
        @block.sync
        def _(sp):
            store(sp, gdn_prompt[0, 0].rearrange("h k v -> k h v"), S[:, :, :])
            sp.wait_ge(sm["updated"], H)
            store(sp, gdn_sample[0].rearrange("b h k v -> k (b h) v"), st[:, :, :])

        @block.scalar
        def _(act):
            for k in range(STEP_HEAD, STEP_REST):
                sampled_act(act, k)

        @block.gpsimd
        def _(pool):
            for k in range(STEP_HEAD, STEP_REST):
                sampled_pool(pool, k)

        @block.vector
        def _(dve):
            link = lambda ins: dve_chain.link(dve, ins)
            q_s, k_s, v_s = (qkv[:, i * H:(i + 1) * H, SEQ:TOK] for i in range(3))
            egs = eg[:, G_SMP:G_SMP + 32].rearrange("p (h b) -> p h b", h=H)
            bs = gsb[:, G_BSMP:G_BSMP + 32].rearrange("p (h b) -> p h b", h=H)
            nc.vector.memset(otok[:, 2], 0.0)
            nc.vector.tensor_tensor(pr[:, :, :], q_s, k_s, ALU.mult).then_inc(sm["prod"], 1)
            dve.wait_ge(sm["seen"], 1)
            sqk = ps[:, 0, 0:64].rearrange("p (h b j) -> p h b j", h=H, j=2)
            link(nc.vector.tensor_tensor(dT[:, :, :], sqk[:, :, :, 1], egs, ALU.mult))
            link(nc.vector.tensor_tensor(dT[:, :, :], v_s, dT[:, :, :], ALU.subtract))
            link(nc.vector.tensor_tensor(dT[:, :, :], dT[:, :, :], bs, ALU.mult))
            link(nc.vector.tensor_tensor(pr[:, :, :], dT[:, :, :], ps[:, 0, 64:96].rearrange("p (h b) -> p h b", h=H), ALU.mult))
            link(nc.vector.tensor_tensor(oT[:, :, :], sqk[:, :, :, 0], egs, ALU.mult))
            nc.vector.tensor_tensor(oT[:, :, :], oT[:, :, :], pr[:, :, :], ALU.add).then_inc(sm["delta"], 1)
            dve.wait_ge(sm["turned"], 1)
            nc.vector.tensor_copy(kts[:, :, :], ps[0:DEC, 1, :].rearrange("p (h n) -> p h n", h=H))
            link(nc.vector.tensor_copy(dts[:, :, :], ps[0:DEC, 2, :].rearrange("p (h n) -> p h n", h=H)))
            nc.vector.tensor_copy(otok[0:DEC, 2], ps[0:DEC, 3, :].rearrange("p (h n) -> p h n", h=H))
            for h in range(H):
                nc.vector.tensor_tensor(delta[:, h], rep1(dts[:, h, :], [DEC, DEC, P]), rep(c_(C_ID, DEC, DEC), [DEC, DEC, P]), ALU.mult).then_inc(sm["blocks"], 1)
            for h in range(H):
                dve.wait_ge(sm["outer"], h + 1)
                for b in range(DEC):
                    s = st[:, b * H + h, :]
                    last = nc.vector.scalar_tensor_tensor(s, s, eg[:, G_SMP + 8 * h + b:G_SMP + 8 * h + b + 1],
                                                          ps[:, 2 * (h % 2) + b // 4, (b % 4) * P:(b % 4 + 1) * P], ALU.mult, ALU.add)
                last.then_inc(sm["updated"], 1)
                sampled_dve(dve, STEP_HEAD + h)

        @block.tensor
        def _(pe):
            pe.wait_ge(state_loaded, 16)
            for h in range(H):
                for b in range(DEC):
                    a = 2 * (h * DEC + b)
                    pe.matmul(ps[:, 0, a:a + 2], st[:, b * H + h, :], qkv[:, h:h + 5:4, SEQ + b], start=True, stop=True)
            pe.wait_ge(sm["prod"], 1)
            pe.matmul(ps[:, 0, 64:96], c_(C_ONE), pr[:, :, :], start=True, stop=True).then_inc(sm["seen"], 1)
            pe.wait_ge(sm["delta"], 1)
            for h in range(H):
                pe.transpose(ps[0:DEC, 1, h * P:(h + 1) * P], qkv[:, H + h, SEQ:TOK], ident)
                pe.transpose(ps[0:DEC, 2, h * P:(h + 1) * P], dT[:, h, :], ident)
                last = pe.transpose(ps[0:DEC, 3, h * P:(h + 1) * P], oT[:, h, :], ident)
            last.then_inc(sm["turned"], 1)
            for h in range(H):
                pe.wait_ge(sm["blocks"], h + 1)
                if h >= 2:
                    pe.wait_ge(sm["updated"], h - 1)
                for j in range(2):
                    last = pe.matmul(ps[:, 2 * (h % 2) + j, :], kts[:, h, :], delta[:, h, 4 * j:4 * j + 4, :], start=True, stop=True)
                last.then_inc(sm["outer"], 1)
                sampled_pe(pe, STEP_HEAD + h)

    gn = {n: sem("gnorm_" + n) for n in ("sig", "sq", "var", "root", "ready", "turned")}
    AT_WK, AT_MEMT, AT_MV, AT_WOUT, AT_WV, AT_WXQ, AT_WXO = 0, 8192, 10240, 12288, 20480, 28672, 36864
    AT_QX, AT_MKT = AT_WOUT + 3 * D, AT_WOUT + 3 * D + KD * TOK
    weight = lambda at: Arena(arena, at).take([P, KD, D])
    wk, wv, wout, wxq, wxo = (weight(at) for at in (AT_WK, AT_WV, AT_WOUT, AT_WXQ, AT_WXO))
    memt = Arena(arena, AT_MEMT).take([P, 2, D])
    mem_loaded, wkv_loaded, wout_loaded, wx_loaded = (sem(n, True) for n in ("mem_loaded", "wkv_loaded", "wout_loaded", "wx_loaded"))
    with nc.Block() as block:
        place = Arena(arena, AT_HEADS)
        osq = place.take([P, NT * H, P])
        sig = place.take([P, NT, H * P])
        o3 = otok[:, :, :, :].rearrange("p t h n -> p (t h) n")

        @block.sync
        def _(sp):
            sp.dma_start(wout, w_out[0].rearrange("(k p) n -> p k n", p=P)).then_inc(wout_loaded, 16)
            sp.wait_ge(sa["pv_done"], DEC)
            sp.dma_start(memt, mem_prompt[0].rearrange("(t p) d -> p t d", p=P)).then_inc(mem_loaded, 16)
            sp.dma_start(wk, w_xk[0].rearrange("(k p) n -> p k n", p=P)).then_inc(wkv_loaded, 16)

        @block.gpsimd
        def _(pool):
            for k in range(STEP_REST, STEPS):
                sampled_pool(pool, k)

        @block.scalar
        def _(act):
            nc.scalar.activation(sig[:, :, :], rest[:, :, Z0:Z0 + H * P], ACT.Sigmoid).then_inc(gn["sig"], 1)
            act.wait_ge(gn["var"], 1)
            nc.scalar.activation(gw[:, 1, :], gw[:, 1, :], ACT.Sqrt).then_inc(gn["root"], 1)
            for k in range(STEP_REST, STEPS):
                sampled_act(act, k)

        @block.vector
        def _(dve):
            link = lambda ins: dve_chain.link(dve, ins)
            link(nc.vector.tensor_tensor(osq, o3, o3, ALU.mult))
            link(nc.vector.tensor_reduce(gw[:, 0, :], osq, AX, ALU.add))
            nc.vector.tensor_scalar(gw[:, 1, :], gw[:, 0, :], 1.0 / P, EPS, ALU.mult, ALU.add).then_inc(gn["var"], 1)
            dve.wait_ge(gn["sig"], 1)
            link(nc.vector.tensor_tensor(sig[:, :, :], sig[:, :, :], rest[:, :, Z0:Z0 + H * P], ALU.mult))
            link(nc.vector.tensor_tensor(o3, o3, sig[:, :, :].rearrange("p t (h n) -> p (t h) n", n=P), ALU.mult))
            dve.wait_ge(gn["root"], 1)
            link(nc.vector.reciprocal(gw[:, 1, :], gw[:, 1, :]))
            nc.vector.tensor_tensor(o3, o3, rep(gw[:, 1, :], [P, NT * H, P]), ALU.mult).then_inc(gn["ready"], 1)
            for t in range(NT):
                dve.wait_ge(gn["turned"], t + 1)
                nc.vector.tensor_scalar(yT[:, 0:H, cols(t)], ps[:, t, :].rearrange("p (h n) -> p h n", h=H)[:, :, 0:ROWS[t]],
                                        vec[:, V_GDN:V_GDN + 1], None, ALU.mult)
            for k in range(STEP_REST, STEPS):
                sampled_dve(dve, k)

        @block.tensor
        def _(pe):
            pe.wait_ge(gn["ready"], 1)
            for t in range(NT):
                for h in range(H):
                    r = ROWS[t]
                    last = pe.transpose(ps[:, t, h * P:h * P + r], otok[0:r, t, h, :], c_(C_ID, r, r))
                last.then_inc(gn["turned"], 1)
            for k in range(STEP_REST, STEPS):
                sampled_pe(pe, k)

    jn = {n: sem("join_" + n) for n in ("turned", "max", "exp", "coef", "coef_turned", "ready", "summed", "out_ready", "out")}
    with nc.Block() as block:
        place = Arena(arena, AT_HEADS)
        m8 = place.take([DEC, 4, 32])
        l8 = place.take([DEC, 4, 32])
        own, top, tot, tmp8 = (place.take([DEC, H]) for _ in range(4))
        coef8 = place.take([DEC, 4, 32])
        part = place.take([DEC, 4, H])
        ownm = place.take([DEC, DEC, H])
        csel = place.take([P, DEC, H])
        oLT = place.take([P, 2, DEC, H])

        @block.sync
        def _(sp):
            sp.wait_ge(jn["summed"], 1)
            sp.dma_start(res[:, 0:2, :], x_prompt[0].rearrange("(t p) d -> p t d", p=P)).then_inc(x_loaded, 16)
            sp.dma_start(res[0:DEC, 2, :], x_sample[:, 0, :]).then_inc(x_loaded, 16)
            sp.wait_ge(stored, n_stored[0])

        @block.tensor
        def _(pe):
            pe.transpose(ps[0:DEC, 0, 0:P], lmax, ident)
            pe.transpose(ps[0:DEC, 0, P:2 * P], lsum, ident).then_inc(jn["turned"], 1)
            pe.wait_ge(jn["coef"], 1)
            pe.transpose(ps[:, 1, 0:DEC], coef8.rearrange("p i n -> p (i n)"), c_(C_ID, DEC, DEC))
            for k in range(2):
                last = pe.matmul(ps[:, 2, 32 * k:32 * k + 32], rest[0:DEC, 2, CKV0 + k * P:CKV0 + (k + 1) * P],
                                 ownm.rearrange("p b h -> p (b h)"), start=True, stop=True)
            last.then_inc(jn["coef_turned"], 1)
            pe.wait_ge(jn["ready"], 1)
            for k in range(2):
                for b in range(DEC):
                    a = 32 * k + H * b
                    last = pe.matmul(ps[:, 3, a:a + H], acc[:, b, k * P:(k + 1) * P], csel[:, b, :], start=True, stop=True)
            last.then_inc(jn["summed"], 1)
            pe.wait_ge(jn["out_ready"], 1)
            for h in range(H):
                for k in range(2):
                    last = pe.matmul(ps[:, 0, h * DEC:(h + 1) * DEC], uv[:, k, h, :], oLT[:, k, :, h], start=(k == 0), stop=(k == 1))
            last.then_inc(jn["out"], 1)

        @block.scalar
        def _(act):
            act.wait_ge(jn["max"], 1)
            nc.scalar.activation(part, part, ACT.Exp, scale=MLA_SCALE)
            nc.scalar.activation(own, own, ACT.Exp, scale=MLA_SCALE).then_inc(jn["exp"], 1)

        @block.vector
        def _(dve):
            link = lambda ins: dve_chain.link(dve, ins)
            link(nc.vector.tensor_reduce(own, snew.rearrange("p b h -> p h b"), AX, ALU.add))
            nc.vector.memset(coef8, 0.0)
            dve.wait_ge(jn["turned"], 1)
            nc.vector.tensor_copy(m8.rearrange("p i n -> p (i n)"), ps[0:DEC, 0, 0:P])
            link(nc.vector.tensor_copy(l8.rearrange("p i n -> p (i n)"), ps[0:DEC, 0, P:2 * P]))
            link(nc.vector.tensor_reduce(top, m8[:, :, 0:H].rearrange("p i h -> p h i"), AX, ALU.max))
            link(nc.vector.tensor_tensor(top, top, own, ALU.max))
            nc.vector.tensor_tensor(part, m8[:, :, 0:H], rep1(top, [DEC, 4, H]), ALU.subtract)
            nc.vector.tensor_tensor(own, own, top, ALU.subtract).then_inc(jn["max"], 1)
            dve.wait_ge(jn["exp"], 1)
            link(nc.vector.tensor_tensor(l8[:, :, 0:H], l8[:, :, 0:H], part, ALU.mult))
            link(nc.vector.tensor_reduce(tot, l8[:, :, 0:H].rearrange("p i h -> p h i"), AX, ALU.add))
            link(nc.vector.tensor_tensor(tot, tot, own, ALU.add))
            link(nc.vector.reciprocal(tot, tot))
            link(nc.vector.tensor_tensor(own, own, tot, ALU.mult))
            nc.vector.tensor_tensor(coef8[:, :, 0:H], part, rep1(tot, [DEC, 4, H]), ALU.mult)
            nc.vector.tensor_tensor(ownm, rep1(own, [DEC, DEC, H]), rep(c_(C_ID, DEC, DEC), [DEC, DEC, H]), ALU.mult).then_inc(jn["coef"], 1)
            dve.wait_ge(jn["coef_turned"], 1)
            link(nc.vector.tensor_copy(csel, rep(ps[:, 1, 0:DEC], [P, DEC, H])))
            link(nc.vector.tensor_copy(oLT, ps[:, 2, 0:64].rearrange("p (k b h) -> p k b h", k=2, b=DEC)))
            nc.vector.tensor_tensor(csel, csel, rep1(c_(C_HEAD, H), [P, DEC, H]), ALU.mult).then_inc(jn["ready"], 1)
            dve.wait_ge(jn["summed"], 1)
            nc.vector.tensor_tensor(oLT, oLT, ps[:, 3, 0:64].rearrange("p (k b h) -> p k b h", k=2, b=DEC), ALU.add).then_inc(jn["out_ready"], 1)
            dve.wait_ge(jn["out"], 1)
            nc.vector.tensor_copy(yT[:, H:2 * H, SEQ:TOK], ps[:, 0, 0:H * DEC].rearrange("p (h b) -> p h b", h=H))
    clear_semaphores()
    def add_projection(tag, src, w, loaded, at, beside_sync, beside_vector=None):
        made = sem(f"{tag}_made")
        with nc.Block() as block:
            @block.sync
            def _(sp):
                beside_sync(sp)

            @block.tensor
            def _(pe):
                pe.wait_ge(loaded, at)
                pe.wait_ge(x_loaded, 64)
                for t in range(2):
                    for n in range(2):
                        for k in range(KD):
                            last = pe.matmul(ps[0:ROWS[t], 2 * t + n, :], src[:, k, cols(t)], w[:, k, n * 512:(n + 1) * 512],
                                             start=(k == 0), stop=(k == KD - 1))
                        last.then_inc(made, 1)
                for k in range(KD):
                    for j in range(4):
                        last = pe.matmul(ps[32 * j:32 * j + DEC, 4, 0:D // 4], src[:, k, cols(2)], w[:, k, j * D // 4:(j + 1) * D // 4],
                                         start=(k == 0), stop=(k == KD - 1), tile_position=(0, 32 * j))
                last.then_inc(made, 1)

            @block.vector
            def _(dve):
                if beside_vector:
                    beside_vector(dve)
                for t in range(2):
                    for n in range(2):
                        dve.wait_ge(made, 2 * t + n + 1)
                        r = res[0:ROWS[t], t, n * 512:(n + 1) * 512]
                        nc.vector.tensor_tensor(r, r, ps[0:ROWS[t], 2 * t + n, :], ALU.add)
                dve.wait_ge(made, 5)
                for j in range(4):
                    r = res[0:DEC, 2, j * D // 4:(j + 1) * D // 4]
                    nc.vector.tensor_tensor(r, r, ps[32 * j:32 * j + DEC, 4, 0:D // 4], ALU.add)

    def load_cross_weights(sp):
        sp.dma_start(wv, w_xv[0].rearrange("(k p) n -> p k n", p=P)).then_inc(wkv_loaded, 16)
        sp.dma_start(wxq, w_xq[0].rearrange("(k p) n -> p k n", p=P)).then_inc(wx_loaded, 16)
        sp.dma_start(wxo, w_xo[0].rearrange("(k p) n -> p k n", p=P)).then_inc(wx_loaded, 16)

    add_projection("mix_out", yT, wout, wout_loaded, 16, load_cross_weights)

    mk = Arena(arena, AT_QX).take([P, 2, D])
    mkT = Arena(arena, AT_MKT).take([P, KD, MEM])
    mv = Arena(arena, AT_MV).take([P, 2, D])
    qxT = Arena(arena, AT_QX).take([P, KD, TOK])
    oxT = xnT
    normed_transposed("mem", memt, (0, 1), V_MEM, mem_loaded, 16, AT_WOUT)

    G = 4
    Kx = Arena(arena, AT_WK).take([P, G, 2, D])
    Vx = Arena(arena, AT_WV).take([P, G, 2, D])
    kx_loaded = [sem(f"xkey{b}_loaded") for b in range(G)]
    vx_loaded = sem("xvalue_loaded")
    kv_made, kv_moved, mk_turned = sem("kv_made"), sem("kv_moved"), sem("mk_turned")
    with nc.Block() as block:
        @block.sync
        def _(sp):
            sp.wait_ge(kv_moved, 8)
            store(sp, memk_prompt[0, 0].rearrange("(t p) h n -> p t (h n)", p=P), mk)
            store(sp, memv_prompt[0, 0].rearrange("(t p) h n -> p t (h n)", p=P), mv)
            for b in range(G):
                sp.dma_start(Kx[:, b], cache_mem_k[0, b].rearrange("(s p) h n -> p s (h n)", p=P)).then_inc(kx_loaded[b], 16)
            sp.dma_start(Vx, cache_mem_v[0, 0:G].rearrange("b (s p) h n -> p b s (h n)", p=P)).then_inc(vx_loaded, 16)
            sp.wait_ge(stored, n_stored[0])

        @block.tensor
        def _(pe):
            pe.wait_ge(wkv_loaded, 32)
            i = 0
            for w in range(2):
                for t in range(2):
                    for n in range(2):
                        for k in range(KD):
                            last = pe.matmul(ps[:, i, :], xnT[:, k, cols(t)], (wk, wv)[w][:, k, n * 512:(n + 1) * 512], start=(k == 0), stop=(k == KD - 1))
                        last.then_inc(kv_made, 1)
                        i += 1
            pe.wait_ge(kv_moved, 4)
            for j in range(4):
                for k in range(2):
                    for t in range(2):
                        b = 2 * j + k
                        last = pe.transpose(ps[:, j, (2 * k + t) * P:(2 * k + t + 1) * P], mk[:, t, b * P:(b + 1) * P], ident)
                last.then_inc(mk_turned, 1)

        @block.vector
        def _(dve):
            for i in range(8):
                dve.wait_ge(kv_made, i + 1)
                dst = (mk if i < 4 else mv)[:, (i // 2) % 2, (i % 2) * 512:(i % 2 + 1) * 512]
                nc.vector.tensor_copy(dst, ps[:, i, :]).then_inc(kv_moved, 1)
            for j in range(4):
                dve.wait_ge(mk_turned, j + 1)
                nc.vector.tensor_copy(mkT[:, 2 * j:2 * j + 2, :].rearrange("p k n -> p (k n)"), ps[:, j, :])

    normed_transposed("x", res, (0, 1, 2), V_X, x_loaded, 64, AT_WOUT)

    RING = 12
    AT_RING = (AT_MEMT, AT_WOUT, AT_MV, AT_MKT, *(AT_WK + 2048 * i for i in range(4)), *(AT_WV + 2048 * i for i in range(4)))
    ring = [arena[:, at:at + 2048] for at in AT_RING]
    full = [sem(f"ring{s}_full", True) for s in range(RING)]
    free = [sem(f"ring{s}_free", True) for s in range(RING)]
    FILLS = 24

    def fill(sp, n, e):
        s, x = n % RING, n % 2
        if n < 16:
            k = n // 2
            src = w_e1[0, bass.ds(e + x, 1), k * P:(k + 1) * P, :].rearrange("a p n -> (a p) n")
            sp.dma_start(ring[s], src).then_inc(full[s], 16)
        else:
            k = 2 * ((n - 16) // 2)
            src = w_e2[0, bass.ds(e + x, 1), k * P:(k + 2) * P, :].rearrange("a (k p) n -> p (a k) n", p=P)
            sp.dma_start(ring[s].rearrange("p (k n) -> p k n", k=2), src).then_inc(full[s], 16)


    after_wxq = Arena(arena, AT_WXQ)
    scx = after_wxq.take([P, 8, MEM])
    pTx = after_wxq.take([P, H, 2, SEQ])
    X_SCALE = XD ** -0.5
    cx = {n: sem("cross_" + n) for n in ("q_made", "q_moved", "scored", "max", "exp", "probs", "turned", "pt_ready", "out", "out_moved")}
    with nc.Block() as block:
        @block.sync
        def _(sp):
            for n in range(2):
                fill(sp, n, 0)

        @block.tensor
        def _(pe):
            pe.wait_ge(wx_loaded, 32)
            for c in range(KD):
                if c >= 4:
                    pe.wait_ge(cx["q_moved"], c - 3)
                for k in range(KD):
                    last = pe.matmul(ps[:, c % 4, 0:TOK], wxq[:, k, c * P:(c + 1) * P], xnT[:, k, :], start=(k == 0), stop=(k == KD - 1))
                last.then_inc(cx["q_made"], 1)
            pe.wait_ge(cx["q_moved"], KD)
            for h in range(H):
                for q in range(2):
                    for k in range(2):
                        last = pe.matmul(ps[:, 4 + h, q * MEM:(q + 1) * MEM], qxT[:, 2 * h + k, q * P:(q + 1) * P], mkT[:, 2 * h + k, :], start=(k == 0), stop=(k == 1))
            last.then_inc(cx["scored"], 1)
            pe.wait_ge(cx["probs"], 1)
            for h in range(H):
                for q in range(2):
                    for s in range(2):
                        last = pe.transpose(ps[:, h, s * SEQ + q * P:s * SEQ + (q + 1) * P], scx[:, 2 * h + q, s * P:(s + 1) * P], ident)
                last.then_inc(cx["turned"], 1)
            for k in range(KD):
                pe.wait_ge(cx["pt_ready"], k // 2 + 1)
                if k >= 4:
                    pe.wait_ge(cx["out_moved"], k - 3)
                for s in range(2):
                    last = pe.matmul(ps[:, 4 + k % 4, 0:SEQ], mv[:, s, k * P:(k + 1) * P], pTx[:, k // 2, s, :], start=(s == 0), stop=(s == 1))
                last.then_inc(cx["out"], 1)

        @block.scalar
        def _(act):
            for c in range(KD):
                act.wait_ge(cx["q_made"], c + 1)
                nc.scalar.copy(qxT[:, c, :], ps[:, c % 4, 0:TOK]).then_inc(cx["q_moved"], 1)
            act.wait_ge(cx["max"], 1)
            for i in range(8):
                act_chain.link(act, nc.scalar.activation(scx[:, i, :], ps[:, 4 + i // 2, (i % 2) * MEM:(i % 2 + 1) * MEM], ACT.Exp,
                                                         bias=small[:, 30 + i:31 + i], scale=X_SCALE, accum_out=small[:, 38 + i:39 + i]))
            nc.scalar.copy(small[:, 60:61], small[:, 38:39]).then_inc(cx["exp"], 1)

        @block.vector
        def _(dve):
            link = lambda ins: dve_chain.link(dve, ins)
            dve.wait_ge(cx["scored"], 1)
            link(nc.vector.tensor_reduce(small[:, 30:38], ps[:, 4:8, :].rearrange("p h (q n) -> p (h q) n", q=2), AX, ALU.max))
            nc.vector.tensor_scalar(small[:, 30:38], small[:, 30:38], -X_SCALE, None, ALU.mult).then_inc(cx["max"], 1)
            dve.wait_ge(cx["exp"], 1)
            link(nc.vector.reciprocal(small[:, 38:46], small[:, 38:46]))
            nc.vector.tensor_tensor(scx, scx, rep(small[:, 38:46], [P, 8, MEM]), ALU.mult).then_inc(cx["probs"], 1)
            for h in range(H):
                dve.wait_ge(cx["turned"], h + 1)
                nc.vector.tensor_copy(pTx[:, h, :, :].rearrange("p s n -> p (s n)"), ps[:, h, :]).then_inc(cx["pt_ready"], 1)
            for k in range(KD):
                dve.wait_ge(cx["out"], k + 1)
                nc.vector.tensor_copy(oxT[:, k, 0:SEQ], ps[:, 4 + k % 4, 0:SEQ]).then_inc(cx["out_moved"], 1)

    after_wxq = Arena(arena, AT_WXQ)
    KTx = after_wxq.take([P, 2, KD, MEM])
    qpad = after_wxq.take([P, KD, DEC, 32])
    pS = after_wxq.take([P, MEM])
    pST = after_wxq.take([P, 2, P])
    oS = after_wxq.take([P, D])
    sx = {n: sem("scross_" + n) for n in ("q_ready", "turned", "moved_act", "moved_dve", "scored", "max", "exp", "probs", "p_turned", "pt_ready",
                                          "out", "o_moved", "o_turned", "o_done")}
    with nc.Block() as block:
        @block.sync
        def _(sp):
            for n in (2, 3):
                fill(sp, n, 0)
            for b in range(G):
                sp.wait_ge(sx["scored"], b + 1)
                sp.dma_start(Kx[:, b], cache_mem_k[0, G + b].rearrange("(s p) h n -> p s (h n)", p=P)).then_inc(kx_loaded[b], 16)
            sp.wait_ge(sx["out"], 1)
            sp.dma_start(Vx, cache_mem_v[0, G:2 * G].rearrange("b (s p) h n -> p b s (h n)", p=P)).then_inc(vx_loaded, 16)
            for b in range(G):
                sp.wait_ge(sx["scored"], G + b + 1)
                fill(sp, 4 + b, 0)
            sp.wait_ge(sx["out"], 2)
            for n in range(8, RING):
                fill(sp, n, 0)

        @block.tensor
        def _(pe):
            pe.wait_ge(sx["q_ready"], 1)
            for g in range(2):
                for b in range(G):
                    n = g * G + b
                    pe.wait_ge(kx_loaded[b], 16 * (g + 1))
                    for s in range(2):
                        m = 2 * n + s
                        if m >= 2:
                            pe.wait_ge(sx["moved_act"], m - 1)
                            pe.wait_ge(sx["moved_dve"], m - 1)
                        if g and b == 0:
                            pe.wait_ge(sx["o_done"], g)
                        for k in range(KD):
                            last = pe.transpose(ps[:, 2 * (m % 2) + k // 4, (k % 4) * P:(k % 4 + 1) * P], Kx[:, b, s, k * P:(k + 1) * P], ident)
                        last.then_inc(sx["turned"], 1)
                    pe.wait_ge(sx["moved_act"], 2 * n + 2)
                    pe.wait_ge(sx["moved_dve"], 2 * n + 2)
                    for k in range(KD):
                        last = pe.matmul(ps[32 * b:32 * b + 32, 4, 0:MEM], qpad[:, k, n, :], KTx[:, n % 2, k, :],
                                         start=(k == 0), stop=(k == KD - 1), tile_position=(0, 32 * b))
                    last.then_inc(sx["scored"], 1)
                pe.wait_ge(sx["probs"], g + 1)
                for s in range(2):
                    last = pe.transpose(ps[:, 5, s * P:(s + 1) * P], pS[:, s * P:(s + 1) * P], ident)
                last.then_inc(sx["p_turned"], 1)
                pe.wait_ge(sx["pt_ready"], g + 1)
                pe.wait_ge(vx_loaded, 16 * (g + 1))
                for j in range(2):
                    for s in range(2):
                        for b in range(G):
                            last = pe.matmul(ps[32 * b:32 * b + 32, 6 + j, :], pST[:, s, 32 * b:32 * b + 32], Vx[:, b, s, j * 512:(j + 1) * 512],
                                             start=(s == 0), stop=(s == 1), tile_position=(0, 32 * b))
                last.then_inc(sx["out"], 1)
                pe.wait_ge(sx["o_moved"], g + 1)
                for k in range(KD):
                    last = pe.transpose(ps[:, 2 + k // 4, (k % 4) * P:(k % 4 + 1) * P], oS[:, k * P:(k + 1) * P], ident)
                last.then_inc(sx["o_turned"], 1)

        @block.scalar
        def _(act):
            for g in range(2):
                for m in range(2 * G * g, 2 * G * (g + 1)):
                    act.wait_ge(sx["turned"], m + 1)
                    n = m // 2
                    if n >= 2:
                        act.wait_ge(sx["scored"], n - 1)
                    nc.scalar.copy(KTx[:, n % 2, 0:4, (m % 2) * P:(m % 2 + 1) * P], ps[:, 2 * (m % 2), :].rearrange("p (k n) -> p k n", k=4)).then_inc(sx["moved_act"], 1)
                act.wait_ge(sx["max"], g + 1)
                nc.scalar.activation(pS[:, :], ps[:, 4, 0:MEM], ACT.Exp, bias=small[:, 46:47], scale=X_SCALE, accum_out=small[:, 47:48]).then_inc(sx["exp"], 1)
                act.wait_ge(sx["out"], g + 1)
                nc.scalar.copy(oS.rearrange("p (a n) -> p a n", a=2), ps[:, 6:8, :]).then_inc(sx["o_moved"], 1)

        @block.vector
        def _(dve):
            link = lambda ins: dve_chain.link(dve, ins)
            link(nc.vector.memset(qpad, 0.0))
            for h in range(H):
                last = nc.vector.tensor_copy(qpad[:, 2 * h:2 * h + 2, :, h], qxT[:, 2 * h:2 * h + 2, SEQ:TOK])
            last.then_inc(sx["q_ready"], 1)
            for g in range(2):
                for m in range(2 * G * g, 2 * G * (g + 1)):
                    dve.wait_ge(sx["turned"], m + 1)
                    n = m // 2
                    if n >= 2:
                        dve.wait_ge(sx["scored"], n - 1)
                    nc.vector.tensor_copy(KTx[:, n % 2, 4:8, (m % 2) * P:(m % 2 + 1) * P], ps[:, 2 * (m % 2) + 1, :].rearrange("p (k n) -> p k n", k=4)).then_inc(sx["moved_dve"], 1)
                dve.wait_ge(sx["scored"], G * (g + 1))
                link(nc.vector.tensor_reduce(small[:, 46:47], ps[:, 4, 0:MEM], AX, ALU.max))
                nc.vector.tensor_scalar(small[:, 46:47], small[:, 46:47], -X_SCALE, None, ALU.mult).then_inc(sx["max"], 1)
                dve.wait_ge(sx["exp"], g + 1)
                link(nc.vector.reciprocal(small[:, 48:49], small[:, 47:48]))
                nc.vector.tensor_scalar(pS[:, :], pS[:, :], small[:, 48:49], None, ALU.mult).then_inc(sx["probs"], 1)
                dve.wait_ge(sx["p_turned"], g + 1)
                nc.vector.tensor_copy(pST[:, :, :].rearrange("p s n -> p (s n)"), ps[:, 5, 0:2 * P]).then_inc(sx["pt_ready"], 1)
                dve.wait_ge(sx["o_turned"], g + 1)
                for h in range(H):
                    src = ps[:, 2 + h // 2, :].rearrange("p (k b n) -> p k b n", k=4, b=G)[:, 2 * (h % 2):2 * (h % 2) + 2, :, h]
                    last = nc.vector.tensor_copy(oxT[:, 2 * h:2 * h + 2, SEQ + g * G:SEQ + (g + 1) * G], src)
                last.then_inc(sx["o_done"], 1)

    early_moe = Arena(arena, AT_WXQ)
    b1 = early_moe.take([3 * NE, 3 * D], BF16)
    pick = early_moe.take([3 * NE, NE * SLOTS], BF16)
    wr = early_moe.take([P, KD, NE])
    br = early_moe.take([P, NE])
    AT_MOE = early_moe.at
    bias = early_moe.take([NE, 3 * D])
    part = early_moe.take([NE, 3 * D], BF16)
    assert early_moe.at <= AT_WXO
    mo = {n: sem("moe_" + n, n.endswith("loaded")) for n in ("r_loaded", "b_loaded", "pick_loaded", "logits", "top", "exp", "sel", "pos", "rounds")}

    def load_router(sp):
        sp.dma_start(bias[:, 0:2 * D], b_e1[0]).then_inc(mo["b_loaded"], 16)
        sp.dma_start(bias[:, 2 * D:3 * D], b_e2[0]).then_inc(mo["b_loaded"], 16)
        sp.dma_start(wr, w_router[0].rearrange("(k p) n -> p k n", p=P)).then_inc(mo["r_loaded"], 16)
        sp.dma_start(br, b_router[0].partition_broadcast(P)).then_inc(mo["r_loaded"], 16)
        sp.dma_start(pick, const_bf16).then_inc(mo["pick_loaded"], 16)

    def split_biases(dve):
        dve.wait_ge(mo["b_loaded"], 32)
        for i in range(3):
            dve_chain.link(dve, nc.vector.tensor_copy(b1[i * NE:(i + 1) * NE, :], bias[:, :]))
            if i < 2:
                dve_chain.link(dve, nc.vector.tensor_copy(part[:, :], bias[:, :]))
                dve_chain.link(dve, nc.vector.tensor_tensor(bias[:, :], bias[:, :], part[:, :], ALU.subtract))

    add_projection("cross_out", oxT, wxo, wx_loaded, 32, load_router, split_biases)
    late_moe = Arena(arena, AT_MOE)
    xh = late_moe.take([P, NT, D])
    LG = late_moe.take([P, NT, NE + 8])
    LR = late_moe.take([P, NT, NE + 8])
    top = late_moe.take([P, NT, 8])
    sel = late_moe.take([P, NT, NE])
    gate = late_moe.take([P, NT, NE])
    MAXR = -(-TOK // SLOTS)
    slot = late_moe.take([P, NT, MAXR * NE + 2])
    cnt = late_moe.take([P, 8])
    rounds = late_moe.take([P, 2], I32)

    normed_transposed("ffn", res, (0, 1, 2), V_FFN, x_loaded, 64, late_moe.at, xh)

    with nc.Block() as block:
        @block.tensor
        def _(pe):
            pe.wait_ge(mo["r_loaded"], 32)
            for t in range(NT):
                for k in range(KD):
                    last = pe.matmul(ps[0:ROWS[t], t, 0:NE], xnT[:, k, cols(t)], wr[:, k, :], start=(k == 0), stop=(k == KD - 1))
            last.then_inc(mo["logits"], 1)
            pe.wait_ge(mo["sel"], 1)
            for t in range(NT):
                r = ROWS[t]
                for j in range(t):
                    pe.matmul(ps[0:r, 4 + t, 0:NE], c_(C_ONE, r), sel[:, j, :], start=(j == 0), stop=False)
                pe.matmul(ps[0:r, 4 + t, 0:NE], c_(C_BEF, r, r), sel[0:r, t, :], start=(t == 0), stop=True)
            for t in range(NT):
                last = pe.matmul(ps[:, 7, 0:NE], c_(C_ONE), sel[:, t, :], start=(t == 0), stop=(t == NT - 1))
            last.then_inc(mo["pos"], 1)

        @block.scalar
        def _(act):
            act.wait_ge(mo["top"], NT)
            for t in range(NT):
                r = ROWS[t]
                last = nc.scalar.activation(gate[0:r, t, :], LG[0:r, t, 0:NE], ACT.Exp, bias=cnt[0:r, t:t + 1])
            last.then_inc(mo["exp"], 1)

        @block.vector
        def _(dve):
            link = lambda ins: dve_chain.link(dve, ins)
            nc.vector.memset(LG[:, :, NE:NE + 8], 3 * NEG)
            nc.vector.memset(sel[:, :, :], 0.0)
            nc.vector.memset(slot, -1.0)
            link(nc.vector.memset(gate[:, :, :], 0.0))
            dve.wait_ge(mo["logits"], 1)
            for t in range(NT):
                r = ROWS[t]
                link(nc.vector.tensor_tensor(LG[0:r, t, 0:NE], ps[0:r, t, 0:NE], br[0:r, :], ALU.add))
                link(nc.vector.max(top[0:r, t, :], LG[0:r, t, :]))
                nc.vector.tensor_scalar(cnt[0:r, t:t + 1], top[0:r, t, 0:1], -1.0, None, ALU.mult).then_inc(mo["top"], 1)
                link(nc.vector.memset(top[0:r, t, TOPK:8], 3 * NEG))
                link(nc.vector.match_replace(LR[0:r, t, :], top[0:r, t, :], LG[0:r, t, :], 4 * NEG))
                link(nc.vector.tensor_tensor(sel[0:r, t, :], LR[0:r, t, 0:NE], LG[0:r, t, 0:NE], ALU.not_equal))
            nc.vector.tensor_copy(small[:, 61:62], small[:, 62:63]).then_inc(mo["sel"], 1)
            dve.wait_ge(mo["exp"], 1)
            link(nc.vector.tensor_tensor(gate[:, :, :], gate[:, :, :], sel[:, :, :], ALU.mult))
            link(nc.vector.tensor_reduce(cnt[:, 3:6], gate[:, :, :], AX, ALU.add))
            link(nc.vector.tensor_scalar(cnt[:, 3:6], cnt[:, 3:6], 1e-30, None, ALU.max))
            link(nc.vector.reciprocal(cnt[:, 3:6], cnt[:, 3:6]))
            nc.vector.tensor_tensor(gate[:, :, :], gate[:, :, :], rep(cnt[:, 3:6], [P, NT, NE]), ALU.mult)
            dve.wait_ge(mo["pos"], 1)
            for t in range(NT):
                r = ROWS[t]
                first = slot[0:r, t, 0:NE]
                link(nc.vector.scalar_tensor_tensor(first, ps[0:r, 4 + t, 0:NE], 1.0, sel[0:r, t, :], ALU.add, ALU.mult))
                link(nc.vector.tensor_scalar(first, first, -1.0, None, ALU.add))
                for i in range(1, MAXR):
                    nc.vector.tensor_scalar(slot[0:r, t, i * NE:(i + 1) * NE], first, -float(SLOTS * i), None, ALU.add)
            link(nc.vector.tensor_reduce(cnt[:, 6:7], ps[:, 7, 0:NE], AX, ALU.max))
            link(nc.vector.memset(cnt[:, 7:8], 1.0))
            for i in range(1, MAXR):
                link(nc.vector.scalar_tensor_tensor(cnt[:, 7:8], cnt[:, 6:7], float(SLOTS * i), cnt[:, 7:8], ALU.is_gt, ALU.add))
            link(nc.vector.tensor_scalar(cnt[:, 6:7], cnt[:, 7:8], float(NE // 2), -1.0, ALU.mult, ALU.add))
            nc.vector.tensor_copy(rounds[:, 0:1], cnt[:, 7:8])
            nc.vector.tensor_copy(rounds[:, 1:2], cnt[:, 6:7]).then_inc(mo["rounds"], 1)

    PAIRS = NE // 2
    picked = late_moe.take([P, NT, P])
    gated = late_moe.take([P, NT, P])
    gT = late_moe.take([P, NT, P])
    xe = late_moe.take([P, KD, P])
    glu = late_moe.take([P, D])
    lin = late_moe.take([P, D])
    sg = late_moe.take([P, D])
    aT = late_moe.take([P, KD, P])
    ye = late_moe.take([P, D])
    lp = {n: sem("pair_" + n) for n in ("picked", "gathered", "xe_ready", "gt_turned", "gt_ready", "glu", "clipped", "joined", "sig", "act", "a_turned",
                                        "a_act", "a_dve", "y_act", "y_dve", "combined", "added")}

    COMBINE_BANKS = (6, 7, 4, 5, 6, 7)

    def wait_hidden(eng, it):
        eng.wait_ge(free[15 % RING], it * 2 + 2)

    def wait_y(eng, it):
        eng.wait_ge(free[23 % RING], it * 2 + 2)

    def n_rounds(eng):
        return eng.value_load(rounds[0:1, 0:1], min_val=1, max_val=MAXR)

    def last_pair(eng):
        return eng.value_load(rounds[0:1, 1:2], min_val=PAIRS - 1, max_val=MAXR * PAIRS - 1)

    with nc.Block() as block:
        @block.sync
        def _(sp):
            nr = n_rounds(sp)
            with sp.Fori(0, nr * PAIRS - 1) as it:
                e = sp.snap((it % PAIRS) * 2)
                after = sp.snap(((it + 1) % PAIRS) * 2)
                for n in range(RING, FILLS):
                    sp.wait_ge(free[n % RING], it * 2 + 1)
                    fill(sp, n, e)
                for n in range(RING):
                    sp.wait_ge(free[n % RING], it * 2 + 2)
                    fill(sp, n, after)
            final = last_pair(sp)
            for n in range(RING, FILLS):
                sp.wait_ge(free[n % RING], final * 2 + 1)
                fill(sp, n, NE - 2)

        @block.tensor
        def _(pe):
            def gather(done):
                pe.wait_ge(lp["picked"], done + 1)
                for k in range(KD):
                    for t in range(NT):
                        last = pe.matmul(ps[:, 6 + k // 4, (k % 4) * P:(k % 4 + 1) * P], xh[0:ROWS[t], t, k * P:(k + 1) * P],
                                         picked[0:ROWS[t], t, :], start=(t == 0), stop=(t == NT - 1))
                last.then_inc(lp["gathered"], 1)

            def expert_bias(it, a, banks):
                mine = pick[:, bass.ds(pe.snap((it % PAIRS) * P), P)] if type(it) is not int else pick[:, 0:P]
                for i, bank in enumerate(banks):
                    pe.matmul(ps[:, bank, :], mine, b1[:, a + i * 512:a + (i + 1) * 512], start=True, stop=True)

            def hidden(it, k):
                for x in range(2):
                    n = 2 * k + x
                    pe.wait_ge(full[n % RING], (it * 2 + n // RING + 1) * 16)
                for c in range(4):
                    for x in range(2):
                        n = 2 * k + x
                        last = pe.matmul(ps[64 * x:64 * x + 64, c, :], xe[:, k, 64 * x:64 * x + 64], ring[n % RING][:, c * 512:(c + 1) * 512],
                                         start=False, stop=(k == KD - 1), skip_group_check=True)
                        if c == 3:
                            last.then_inc(free[n % RING], 1)

            def start_hidden(it):
                expert_bias(it, 0, range(4))
                pe.wait_ge(lp["xe_ready"], it + 1)
                hidden(it, 0)

            def turn_gates(it):
                pe.wait_ge(lp["added"], it * 6 + 3)
                for t in range(NT):
                    last = pe.transpose(ps[:, 4, t * P:t * P + ROWS[t]], gated[0:ROWS[t], t, :], c_(C_ID, ROWS[t], ROWS[t]))
                last.then_inc(lp["gt_turned"], 1)

            def output(it):
                pe.wait_ge(lp["act"], it + 1)
                for k in range(KD):
                    last = pe.transpose(ps[:, 6 + k // 4, (k % 4) * P:(k % 4 + 1) * P], lin[:, k * P:(k + 1) * P], ident)
                last.then_inc(lp["a_turned"], 1)
                pe.wait_ge(lp["gt_ready"], it + 1)
                expert_bias(it, 2 * D, (4, 5))
                pe.wait_ge(lp["a_act"], it + 1)
                pe.wait_ge(lp["a_dve"], it + 1)
                for n in range(16, FILLS, 2):
                    for x in range(2):
                        pe.wait_ge(full[(n + x) % RING], (it * 2 + (n + x) // RING + 1) * 16)
                    for j in range(2):
                        k = n - 16 + j
                        for c in range(2):
                            for x in range(2):
                                last = pe.matmul(ps[64 * x:64 * x + 64, 4 + c, :], aT[:, k, 64 * x:64 * x + 64],
                                                 ring[(n + x) % RING][:, j * D + c * 512:j * D + (c + 1) * 512],
                                                 start=False, stop=(k == KD - 1), skip_group_check=True)
                                if c == 1 and j == 1:
                                    last.then_inc(free[(n + x) % RING], 1)

            def combine(it):
                pe.wait_ge(lp["y_act"], it + 1)
                pe.wait_ge(lp["y_dve"], it + 1)
                for t in range(NT):
                    for c in range(2):
                        if t == 2:
                            pe.wait_ge(lp["added"], it * 6 + (7 + c))
                        pe.matmul(ps[0:ROWS[t], COMBINE_BANKS[2 * t + c], :], gT[:, t, 0:ROWS[t]], ye[:, c * 512:(c + 1) * 512],
                                  start=True, stop=True).then_inc(lp["combined"], 1)

            pe.wait_ge(mo["pick_loaded"], 16)
            nr = n_rounds(pe)
            gather(0)
            start_hidden(0)
            with pe.Fori(0, nr * PAIRS - 1) as it:
                hidden(it, 1)
                turn_gates(it)
                for k in range(2, KD):
                    hidden(it, k)
                after = pe.snap(it + 1)
                pe.wait_ge(lp["added"], it * 6 + 6)
                gather(after)
                pe.wait_ge(lp["xe_ready"], it + 2)
                output(it)
                start_hidden(after)
                combine(it)
            final = last_pair(pe)
            hidden(final, 1)
            turn_gates(final)
            for k in range(2, KD):
                hidden(final, k)
            pe.wait_ge(lp["added"], final * 6 + 6)
            output(final)
            combine(final)

        @block.scalar
        def _(act):
            def pair(it):
                act.wait_ge(lp["gt_turned"], it + 1)
                nc.scalar.copy(gT[:, 0:2, :], ps[:, 4, 0:2 * P].rearrange("p (t n) -> p t n", t=2))
                nc.scalar.copy(gT[:, 2, 0:DEC], ps[:, 4, 2 * P:2 * P + DEC]).then_inc(lp["gt_ready"], 1)
                act.wait_ge(lp["glu"], it + 1)
                nc.scalar.activation(sg[:, :], glu[:, :], ACT.Sigmoid, scale=1.702).then_inc(lp["sig"], 1)
                act.wait_ge(lp["a_turned"], it + 1)
                nc.scalar.copy(aT[:, 0:4, :].rearrange("p k n -> p (k n)"), ps[:, 6, :]).then_inc(lp["a_act"], 1)
                wait_y(act, it)
                nc.scalar.copy(ye[:, 0:512], ps[:, 4, :]).then_inc(lp["y_act"], 1)

            nr = n_rounds(act)
            with act.Fori(0, nr * PAIRS) as it:
                pair(it)

        @block.vector
        def _(dve):
            def tables(done):
                for x in range(2):
                    for t in range(NT):
                        q = ROWS[t]
                        io = c_(C_IOTA, SLOTS, q)
                        if type(done) is int:
                            place, mine = slice(x, x + 1), slice(x, x + 1)
                        else:
                            place, mine = bass.ds(done * 2 + x, 1), bass.ds((done % PAIRS) * 2 + x, 1)
                        nc.vector.tensor_scalar(picked[0:q, t, 64 * x:64 * x + 64], io, slot[0:q, t, place], None, ALU.is_equal)
                        last = nc.vector.tensor_scalar(gated[0:q, t, 64 * x:64 * x + 64], io, slot[0:q, t, place], gate[0:q, t, mine], ALU.is_equal, ALU.mult)
                last.then_inc(lp["picked"], 1)

            def expert_input(done):
                dve.wait_ge(lp["gathered"], done + 1)
                for j in range(2):
                    last = nc.vector.tensor_tensor(xe[:, 4 * j:4 * j + 4, :], ps[:, 6 + j, :].rearrange("p (k n) -> p k n", k=4),
                                                   rep(vec[:, V_FFN + 4 * j:V_FFN + 4 * j + 4], [P, 4, P]), ALU.mult)
                last.then_inc(lp["xe_ready"], 1)

            def activation(it):
                wait_hidden(dve, it)
                hid = ps[:, 0:4, :].rearrange("p c (n j) -> p c n j", j=2)
                nc.vector.tensor_scalar(glu[:, :].rearrange("p (c n) -> p c n", c=4), hid[:, :, :, 0], 7.0, None, ALU.min).then_inc(lp["glu"], 1)
                nc.vector.tensor_scalar(lin[:, :].rearrange("p (c n) -> p c n", c=4), hid[:, :, :, 1], 7.0, -7.0, ALU.min, ALU.max).then_inc(lp["clipped"], 1)
                dve.wait_ge(lp["clipped"], it + 1)
                nc.vector.scalar_tensor_tensor(lin[:, :], lin[:, :], 1.0, glu[:, :], ALU.add, ALU.mult).then_inc(lp["joined"], 1)
                dve.wait_ge(lp["joined"], it + 1)
                dve.wait_ge(lp["sig"], it + 1)
                nc.vector.tensor_tensor(lin[:, :], lin[:, :], sg[:, :], ALU.mult).then_inc(lp["act"], 1)

            def add_outputs(it):
                dve.wait_ge(lp["a_turned"], it + 1)
                nc.vector.tensor_copy(aT[:, 4:8, :].rearrange("p k n -> p (k n)"), ps[:, 7, :]).then_inc(lp["a_dve"], 1)
                wait_y(dve, it)
                nc.vector.tensor_copy(ye[:, 512:D], ps[:, 5, :]).then_inc(lp["y_dve"], 1)
                for t in range(NT):
                    for c in range(2):
                        i = 2 * t + c
                        dve.wait_ge(lp["combined"], it * 6 + (i + 1))
                        a = res[0:ROWS[t], t, c * 512:(c + 1) * 512]
                        nc.vector.tensor_tensor(a, a, ps[0:ROWS[t], COMBINE_BANKS[i], :], ALU.add).then_inc(lp["added"], 1)

            nr = n_rounds(dve)
            dve.sem_inc(lp["added"], 6)
            tables(0)
            expert_input(0)
            with dve.Fori(0, nr * PAIRS - 1) as it:
                after = dve.snap(it + 1)
                dve.wait_ge(lp["gt_turned"], it + 1)
                tables(after)
                activation(it)
                expert_input(after)
                add_outputs(it)
            final = last_pair(dve)
            activation(final)
            add_outputs(final)

    fn = {n: sem("final_" + n) for n in ("gain", "sq", "var", "root", "done")}
    with nc.Block() as block:
        place = Arena(arena, AT_MOE)
        nf, junk = place.take([P, D]), place.take([P, D])

        @block.sync
        def _(sp):
            sp.dma_start(nf[:, :], norm_final.partition_broadcast(P)).then_inc(fn["gain"], 16)
            sp.wait_ge(fn["done"], 1)
            store(sp, y_prompt[0, 0:P, :], res[:, 0, :])
            sp.wait_ge(fn["done"], 2)
            store(sp, y_prompt[0, P:SEQ, :], res[:, 1, :])
            sp.wait_ge(fn["done"], 3)
            store(sp, y_sample[:, 0, :], res[0:DEC, 2, :])
            sp.wait_ge(stored, n_stored[0])

        @block.scalar
        def _(act):
            for t in range(NT):
                act_chain.link(act, nc.scalar.activation(junk[0:ROWS[t], :], res[0:ROWS[t], t, :], ACT.Square, accum_out=small[0:ROWS[t], t:t + 1]))
            nc.scalar.copy(small[:, 3:4], small[:, 3:4]).then_inc(fn["sq"], 1)
            act.wait_ge(fn["var"], 1)
            nc.scalar.activation(small[:, 4:7], small[:, 4:7], ACT.Sqrt).then_inc(fn["root"], 1)

        @block.vector
        def _(dve):
            dve.wait_ge(fn["sq"], 1)
            nc.vector.tensor_scalar(small[:, 4:7], small[:, 0:3], 1.0 / D, EPS, ALU.mult, ALU.add).then_inc(fn["var"], 1)
            dve.wait_ge(fn["root"], 1)
            dve_chain.link(dve, nc.vector.reciprocal(small[:, 8:11], small[:, 4:7]))
            dve.wait_ge(fn["gain"], 16)
            for t in range(NT):
                a = res[0:ROWS[t], t, :]
                nc.vector.scalar_tensor_tensor(a, a, small[0:ROWS[t], 8 + t:9 + t], nf[0:ROWS[t], :], ALU.mult, ALU.mult).then_inc(fn["done"], 1)

INPUTS = ("x_prompt", "x_sample", "state_gdn", "state_conv", "cache_latent", "cache_krope", "page_table",
          "cache_mem_k", "cache_mem_v", "mem_prompt", "norm_mix", "w_in", "conv_w", "a_log", "dt_bias", "gdn_norm",
          "q_norm", "w_uq", "kv_norm", "w_uk", "w_uv", "w_out", "norm_x", "mem_norm", "w_xq", "w_xk", "w_xv", "w_xo",
          "norm_ffn", "w_router", "b_router", "w_e1", "b_e1", "w_e2", "b_e2", "norm_final")
OUTPUTS = ((1, SEQ, D), (DEC, 1, D), (1, 1, H, P, P), (1, 1, 3, CONV), (1, 1, SEQ, KVR), (1, 1, SEQ, ROPE),
           (1, 1, MEM, H, XD), (1, 1, MEM, H, XD), (1, DEC, H, P, P), (1, DEC, 3, CONV), (DEC, 1, 1, KVR),
           (DEC, 1, 1, ROPE))


def kernel(**inputs):
    import concourse.bacc as bacc
    from concourse.bass_utils import run_bass_kernel_spmd

    nc = bacc.Bacc("TRN2", target_bir_lowering=False, num_devices=1)
    arrays = {name: np.ascontiguousarray(inputs[name]) for name in INPUTS}
    arrays["const_f32"], arrays["const_bf16"] = constants()
    args = [nc.dram_tensor(f"in_{n}", a.shape, mybir.dt.from_np(a.dtype), kind="ExternalInput").ap()
            for n, a in arrays.items()]
    args += [nc.dram_tensor(f"out_{i}", s, F32, kind="ExternalOutput").ap() for i, s in enumerate(OUTPUTS)]
    build(nc, *args)
    ran = run_bass_kernel_spmd(nc, [{f"in_{n}": a for n, a in arrays.items()}], core_ids=[0])
    return tuple(ran.results[0][f"out_{i}"] for i in range(len(OUTPUTS)))
```

```python
import numpy as np

import concourse.bass as bass
from concourse import mybir

F32 = mybir.dt.float32
BF16 = mybir.dt.bfloat16
I32 = mybir.dt.int32
ALU = mybir.AluOpType
ACT = mybir.ActivationFunctionType
AX = mybir.AxisListType.X

P = 128
D = 1024
KD = D // P
SEQ, DEC = 256, 8
TOK = SEQ + DEC
NT = 3
ROWS = (P, P, DEC)
H = 4
CHUNK = 64
CONV = 1536
CB = CONV // P
TAPS = 4
REST = 1224
Z0, B0, A0, CQ0, CKV0, KR0 = 0, 512, 516, 520, 904, 1160
IN_COLS = CONV + REST
QR, KVR, ROPE, NOPE = 384, 256, 64, 128
QK = NOPE + ROPE
PAST, PAGE = 2048, 128
NPAGE = PAST // PAGE
MLA_SCALE = QK ** -0.5
XD = 256
MEM = 256
NE, TOPK = 32, 4
SLOTS = 64
EPS = 1e-6
NEG = -1e30
LEVELS = 6

C_ID, C_ONE, C_TRI, C_BLK, C_LVL = 0, 128, 256, 384, 512
C_BEF = C_LVL + LEVELS * P
C_CAUS = C_BEF + P
C_IOTA = C_CAUS + P
C_CH2 = C_IOTA + SLOTS
C_SEQ = C_CH2 + 2
C_COS = C_SEQ + 2 * P
C_SIN = C_COS + NT * 32
C_PAGE = C_SIN + NT * 32
C_SUB = C_PAGE + P
C_HEAD = C_SUB + 1
C_ALL = C_HEAD + H

ARENA = 45680
CACHED = (PAST // P) * (KVR + ROPE)
AT_WIN, AT_HEADS, AT_HIST = 0, 22528, 44032

V_CONV, V_MIX, V_MEM, V_X, V_FFN, V_Q, V_GDN, V_ALL = 0, 48, 56, 64, 72, 80, 83, 84


def constants():
    r = np.arange(P)
    row, col = r[:, None], r[None, :]
    c = np.zeros((P, C_ALL), np.float32)
    c[:, C_ID:C_ID + P] = row == col
    c[:, C_ONE:C_ONE + P] = 1.0
    same = row // CHUNK == col // CHUNK
    c[:, C_TRI:C_TRI + P] = (row <= col) & same
    c[:, C_BLK:C_BLK + P] = same
    for m in range(LEVELS):
        c[:, C_LVL + m * P:C_LVL + (m + 1) * P] = (row < col) & ((row ^ col) >> m == 1)
    c[:, C_BEF:C_BEF + P] = row < col
    c[:, C_CAUS:C_CAUS + P] = np.where(col <= row, 0.0, NEG)
    c[:, C_IOTA:C_IOTA + SLOTS] = np.arange(SLOTS)[None, :]
    c[:, C_CH2:C_CH2 + 2] = row // CHUNK == np.arange(2)[None, :]
    for g in range(2):
        c[:, C_SEQ + g * P:C_SEQ + (g + 1) * P] = row == 4 * g + col // 32
    half = ROPE // 2
    freq = (1.0 / (np.float32(10000.0) ** (np.arange(half, dtype=np.float32) / np.float32(half)))).astype(np.float32)
    for t in range(NT):
        pos = (t * P + r if t < 2 else np.full(P, PAST)).astype(np.float32)
        ang = (pos[:, None] * freq[None, :]).astype(np.float32)
        c[:, C_COS + 32 * t:C_COS + 32 * (t + 1)] = np.cos(ang)
        c[:, C_SIN + 32 * t:C_SIN + 32 * (t + 1)] = np.sin(ang)
    c[:, C_PAGE:C_PAGE + P] = row == col // (P // NPAGE)
    c[:, C_SUB] = r % (P // NPAGE)
    c[:, C_HEAD:C_HEAD + H] = row % 32 == np.arange(H)[None, :]
    sel = np.repeat(np.tile(np.eye(NE, dtype=np.float32), (3, 1)), SLOTS, axis=1)
    return c, sel.astype("bfloat16")


class Chain:

    def __init__(self, sem):
        self.sem, self.n = sem, 0

    def link(self, eng, ins):
        self.n += 1
        ins.then_inc(self.sem, 1)
        eng.wait_ge(self.sem, self.n)


class Arena:

    def __init__(self, tensor, at):
        self.tensor, self.at = tensor, at

    def take(self, shape, dt=F32):
        n = int(np.prod(shape[1:])) * (2 if dt is BF16 else 4) // 4
        ap = self.tensor[0:shape[0], self.at:self.at + n]
        self.at += n
        assert self.at <= self.tensor.shape[1], self.at
        if dt is not F32:
            ap = ap.bitcast(dt)
        if len(shape) > 2:
            names = "abcd"[:len(shape) - 1]
            ap = ap.rearrange(f"p ({' '.join(names)}) -> p {' '.join(names)}", **{k: n for k, n in zip(names, shape[1:])})
        return ap


def rep(ap, shape):
    return ap.unsqueeze(len(ap.shape)).broadcast_to(shape)


def rep1(ap, shape):
    return ap.unsqueeze(1).broadcast_to(shape)


def cols(t):
    return slice(t * P, t * P + ROWS[t])


def build(nc, x_prompt, x_sample, state_gdn, state_conv, cache_latent, cache_krope, page_table,
          cache_mem_k, cache_mem_v, mem_prompt, norm_mix, w_in, conv_w, a_log, dt_bias, gdn_norm,
          q_norm, w_uq, kv_norm, w_uk, w_uv, w_out, norm_x, mem_norm, w_xq, w_xk, w_xv, w_xo,
          norm_ffn, w_router, b_router, w_e1, b_e1, w_e2, b_e2, norm_final, const_f32, const_bf16,
          y_prompt, y_sample, gdn_prompt, conv_prompt, lat_prompt, kr_prompt, memk_prompt,
          memv_prompt, gdn_sample, conv_sample, lat_sample, kr_sample):
    recent = []

    def sem(name, lasting=False):
        s = nc.alloc_semaphore(name)
        if not lasting:
            recent.append(s)
        return s

    def clear_semaphores():
        nc.clear_and_free_semaphores(list(recent))
        nc.all_engine_barrier()
        recent.clear()

    def keep(name, shape, dt=F32):
        return nc.alloc_sbuf_tensor(name, shape, dt)

    cst = keep("cst", [P, C_ALL])
    vec = keep("vec", [P, V_ALL])
    res = keep("res", [P, NT, D])
    xnT = keep("xnT", [P, KD, TOK])
    arena = keep("arena", [P, ARENA])
    small = keep("small", [P, 64])
    ps = nc.alloc_psum_tensor("ps", [P, 8, 512], F32)

    def c_(at, n=P, rows=P):
        return cst[0:rows, at:at + n]

    ident = c_(C_ID)
    dve_chain, act_chain, pool_chain = (Chain(sem(n, True)) for n in ("dve_steps", "act_steps", "pool_steps"))
    stored = sem("outputs_stored", True)
    n_stored = [0]

    def store(eng, dst, src):
        n_stored[0] += 16
        eng.dma_start(dst, src).then_inc(stored, 16)

    const_loaded, x_loaded, vec_loaded = sem("const_loaded"), sem("x_loaded", True), sem("vec_loaded")
    vec_turned, small_cleared = sem("vec_turned"), sem("small_cleared")
    w_in_loaded = [sem(f"w_in{k}_loaded") for k in range(KD)]
    hist_loaded = sem("history_loaded")
    hist = Arena(arena, AT_HIST).take([DEC * 3, CONV])
    win = Arena(arena, AT_WIN).take([P, KD, IN_COLS])
    def norm_steps(tag, src, tiles, gain_at, ready, ready_at, at, dst=None, kept=None, banks=range(8)):
        squared, varied, rooted, scaled = (sem(f"{tag}_{n}") for n in ("squared", "varied", "rooted", "scaled"))
        turned, emptied = sem(f"{tag}_turned"), sem(f"{tag}_emptied")
        place_of = Arena(arena, at)
        junk = place_of.take([P, D])
        xs = place_of.take([P, 2, D]) if kept is None else kept
        dst = xnT if dst is None else dst
        n, nb = len(tiles), len(banks)

        def squares(act):
            act.wait_ge(ready, ready_at)
            for t in tiles:
                act_chain.link(act, nc.scalar.activation(junk[0:ROWS[t], :], src[0:ROWS[t], t, :], ACT.Square,
                                                        accum_out=small[0:ROWS[t], t:t + 1]))
            nc.scalar.copy(small[:, 3:4], small[:, 3:4]).then_inc(squared, 1)
            act.wait_ge(varied, 1)
            nc.scalar.activation(small[:, 4:4 + n], small[:, 4:4 + n], ACT.Sqrt).then_inc(rooted, 1)

        def factors(dve):
            dve.wait_ge(squared, 1)
            nc.vector.tensor_scalar(small[:, 4:4 + n], small[:, 0:n], 1.0 / D, EPS, ALU.mult, ALU.add).then_inc(varied, 1)
            dve.wait_ge(rooted, 1)
            dve_chain.link(dve, nc.vector.reciprocal(small[:, 8:8 + n], small[:, 4:4 + n]))

        def scale(dve, i):
            t, place = tiles[i], i % 2 if kept is None else i
            if i >= 2 and kept is None:
                dve.wait_ge(turned, 2 * (i - 1))
            nc.vector.tensor_scalar(xs[0:ROWS[t], place, :], src[0:ROWS[t], t, :], small[0:ROWS[t], 8 + t:9 + t], None, ALU.mult).then_inc(scaled, 1)

        def turn(pe, i):
            r, place = ROWS[tiles[i]], i % 2 if kept is None else i
            pe.wait_ge(scaled, i + 1)
            for j in range(2):
                if 2 * i + j >= nb:
                    pe.wait_ge(emptied, 2 * i + j - nb + 1)
                for k in range(4):
                    last = pe.transpose(ps[:, banks[(2 * i + j) % nb], k * P:k * P + r],
                                        xs[0:r, place, (4 * j + k) * P:(4 * j + k + 1) * P], c_(C_ID, r, r))
                last.then_inc(turned, 1)

        def take_out(dve, i):
            r = ROWS[tiles[i]]
            for j in range(2):
                dve.wait_ge(turned, 2 * i + j + 1)
                nc.vector.tensor_tensor(dst[:, 4 * j:4 * j + 4, cols(tiles[i])],
                                        ps[:, banks[(2 * i + j) % nb], :].rearrange("p (k n) -> p k n", k=4)[:, :, 0:r],
                                        rep(vec[:, gain_at + 4 * j:gain_at + 4 * j + 4], [P, 4, r]), ALU.mult).then_inc(emptied, 1)

        return squares, factors, scale, turn, take_out

    def normed_transposed(tag, src, tiles, *rest_of, **named):
        squares, factors, scale, turn, take_out = norm_steps(tag, src, tiles, *rest_of, **named)
        with nc.Block() as block:
            @block.scalar
            def _(act):
                squares(act)

            @block.vector
            def _(dve):
                factors(dve)
                scale(dve, 0)
                for i in range(len(tiles)):
                    if i + 1 < len(tiles):
                        scale(dve, i + 1)
                    take_out(dve, i)

            @block.tensor
            def _(pe):
                for i in range(len(tiles)):
                    turn(pe, i)

    with nc.Block() as block:
        squares, factors, scale, turn, take_out = norm_steps("mix", res, (0, 1, 2), V_MIX, x_loaded, 32, AT_HEADS, banks=range(6))
        vrow = Arena(arena, AT_HEADS + 3 * D).take([V_ALL, P])

        @block.sync
        def _(sp):
            sp.dma_start(res[:, 0:2, :], x_prompt[0].rearrange("(t p) d -> p t d", p=P)).then_inc(x_loaded, 16)
            sp.dma_start(res[0:DEC, 2, :], x_sample[:, 0, :]).then_inc(x_loaded, 16)
            sp.dma_start(hist, state_conv[0].rearrange("b j c -> (b j) c")).then_inc(hist_loaded, 16)
            sp.wait_ge(const_loaded, 16)
            sp.wait_ge(vec_loaded, 7 * 16)
            for k in range(KD):
                sp.dma_start(win[:, k, :], w_in[0, k * P:(k + 1) * P, :]).then_inc(w_in_loaded[k], 16)

        @block.scalar
        def _(act):
            act.dma_start(cst[:, :], const_f32).then_inc(const_loaded, 16)
            for at, v, n in ((V_MIX, norm_mix, KD), (V_MEM, mem_norm, KD), (V_X, norm_x, KD),
                             (V_FFN, norm_ffn, KD), (V_Q, q_norm, 3), (V_GDN, gdn_norm, 1)):
                act.dma_start(vrow[at:at + n, :], v[0].rearrange("(k p) -> k p", p=P)).then_inc(vec_loaded, 16)
            act.dma_start(vrow[V_CONV:V_MIX, :], conv_w[0].rearrange("j (c p) -> (j c) p", p=P)).then_inc(vec_loaded, 16)
            act.wait_ge(small_cleared, 1)
            squares(act)

        @block.tensor
        def _(pe):
            pe.wait_ge(const_loaded, 16)
            pe.wait_ge(vec_loaded, 7 * 16)
            pe.transpose(ps[:, 7, 0:V_ALL], vrow[:, :], c_(C_ID, V_ALL, V_ALL)).then_inc(vec_turned, 1)
            for i in range(NT):
                turn(pe, i)

        @block.vector
        def _(dve):
            dve.memset(small[:, :], 0.0).then_inc(small_cleared, 1)
            factors(dve)
            scale(dve, 0)
            scale(dve, 1)
            dve.wait_ge(vec_turned, 1)
            dve_chain.link(dve, dve.tensor_copy(vec[:, :], ps[:, 7, 0:V_ALL]))
            take_out(dve, 0)
            scale(dve, 2)
            take_out(dve, 1)
            take_out(dve, 2)

    heads = Arena(arena, AT_HEADS)
    qkv = heads.take([P, CB, TOK])
    rest = heads.take([P, NT, REST])
    AT_STATES = heads.at
    cp = heads.take([P, CB, SEQ + TAPS - 1])
    cs = heads.take([P, CB, DEC, TAPS])
    tail = heads.take([3 + DEC, CONV])
    tmp = heads.take([P, CB, DEC])
    raw = heads.take([P, CB, 3 + DEC])
    sig = heads.take([P, CB, TOK])
    yT = xnT
    AT_SLOTS = 2 * CACHED
    keepers = Arena(arena, AT_STATES)
    st = keepers.take([P, DEC * H, P])
    otok = keepers.take([P, NT, H, P])
    S = keepers.take([P, H, P])
    gsb = keepers.take([P, 104])
    eg = keepers.take([P, 104])
    gw = keepers.take([P, 8, NT * H])
    alog = keepers.take([P, H])
    dtb = keepers.take([P, H])
    kts, dts = keepers.take([DEC, H, P]), keepers.take([DEC, H, P])
    dT, oT, pr = (keepers.take([P, H, DEC]) for _ in range(3))
    AT_LATENT = keepers.at
    latT = keepers.take([P, 2, TOK])
    krT = keepers.take([P, TOK])
    qnT = keepers.take([P, H, TOK])
    qrT = keepers.take([P, H, TOK])
    kvn = keepers.take([P, KVR])
    ukT = keepers.take([P, H, KVR])
    assert keepers.at - AT_LATENT >= PAST // P * KVR
    brief = Arena(arena, AT_SLOTS)
    cqT = brief.take([P, 3, TOK])
    knT = brief.take([P, H, SEQ])
    vtok = brief.take([P, 2, H * P])
    qr = brief.take([P, NT, H * ROPE])
    kr = brief.take([P, NT, ROPE])
    rt = brief.take([P, NT, H, 32])
    sc = brief.take([P, H, 384])
    pT = brief.take([P, H, 384])
    upper = Arena(arena, AT_SLOTS + 10 * 1024)
    uk, uv = upper.take([P, 2, H, NOPE]), upper.take([P, 2, H, P])
    qlp = keepers.take([P, 2, DEC, 32])
    qrp = keepers.take([P, 2, DEC, 32])
    KT = keepers.take([P, 2, 2, 640])
    uq = KT[:, :, :, :].rearrange("p g a n -> p (g a n)")[:, 0:3 * H * QK].rearrange("p (k h n) -> p k h n", k=3, h=H)
    snew = keepers.take([DEC, DEC, H])
    idx = keepers.take([P, DEC], I32)
    idxf = keepers.take([P, DEC])
    pgi = keepers.take([NPAGE, DEC], I32)
    pgf = keepers.take([NPAGE, DEC])
    lmax, nmax, lsum = (keepers.take([P, DEC]) for _ in range(3))
    early = res[:, :, :].rearrange("p t n -> p (t n)")
    Pb = early[:, 0:512]
    PT = early[:, 512:1024].rearrange("p (m n) -> p m n", m=4)
    acc = early[:, 1024:1024 + DEC * KVR].rearrange("p (b n) -> p b n", b=DEC)
    ml = {n: sem("mla_" + n) for n in ("w_loaded", "uq_loaded", "kvn_loaded", "var", "root", "lat_ready", "kr_ready", "turned",
                                       "moved", "proj", "proj_moved", "qr_made", "qr_ready", "qr_turned", "k_made", "k_moved", "pages", "pages_f", "pages_spread", "idx", "uk_turned", "uk_moved", "ql_made", "ql_ready", "snew")}

    REST_CUTS = ((0, 512), (512, 904), (904, REST))
    QUARTER = REST // 4
    conv_proj, conv_moved = sem("conv_projected"), sem("conv_moved")
    rest_proj, rest_moved = sem("rest_projected"), sem("rest_moved")
    hist_turned = sem("history_turned")
    hist_moved, raw_moved = sem("history_moved"), sem("raw_moved")
    rest_cleared = sem("rest_cleared")
    tail_turned, tail_moved = sem("tail_turned"), sem("tail_moved")
    conv_done, sig_done = sem("conv_done"), sem("conv_sigmoid_done")
    with nc.Block() as block:
        @block.sync
        def _(sp):
            sp.wait_ge(hist_moved, 1)
            sp.dma_start(pgi, page_table.rearrange("b j -> j b"), allow_slow_non_contiguous=True).then_inc(ml["pages"], 16)
            sp.dma_start(kvn[:, :], kv_norm[0].partition_broadcast(P)).then_inc(ml["kvn_loaded"], 16)
            sp.dma_start(uq, w_uq[0].rearrange("(k p) h n -> p k h n", p=P)).then_inc(ml["uq_loaded"], 16)
            store(sp, conv_sample[0, :, 0:2, :], state_conv[0, :, 1:3, :])
            sp.wait_ge(tail_moved, 3)
            store(sp, conv_prompt[0, 0], tail[0:3, :])
            store(sp, conv_sample[0, :, 2, :], tail[3:3 + DEC, :])
            sp.wait_ge(stored, n_stored[0])

        @block.tensor
        def _(pe):
            pe.wait_ge(hist_loaded, 16)
            for c in range(CB):
                last = pe.transpose(ps[:, 7, c * 24:(c + 1) * 24], hist[:, c * P:(c + 1) * P], c_(C_ID, 24, 24))
            last.then_inc(hist_turned, 1)
            pe.wait_ge(hist_moved, 1)
            for k in range(KD):
                pe.wait_ge(w_in_loaded[k], 16)
                for c in range(8):
                    last = pe.matmul(ps[:, c, 0:TOK], win[:, k, c * P:(c + 1) * P], xnT[:, k, :],
                                     start=(k == 0), stop=(k == KD - 1))
                    if k == KD - 1:
                        last.then_inc(conv_proj, 1)
            for c in range(8, CB):
                pe.wait_ge(conv_moved, c - 7)
                for k in range(KD):
                    last = pe.matmul(ps[:, c % 8, 0:TOK], win[:, k, c * P:(c + 1) * P], xnT[:, k, :],
                                     start=(k == 0), stop=(k == KD - 1))
                last.then_inc(conv_proj, 1)
            n = 0
            for t in range(2):
                if t == 1:
                    pe.wait_ge(raw_moved, 1)
                    for j in range(3):
                        for c in range(4):
                            last = pe.transpose(ps[0:3 + DEC, j, c * P:(c + 1) * P], raw[:, 4 * j + c, :], ident)
                        last.then_inc(tail_turned, 1)
                for a, b in REST_CUTS:
                    if n < 3:
                        pe.wait_ge(conv_moved, 5 + n)
                    else:
                        pe.wait_ge(rest_moved, n - 2)
                    for k in range(KD):
                        last = pe.matmul(ps[:, 4 + n % 3, 0:b - a], xnT[:, k, cols(t)],
                                         win[:, k, CONV + a:CONV + b], start=(k == 0), stop=(k == KD - 1))
                    last.then_inc(rest_proj, 1)
                    n += 1
            pe.wait_ge(conv_moved, 8)
            for k in range(KD):
                for j in range(4):
                    a = CONV + QUARTER * j
                    last = pe.matmul(ps[32 * j:32 * j + DEC, 7, 0:QUARTER], xnT[:, k, cols(2)], win[:, k, a:a + QUARTER],
                                     start=(k == 0), stop=(k == KD - 1), tile_position=(0, 32 * j))
            last.then_inc(rest_proj, 1)

        @block.vector
        def _(dve):
            link = lambda ins: dve_chain.link(dve, ins)
            nc.vector.memset(rest[:, 2, :], 0.0).then_inc(rest_cleared, 1)
            link(nc.vector.memset(cp[:, :, 0:TAPS - 1], 0.0))
            dve.wait_ge(hist_turned, 1)
            nc.vector.tensor_copy(cs[:, :, :, 0:3], ps[:, 7, 0:CB * 24].rearrange("p (c b j) -> p c b j", c=CB, j=3)).then_inc(hist_moved, 1)
            for c in range(CB):
                dve.wait_ge(conv_proj, c + 1)
                nc.vector.tensor_copy(cs[:, c, :, 3], ps[:, c % 8, SEQ:TOK])
                nc.vector.tensor_copy(raw[:, c, :], ps[:, c % 8, SEQ - 3:TOK])
                link(nc.vector.tensor_copy(cp[:, c, 3:3 + SEQ], ps[:, c % 8, 0:SEQ]))
                nc.vector.tensor_copy(small[:, 63:64], small[:, 62:63]).then_inc(conv_moved, 1)
                for j in range(TAPS):
                    w = vec[:, V_CONV + CB * j + c:V_CONV + CB * j + c + 1]
                    if j == 0:
                        link(nc.vector.tensor_scalar(qkv[:, c, 0:SEQ], cp[:, c, j:j + SEQ], w, None, ALU.mult))
                    else:
                        link(nc.vector.scalar_tensor_tensor(qkv[:, c, 0:SEQ], cp[:, c, j:j + SEQ], w, qkv[:, c, 0:SEQ], ALU.mult, ALU.add))
            nc.vector.tensor_copy(small[:, 63:64], small[:, 62:63]).then_inc(raw_moved, 1)
            for j in range(TAPS):
                w = rep(vec[:, V_CONV + CB * j:V_CONV + CB * (j + 1)], [P, CB, DEC])
                if j == 0:
                    link(nc.vector.tensor_tensor(qkv[:, :, SEQ:TOK], cs[:, :, :, 0], w, ALU.mult))
                else:
                    link(nc.vector.tensor_tensor(tmp, cs[:, :, :, j], w, ALU.mult))
                    link(nc.vector.tensor_tensor(qkv[:, :, SEQ:TOK], qkv[:, :, SEQ:TOK], tmp, ALU.add))
            nc.vector.tensor_copy(small[:, 63:64], small[:, 62:63]).then_inc(conv_done, 1)
            for j in range(3):
                dve.wait_ge(tail_turned, j + 1)
                nc.vector.tensor_copy(tail[:, 4 * P * j:4 * P * (j + 1)], ps[0:3 + DEC, j, :]).then_inc(tail_moved, 1)
            dve.wait_ge(sig_done, 1)
            nc.vector.tensor_tensor(qkv[:, :, 0:TOK], qkv[:, :, 0:TOK], sig, ALU.mult)

        @block.scalar
        def _(act):
            act.wait_ge(rest_cleared, 1)
            n = 0
            for t in range(2):
                if t == 1:
                    act.wait_ge(conv_done, 1)
                    nc.scalar.activation(sig, qkv[:, :, :], ACT.Sigmoid).then_inc(sig_done, 1)
                for a, b in REST_CUTS:
                    act.wait_ge(rest_proj, n + 1)
                    nc.scalar.copy(rest[:, t, a:b], ps[:, 4 + n % 3, 0:b - a]).then_inc(rest_moved, 1)
                    n += 1
            act.wait_ge(rest_proj, n + 1)
            for j in range(4):
                nc.scalar.copy(rest[0:DEC, 2, QUARTER * j:QUARTER * (j + 1)], ps[32 * j:32 * j + DEC, 7, 0:QUARTER])
            act_chain.link(act, nc.scalar.copy(small[:, 60:61], small[:, 59:60]))
            junk = cp[:, 0:2, :].rearrange("p c n -> p (c n)")
            for t in range(NT):
                for at, n, a in ((CQ0, QR, 12), (CKV0, KVR, 15)):
                    act_chain.link(act, nc.scalar.activation(junk[:, 0:n], rest[:, t, at:at + n], ACT.Square, accum_out=small[:, a + t:a + t + 1]))

    def rope(dve, dst, src, tmp, cos, sin):
        half = ROPE // 2
        x1, x2 = (src[..., 0:half], src[..., half:ROPE])
        o1, o2 = (dst[..., 0:half], dst[..., half:ROPE])
        nc.vector.tensor_tensor(o1, x1, cos, ALU.mult)
        dve_chain.link(dve, nc.vector.tensor_tensor(tmp, x2, sin, ALU.mult))
        nc.vector.tensor_tensor(o1, o1, tmp, ALU.subtract)
        dve_chain.link(dve, nc.vector.tensor_tensor(o2, x2, cos, ALU.mult))
        dve_chain.link(dve, nc.vector.tensor_tensor(tmp, x1, sin, ALU.mult))
        return nc.vector.tensor_tensor(o2, o2, tmp, ALU.add)

    TILES = PAST // P
    cached = Arena(arena, 0)
    lat_slots, kr_slots = [], []
    for _ in range(2):
        lat_slots.append(cached.take([P, TILES, KVR]))
        kr_slots.append(cached.take([P, TILES, ROPE]))
    lat_slots.append(Arena(arena, AT_LATENT).take([P, TILES, KVR]))
    kr_slots.append(Arena(arena, AT_SLOTS + 10 * 1024).take([P, TILES, ROPE]))
    NSLOT = len(lat_slots)
    seq_loaded = [sem(f"sequence_slot{i}_loaded", True) for i in range(NSLOT)]
    lat_rows = cache_latent.rearrange("n l (r s) d -> (n l r) (s d)", r=P // NPAGE)
    kr_rows = cache_krope.rearrange("n l (r s) d -> (n l r) (s d)", r=P // NPAGE)

    def load_sequence(pool, b):
        for slots, rows in ((lat_slots, lat_rows), (kr_slots, kr_rows)):
            pool.indirect_dma_start(slots[b % NSLOT].rearrange("p i n -> p (i n)"), None, rows,
                                    bass.IndirectOffsetOnAxis(ap=idx[:, b:b + 1].bitcast(mybir.dt.uint32), axis=0)).then_inc(seq_loaded[b % NSLOT], 16)

    cos3 = cst[:, C_COS:C_COS + NT * 32].rearrange("p (t n) -> p t n", t=NT)
    sin3 = cst[:, C_SIN:C_SIN + NT * 32].rearrange("p (t n) -> p t n", t=NT)
    with nc.Block() as block:
        @block.sync
        def _(sp):
            sp.dma_start(uk, w_uk[0].rearrange("(k p) h n -> p k h n", p=P)).then_inc(ml["w_loaded"], 16)
            sp.dma_start(uv, w_uv[0].rearrange("(k p) h n -> p k h n", p=P)).then_inc(ml["w_loaded"], 16)
            sp.wait_ge(ml["lat_ready"], NT)
            store(sp, lat_prompt[0, 0].rearrange("(t p) n -> p t n", p=P), rest[:, 0:2, CKV0:CKV0 + KVR])
            store(sp, lat_sample[:, 0, 0, :], rest[0:DEC, 2, CKV0:CKV0 + KVR])
            sp.wait_ge(ml["kr_ready"], 1)
            store(sp, kr_prompt[0, 0].rearrange("(t p) n -> p t n", p=P), kr[:, 0:2, :])
            store(sp, kr_sample[:, 0, 0, :], kr[0:DEC, 2, :])
            sp.wait_ge(stored, n_stored[0])

        @block.gpsimd
        def _(pool):
            pool.wait_ge(ml["idx"], 1)
            for b in range(2):
                load_sequence(pool, b)

        @block.scalar
        def _(act):
            act.wait_ge(ml["var"], 1)
            nc.scalar.activation(small[:, 18:24], small[:, 18:24], ACT.Sqrt).then_inc(ml["root"], 1)
            for h in range(H):
                act.wait_ge(ml["proj"], h + 1)
                nc.scalar.copy(qnT[:, h, :], ps[:, h, 0:TOK]).then_inc(ml["proj_moved"], 1)
            for h in range(H):
                act.wait_ge(ml["k_made"], h + 1)
                nc.scalar.copy(knT[:, h, :], ps[:, h, 0:SEQ]).then_inc(ml["k_moved"], 1)
            for t in range(2):
                act.wait_ge(ml["k_made"], H + t + 1)
                nc.scalar.copy(vtok[:, t, :], ps[:, 7 * t, :])

        @block.vector
        def _(dve):
            link = lambda ins: dve_chain.link(dve, ins)
            nc.vector.tensor_scalar(small[:, 18:21], small[:, 12:15], 1.0 / QR, EPS, ALU.mult, ALU.add)
            nc.vector.tensor_scalar(small[:, 21:24], small[:, 15:18], 1.0 / KVR, EPS, ALU.mult, ALU.add).then_inc(ml["var"], 1)
            nc.vector.memset(krT[:, :], 0.0)
            dve.wait_ge(ml["pages"], 16)
            nc.vector.tensor_copy(pgf, pgi).then_inc(ml["pages_f"], 1)
            link(nc.vector.memset(qrT[:, :, :], 0.0))
            link(rope(dve, kr[:, :, :], rest[:, :, KR0:KR0 + ROPE], rt[:, :, 0, :], cos3, sin3))
            nc.vector.tensor_copy(small[:, 61:62], small[:, 62:63]).then_inc(ml["kr_ready"], 1)
            dve.wait_ge(ml["root"], 1)
            link(nc.vector.reciprocal(small[:, 24:30], small[:, 18:24]))
            dve.wait_ge(ml["kvn_loaded"], 16)
            for t in range(NT):
                cq = rest[:, t, CQ0:CQ0 + QR]
                ck = rest[:, t, CKV0:CKV0 + KVR]
                nc.vector.tensor_scalar(cq, cq, small[:, 24 + t:25 + t], None, ALU.mult)
                nc.vector.scalar_tensor_tensor(ck, ck, small[:, 27 + t:28 + t], kvn[:, :], ALU.mult, ALU.mult).then_inc(ml["lat_ready"], 1)
            dve.wait_ge(ml["pages_spread"], 1)
            link(nc.vector.tensor_copy(idxf, ps[:, 7, 0:DEC]))
            nc.vector.tensor_scalar(idx, idxf, float(P // NPAGE), c_(C_SUB, 1), ALU.mult, ALU.add).then_inc(ml["idx"], 1)
            for t in range(NT):
                r = ROWS[t]
                dve.wait_ge(ml["turned"], t + 1)
                nc.vector.tensor_tensor(cqT[:, :, cols(t)], ps[:, 2 * t, 0:3 * P].rearrange("p (k n) -> p k n", k=3)[:, :, 0:r],
                                        rep(vec[:, V_Q:V_Q + 3], [P, 3, r]), ALU.mult)
                nc.vector.tensor_copy(latT[:, :, cols(t)], ps[:, 2 * t + 1, 0:2 * P].rearrange("p (k n) -> p k n", k=2)[:, :, 0:r])
                nc.vector.tensor_copy(krT[0:ROPE, cols(t)], ps[0:ROPE, 2 * t + 1, 2 * P:2 * P + r]).then_inc(ml["moved"], 1)
            link(nc.vector.memset(qr[:, 2, :], 0.0))
            for t in range(NT):
                dve.wait_ge(ml["qr_made"], t + 1)
                r = ROWS[t]
                src = ps[0:r, 4 + t, 0:H * ROPE].rearrange("p (h n) -> p h n", h=H)
                link(rope(dve, qr[0:r, t, :].rearrange("p (h n) -> p h n", h=H), src, rt[0:r, t], rep1(cos3[0:r, t, :], [r, H, 32]),
                          rep1(sin3[0:r, t, :], [r, H, 32])))
            nc.vector.tensor_copy(small[:, 61:62], small[:, 62:63]).then_inc(ml["qr_ready"], 1)
            for t in range(NT):
                r = ROWS[t]
                dve.wait_ge(ml["qr_turned"], t + 1)
                nc.vector.tensor_copy(qrT[0:ROPE, :, cols(t)], ps[0:ROPE, 4 + t, :].rearrange("p (h n) -> p h n", h=H)[:, :, 0:r])

        @block.tensor
        def _(pe):
            pe.wait_ge(ml["pages_f"], 1)
            pe.matmul(ps[:, 7, 0:DEC], c_(C_PAGE, P, NPAGE), pgf, start=True, stop=True).then_inc(ml["pages_spread"], 1)
            pe.wait_ge(ml["kr_ready"], 1)
            for t in range(NT):
                r = ROWS[t]
                pe.wait_ge(ml["lat_ready"], t + 1)
                i = c_(C_ID, r, r)
                for k in range(3):
                    pe.transpose(ps[:, 2 * t, k * P:k * P + r], rest[0:r, t, CQ0 + k * P:CQ0 + (k + 1) * P], i)
                for k in range(2):
                    pe.transpose(ps[:, 2 * t + 1, k * P:k * P + r], rest[0:r, t, CKV0 + k * P:CKV0 + (k + 1) * P], i)
                pe.transpose(ps[0:ROPE, 2 * t + 1, 2 * P:2 * P + r], kr[0:r, t, :], i).then_inc(ml["turned"], 1)
            pe.wait_ge(ml["uq_loaded"], 16)
            pe.wait_ge(ml["moved"], NT)
            for t in range(NT):
                for k in range(3):
                    last = pe.matmul(ps[0:ROWS[t], 4 + t, 0:H * ROPE], cqT[:, k, cols(t)], uq[:, k, :, NOPE:QK], start=(k == 0), stop=(k == 2))
                last.then_inc(ml["qr_made"], 1)
            for h in range(H):
                for k in range(3):
                    last = pe.matmul(ps[:, h, 0:TOK], uq[:, k, h, 0:NOPE], cqT[:, k, :], start=(k == 0), stop=(k == 2))
                last.then_inc(ml["proj"], 1)
            pe.wait_ge(ml["w_loaded"], 32)
            for h in range(H):
                pe.wait_ge(ml["proj_moved"], h + 1)
                for k in range(2):
                    last = pe.matmul(ps[:, h, 0:SEQ], uk[:, k, h, :], latT[:, k, 0:SEQ], start=(k == 0), stop=(k == 1))
                last.then_inc(ml["k_made"], 1)
            pe.wait_ge(ml["qr_ready"], 1)
            for t in range(NT):
                r = ROWS[t]
                for h in range(H):
                    last = pe.transpose(ps[0:ROPE, 4 + t, h * P:h * P + r], qr[0:r, t, h * ROPE:(h + 1) * ROPE], c_(C_ID, r, r))
                last.then_inc(ml["qr_turned"], 1)
            for t in range(2):
                if t == 0:
                    pe.wait_ge(ml["k_moved"], 1)
                for k in range(2):
                    last = pe.matmul(ps[:, 7 * t, :], latT[:, k, cols(t)], uv[:, k, :, :], start=(k == 0), stop=(k == 1))
                last.then_inc(ml["k_made"], 1)

    mx = small[:, 30:38]
    ap = {n: sem("att_" + n) for n in ("scored", "max", "exp", "probs", "turned", "pt_ready", "out")}
    with nc.Block() as block:
        @block.tensor
        def _(pe):
            for h in range(H):
                for a, n, q in ((0, P, 0), (P, SEQ, P)):
                    pe.matmul(ps[:, h, a:a + n], qnT[:, h, q:q + P], knT[:, h, 0:n], start=True, stop=False)
                    last = pe.matmul(ps[:, h, a:a + n], qrT[:, h, q:q + P], krT[:, 0:n], start=False, stop=True)
                last.then_inc(ap["scored"], 1)
            for h in range(H):
                for k in range(2):
                    last = pe.transpose(ps[:, 4 + h // 2, (2 * (h % 2) + k) * P:(2 * (h % 2) + k + 1) * P], uk[:, k, h, :], ident)
            last.then_inc(ml["uk_turned"], 1)
            pe.wait_ge(ml["uk_moved"], 1)
            for h in range(H):
                for k in range(2):
                    a = (k * H + h) * DEC
                    last = pe.matmul(ps[:, 6, a:a + DEC], ukT[:, h, k * P:(k + 1) * P], qnT[:, h, SEQ:TOK], start=True, stop=True)
            last.then_inc(ml["ql_made"], 1)
            pe.wait_ge(ml["ql_ready"], 1)
            for k in range(2):
                pe.matmul(ps[0:DEC, 7, 0:DEC * H], latT[:, k, SEQ:TOK], qlp[:, k, :, 0:H], start=(k == 0), stop=False)
            pe.matmul(ps[0:DEC, 7, 0:DEC * H], krT[:, SEQ:TOK], qrp[:, 0, :, 0:H], start=False, stop=True).then_inc(ml["snew"], 1)
            for h in range(H):
                pe.wait_ge(ap["probs"], h + 1)
                for j in range(3):
                    last = pe.transpose(ps[:, h, j * P:(j + 1) * P], sc[:, h, j * P:(j + 1) * P], ident)
                last.then_inc(ap["turned"], 1)
            for h in range(H):
                pe.wait_ge(ap["pt_ready"], h + 1)
                pe.matmul(ps[:, h, 0:P], vtok[:, 0, h * P:(h + 1) * P], pT[:, h, 0:P], start=True, stop=True)
                pe.matmul(ps[:, h, P:SEQ], vtok[:, 0, h * P:(h + 1) * P], pT[:, h, P:SEQ], start=True, stop=False)
                pe.matmul(ps[:, h, P:SEQ], vtok[:, 1, h * P:(h + 1) * P], pT[:, h, SEQ:384], start=False, stop=True).then_inc(ap["out"], 1)

        @block.vector
        def _(dve):
            link = lambda ins: dve_chain.link(dve, ins)
            nc.vector.memset(qlp, 0.0)
            link(nc.vector.memset(qrp, 0.0))
            nc.vector.tensor_copy(qrp[0:ROPE, 0, :, 0:H].rearrange("p b h -> p h b"), qrT[0:ROPE, :, SEQ:TOK])
            nc.vector.tensor_copy(qrp[ROPE:P, 1, :, 0:H].rearrange("p b h -> p h b"), qrT[0:ROPE, :, SEQ:TOK])
            dve.wait_ge(ml["uk_turned"], 1)
            nc.vector.tensor_copy(ukT, ps[:, 4:6, :].rearrange("p a (h n) -> p (a h) n", h=2)).then_inc(ml["uk_moved"], 1)

            def negative_max(h):
                dve.wait_ge(ap["scored"], h + 1)
                for a in (0, SEQ):
                    nc.vector.tensor_tensor(sc[:, h, a:a + P], ps[:, h, a:a + P], c_(C_CAUS), ALU.add)
                link(nc.vector.tensor_copy(sc[:, h, P:SEQ], ps[:, h, P:SEQ]))
                m = mx[:, 2 * h:2 * h + 2]
                nc.vector.tensor_reduce(m[:, 0:1], sc[:, h, 0:P], AX, ALU.max)
                link(nc.vector.tensor_reduce(m[:, 1:2], sc[:, h, P:384], AX, ALU.max))
                nc.vector.tensor_scalar(m, m, -MLA_SCALE, None, ALU.mult).then_inc(ap["max"], 1)

            for h in range(H):
                negative_max(h)
            dve.wait_ge(ml["ql_made"], 1)
            for k in range(2):
                last = nc.vector.tensor_copy(qlp[:, k, :, 0:H].rearrange("p b h -> p h b"), ps[:, 6, k * 32:k * 32 + 32].rearrange("p (h b) -> p h b", h=H))
            last.then_inc(ml["ql_ready"], 1)
            dve.wait_ge(ml["snew"], 1)
            nc.vector.tensor_tensor(snew, ps[0:DEC, 7, 0:DEC * H].rearrange("p (b h) -> p b h", b=DEC), rep(c_(C_ID, DEC, DEC), [DEC, DEC, H]), ALU.mult)
            for h in range(H):
                dve.wait_ge(ap["exp"], h + 1)
                total = small[:, 38 + 2 * h:40 + 2 * h]
                link(nc.vector.reciprocal(total, total))
                nc.vector.tensor_scalar(sc[:, h, 0:P], sc[:, h, 0:P], total[:, 0:1], None, ALU.mult)
                nc.vector.tensor_scalar(sc[:, h, P:384], sc[:, h, P:384], total[:, 1:2], None, ALU.mult).then_inc(ap["probs"], 1)
            for h in range(H):
                dve.wait_ge(ap["turned"], h + 1)
                nc.vector.tensor_copy(pT[:, h, :], ps[:, h, 0:384]).then_inc(ap["pt_ready"], 1)
            for h in range(H):
                dve.wait_ge(ap["out"], h + 1)
                nc.vector.tensor_copy(yT[:, H + h, 0:SEQ], ps[:, h, 0:SEQ])

        @block.scalar
        def _(act):
            for h in range(H):
                act.wait_ge(ap["max"], h + 1)
                for i, (a, b) in enumerate(((0, P), (P, 384))):
                    n = 2 * h + i
                    last = nc.scalar.activation(sc[:, h, a:b], sc[:, h, a:b], ACT.Exp, bias=mx[:, n:n + 1], scale=MLA_SCALE,
                                                accum_out=small[:, 38 + n:39 + n])
                last.then_inc(ap["exp"], 1)
    clear_semaphores()

    G_CUM, G_TOT, G_CH, G_SMP, G_BSMP, G_LEFT = 0, 8, 16, 32, 64, 96
    slots = Arena(arena, AT_SLOTS)
    decT, X, CT, qTe, iT, kd, LT, kbe, vb, XT = (slots.take([P, 2, H, P]) for _ in range(10))
    Y, u, vnew, wT = decT, decT, X, CT
    delta = Arena(arena, AT_SLOTS + 6 * 1024).take([DEC, H, DEC, P])
    sq = Arena(arena, AT_STATES).take([P, 2 * H, TOK])
    rk = small[:, 30:54]
    g, beta = gw[:, 6, :].rearrange("p (t h) -> p t h", h=H), gw[:, 7, :].rearrange("p (t h) -> p t h", h=H)
    state_loaded = sem("state_loaded")
    decay_loaded = sem("decay_loaded")
    g1 = {n: sem("gdn_" + n) for n in (
        "squared", "rows_made", "summed", "added", "rooted", "inverted", "normed", "neg_abs", "exp", "plus1", "ln", "gates", "sums", "sums_read",
        "exp_sums", "rows_exp", "row_min", "dec_exp", "turned", "products", "rows_read")}
    with nc.Block() as block:
        @block.sync
        def _(sp):
            sp.dma_start(alog[:, :], a_log[0].partition_broadcast(P)).then_inc(decay_loaded, 16)
            sp.dma_start(dtb[:, :], dt_bias[0].partition_broadcast(P)).then_inc(decay_loaded, 16)
            sp.wait_ge(g1["rows_made"], 1)
            sp.dma_start(st[:, :, :], state_gdn[0].rearrange("b h k v -> k (b h) v")).then_inc(state_loaded, 16)

        @block.gpsimd
        def _(pool):
            load_sequence(pool, 2)

        @block.scalar
        def _(act):
            nc.scalar.activation(sq[:, :, :], qkv[:, 0:2 * H, :], ACT.Square).then_inc(g1["squared"], 1)
            act.wait_ge(g1["added"], 1)
            nc.scalar.activation(rk, rk, ACT.Sqrt).then_inc(g1["rooted"], 1)
            act.wait_ge(decay_loaded, 32)
            nc.scalar.activation(alog[:, :], alog[:, :], ACT.Exp)
            nc.scalar.activation(gw[:, 4, :].rearrange("p (t h) -> p t h", h=H), rest[:, :, B0:B0 + H], ACT.Exp, scale=-1.0)
            act.wait_ge(g1["neg_abs"], 1)
            nc.scalar.activation(gw[:, 2, :], gw[:, 1, :], ACT.Exp).then_inc(g1["exp"], 1)
            act.wait_ge(g1["plus1"], 1)
            nc.scalar.activation(gw[:, 3, :], gw[:, 2, :], ACT.Ln).then_inc(g1["ln"], 1)
            act.wait_ge(g1["sums"], 1)
            for t in range(2):
                nc.scalar.activation(qTe[:, t].rearrange("p h n -> p (h n)"), ps[:, 1 + t, :], ACT.Exp).then_inc(g1["rows_exp"], 1)
            act.wait_ge(g1["sums_read"], 1)
            nc.scalar.activation(eg[:, :], gsb[:, :], ACT.Exp).then_inc(g1["exp_sums"], 1)
            act.wait_ge(g1["row_min"], 1)
            nc.scalar.activation(decT[:, :, :, :], decT[:, :, :, :], ACT.Exp).then_inc(g1["dec_exp"], 1)

        @block.vector
        def _(dve):
            link = lambda ins: dve_chain.link(dve, ins)
            dve.wait_ge(g1["summed"], 1)
            link(nc.vector.memset(rk, 1.0))
            for t in range(NT):
                r = ROWS[t]
                nc.vector.tensor_scalar(rk[0:r, 8 * t:8 * t + H], ps[0:r, 0, 8 * t:8 * t + H], EPS, float(P), ALU.add, ALU.mult)
                last = nc.vector.tensor_scalar(rk[0:r, 8 * t + H:8 * t + 2 * H], ps[0:r, 0, 8 * t + H:8 * t + 2 * H], EPS, None, ALU.add)
            last.then_inc(g1["added"], 1)
            dve.wait_ge(g1["rooted"], 1)
            nc.vector.reciprocal(rk, rk).then_inc(g1["inverted"], 1)
            dve.wait_ge(decay_loaded, 32)
            a3 = gw[:, 0, :].rearrange("p (t h) -> p t h", h=H)
            link(nc.vector.tensor_tensor(a3, rest[:, :, A0:A0 + H], rep1(dtb[:, :], [P, NT, H]), ALU.add))
            link(nc.vector.tensor_scalar(gw[:, 1, :], gw[:, 0, :], -1.0, None, ALU.mult))
            nc.vector.tensor_tensor(gw[:, 1, :], gw[:, 1, :], gw[:, 0, :], ALU.min).then_inc(g1["neg_abs"], 1)
            dve.wait_ge(g1["exp"], 1)
            nc.vector.tensor_scalar(gw[:, 2, :], gw[:, 2, :], 1.0, None, ALU.add).then_inc(g1["plus1"], 1)
            link(nc.vector.tensor_scalar(gw[:, 4, :], gw[:, 4, :], 1.0, None, ALU.add))
            link(nc.vector.reciprocal(gw[:, 7, :], gw[:, 4, :]))
            dve.wait_ge(g1["ln"], 1)
            link(nc.vector.scalar_tensor_tensor(gw[:, 5, :], gw[:, 0, :], 0.0, gw[:, 3, :], ALU.max, ALU.add))
            nc.vector.scalar_tensor_tensor(g, gw[:, 5, :].rearrange("p (t h) -> p t h", h=H), -1.0,
                                           rep1(alog[:, :], [P, NT, H]), ALU.mult, ALU.mult).then_inc(g1["gates"], 1)
            dve.wait_ge(g1["rows_made"], 1)
            nc.vector.tensor_tensor(qkv[:, 0:2 * H, :], qkv[:, 0:2 * H, :], ps[:, :, 0:TOK], ALU.mult).then_inc(g1["normed"], 1)
            dve.wait_ge(g1["sums"], 1)
            link(nc.vector.tensor_copy(gsb[:, 0:96], ps[:, 0, 0:96]))
            link(nc.vector.tensor_tensor(gsb[:, G_LEFT:G_LEFT + 8], gsb[:, G_TOT:G_TOT + 8], gsb[:, 0:8], ALU.subtract))
            nc.vector.tensor_copy(small[:, 62:63], gsb[:, 0:1]).then_inc(g1["sums_read"], 1)
            dve.wait_ge(g1["rows_exp"], 2)
            for t in range(2):
                link(nc.vector.tensor_tensor(decT[:, t], ps[:, 1 + t, :].rearrange("p (h n) -> p h n", h=H),
                                             rep(gsb[:, 4 * t:4 * t + 4], [P, H, P]), ALU.subtract))
            nc.vector.tensor_scalar(decT[:, :, :, :], decT[:, :, :, :], 0.0, None, ALU.min).then_inc(g1["row_min"], 1)
            dve.wait_ge(g1["normed"], 1)
            for t in range(2):
                nc.vector.tensor_tensor(qTe[:, t], qTe[:, t], qkv[:, 0:H, cols(t)], ALU.mult)
            dve.wait_ge(g1["exp_sums"], 1)
            link(nc.vector.tensor_tensor(gw[:, 0, 0:8], gw[:, 7, 0:8], eg[:, 0:8], ALU.mult))
            dve.wait_ge(g1["dec_exp"], 1)
            link(nc.vector.tensor_tensor(decT[:, :, :, :].rearrange("p t h n -> p (t h) n"), decT[:, :, :, :].rearrange("p t h n -> p (t h) n"),
                                         rep1(c_(C_TRI), [P, 2 * H, P]), ALU.mult))
            for t in range(2):
                link(nc.vector.tensor_tensor(LT[:, t], decT[:, t], ps[:, 3 + t, :].rearrange("p (h n) -> p h n", h=H), ALU.mult))
            nc.vector.tensor_copy(small[:, 62:63], gsb[:, 0:1]).then_inc(g1["rows_read"], 1)
            dve.wait_ge(g1["turned"], 1)
            for t in range(2):
                kt = ps[:, 5 + t, :].rearrange("p (h n) -> p h n", h=H)
                vt = ps[:, (7 + t) % 8, :].rearrange("p (h n) -> p h n", h=H)
                nc.vector.tensor_tensor(kbe[:, t], kt, rep(gw[:, 0, 4 * t:4 * t + 4], [P, H, P]), ALU.mult)
                nc.vector.tensor_tensor(kd[:, t], kt, rep(eg[:, G_LEFT + 4 * t:G_LEFT + 4 * t + 4], [P, H, P]), ALU.mult)
                nc.vector.tensor_tensor(vb[:, t], vt, rep(gw[:, 7, 4 * t:4 * t + 4], [P, H, P]), ALU.mult)
            dve.wait_ge(g1["products"], 1)
            for t in range(2):
                nc.vector.tensor_tensor(LT[:, t], LT[:, t], ps[:, 1 + t, :].rearrange("p (h n) -> p h n", h=H), ALU.mult)
                nc.vector.tensor_tensor(iT[:, t], decT[:, t], ps[:, 3 + t, :].rearrange("p (h n) -> p h n", h=H), ALU.mult)

        @block.tensor
        def _(pe):
            pe.wait_ge(g1["squared"], 1)
            for t in range(NT):
                for c in range(2 * H):
                    last = pe.matmul(ps[0:ROWS[t], 0, 8 * t + c:8 * t + c + 1], sq[:, c, cols(t)], c_(C_ONE, 1), start=True, stop=True)
            last.then_inc(g1["summed"], 1)
            pe.wait_ge(g1["inverted"], 1)
            for t in range(NT):
                for c in range(2 * H):
                    r = ROWS[t]
                    last = pe.matmul(ps[:, c, cols(t)], rk[0:r, 8 * t + c:8 * t + c + 1].broadcast_to([r, P]), c_(C_ID, r, r), start=True, stop=True)
            last.then_inc(g1["rows_made"], 1)
            pe.wait_ge(g1["normed"], 1)
            pe.wait_ge(g1["gates"], 1)
            for t in range(2):
                pe.matmul(ps[:, 0, 4 * t:4 * t + 4], c_(C_TRI), g[:, t, :], start=True, stop=True)
                pe.matmul(ps[:, 0, 8 + 4 * t:12 + 4 * t], c_(C_BLK), g[:, t, :], start=True, stop=True)
                for h in range(H):
                    gcol = g[:, t, h:h + 1].broadcast_to([P, P])
                    a = G_CH + 2 * (4 * t + h)
                    pe.matmul(ps[:, 0, a:a + 2], gcol, c_(C_CH2, 2), start=True, stop=True)
                    pe.matmul(ps[:, 1 + t, h * P:(h + 1) * P], gcol, c_(C_TRI), start=True, stop=True)
                    pe.matmul(ps[:, 3 + t, h * P:(h + 1) * P], beta[:, t, h:h + 1].broadcast_to([P, P]), ident, start=True, stop=True)
            for h in range(H):
                i8 = c_(C_ID, DEC, DEC)
                pe.matmul(ps[:, 0, G_SMP + 8 * h:G_SMP + 8 * h + 8], g[0:DEC, 2, h:h + 1].broadcast_to([DEC, P]), i8, start=True, stop=True)
                last = pe.matmul(ps[:, 0, G_BSMP + 8 * h:G_BSMP + 8 * h + 8], beta[0:DEC, 2, h:h + 1].broadcast_to([DEC, P]), i8, start=True, stop=True)
            last.then_inc(g1["sums"], 1)
            pe.wait_ge(g1["sums_read"], 1)
            for t in range(2):
                for h in range(H):
                    pe.transpose(ps[:, 5 + t, h * P:(h + 1) * P], qkv[:, H + h, cols(t)], ident)
                    last = pe.transpose(ps[:, (7 + t) % 8, h * P:(h + 1) * P], qkv[:, 2 * H + h, cols(t)], ident)
            last.then_inc(g1["turned"], 1)
            pe.wait_ge(g1["rows_exp"], 2)
            pe.wait_ge(g1["rows_read"], 1)
            for t in range(2):
                for h in range(H):
                    pe.matmul(ps[:, 1 + t, h * P:(h + 1) * P], qkv[:, H + h, cols(t)], qkv[:, H + h, cols(t)], start=True, stop=True)
                    last = pe.matmul(ps[:, 3 + t, h * P:(h + 1) * P], qkv[:, H + h, cols(t)], qkv[:, h, cols(t)], start=True, stop=True)
            last.then_inc(g1["products"], 1)

    STEPS = 4 * DEC + 4
    sa = {n: sem("smla_" + n, True) for n in ("even_turned", "odd_turned", "even_moved", "odd_moved", "scored", "max", "exp",
                                              "p_turned", "pt_moved", "pv_done", "acc_moved")}

    def sampled_pe(pe, k):
        b, m = k // 4, k % 4

        def turn(p):
            n, tile = 2 * k + p, 4 * m + 2 * p
            lat, krc = lat_slots[b % NSLOT], kr_slots[b % NSLOT]
            if n > 0:
                pe.wait_ge(sa["even_moved"], n)
            for j in range(2):
                pe.transpose(ps[:, 5, j * P:(j + 1) * P], lat[:, tile, j * P:(j + 1) * P], ident)
            pe.transpose(ps[:, 5, 2 * P:3 * P], krc[:, tile:tile + 2, :].rearrange("p i n -> p (i n)"), ident).then_inc(sa["even_turned"], 1)
            if n > 0:
                pe.wait_ge(sa["odd_moved"], n)
            for j in range(2):
                last = pe.transpose(ps[:, 6, j * P:(j + 1) * P], lat[:, tile + 1, j * P:(j + 1) * P], ident)
            last.then_inc(sa["odd_turned"], 1)

        def score():
            sb, sm_ = (k - 1) // 4, (k - 1) % 4
            pe.wait_ge(sa["even_moved"], 2 * k)
            pe.wait_ge(sa["odd_moved"], 2 * k)
            if sm_ == 0 and sb > 0:
                pe.wait_ge(sa["exp"], sb)
            for j in range(3):
                for i in range(4):
                    keys = KT[:, (k - 1) % 2, i // 2, :]
                    a = (0, P, 2 * P)[j] if i % 2 == 0 else (3 * P, 4 * P, 2 * P)[j]
                    lhs = qlp[:, j, sb, :] if j < 2 else qrp[:, i % 2, sb, :]
                    last = pe.matmul(ps[32 * i:32 * i + 32, 7, sm_ * P:(sm_ + 1) * P], lhs, keys[:, a:a + P],
                                     start=(j == 0), stop=(j == 2), tile_position=(0, 32 * i))
            last.then_inc(sa["scored"], 1)

        if m == 0 and b < DEC:
            pe.wait_ge(seq_loaded[b % NSLOT], 32 * (b // NSLOT + 1))
        if b < DEC:
            turn(0)
        if m != 1 and 0 < k <= 4 * DEC:
            score()
        if b < DEC:
            turn(1)
        if b > 0 and m == 1:
            pe.wait_ge(sa["exp"], b)
            if b > 1:
                pe.wait_ge(sa["acc_moved"], b - 1)
            for j in range(4):
                last = pe.transpose(ps[:, 4, j * P:(j + 1) * P], Pb[:, j * P:(j + 1) * P], ident)
            last.then_inc(sa["p_turned"], 1)
        if b > 0 and m == 2:
            pe.wait_ge(sa["pt_moved"], b)
            for j in range(4):
                for i in range(4):
                    last = pe.matmul(ps[32 * i:32 * i + 32, 4, 0:KVR], PT[:, j, 32 * i:32 * i + 32], lat_slots[(b - 1) % NSLOT][:, 4 * j + i, :],
                                     start=(j == 0), stop=(j == 3), tile_position=(0, 32 * i))
            last.then_inc(sa["pv_done"], 1)
        if m == 1 and k < 4 * DEC:
            score()

    def sampled_dve(dve, k):
        b, m = k // 4, k % 4
        if b > 0 and m == 1:
            dve.wait_ge(sa["scored"], 4 * b)
            dve_chain.link(dve, nc.vector.tensor_reduce(lmax[:, b - 1:b], ps[:, 7, :], AX, ALU.max))
            nc.vector.tensor_scalar(nmax[:, b - 1:b], lmax[:, b - 1:b], -MLA_SCALE, None, ALU.mult).then_inc(sa["max"], 1)
        for p in range(2 if b < DEC else 0):
            dve.wait_ge(sa["odd_turned"], 2 * k + p + 1)
            if k >= 2:
                dve.wait_ge(sa["scored"], k - 1)
            nc.vector.tensor_copy(KT[:, k % 2, p, 3 * P:5 * P], ps[:, 6, 0:2 * P]).then_inc(sa["odd_moved"], 1)
        if b > 0 and m == 1:
            dve.wait_ge(sa["p_turned"], b)
            nc.vector.tensor_copy(PT[:, :, :], ps[:, 4, :].rearrange("p (m n) -> p m n", m=4)).then_inc(sa["pt_moved"], 1)

    def sampled_act(act, k):
        b, m = k // 4, k % 4

        def even(p):
            act.wait_ge(sa["even_turned"], 2 * k + p + 1)
            if k >= 2:
                act.wait_ge(sa["scored"], k - 1)
            nc.scalar.copy(KT[:, k % 2, p, 0:3 * P], ps[:, 5, 0:3 * P]).then_inc(sa["even_moved"], 1)

        if b < DEC:
            even(0)
        if b > 0 and m == 1:
            act.wait_ge(sa["max"], b)
            if b > 1:
                act.wait_ge(sa["p_turned"], b - 1)
            nc.scalar.activation(Pb[:, :], ps[:, 7, :], ACT.Exp, bias=nmax[:, b - 1:b], scale=MLA_SCALE,
                                 accum_out=lsum[:, b - 1:b]).then_inc(sa["exp"], 1)
        if b < DEC:
            even(1)
        if b > 0 and m == 3:
            act.wait_ge(sa["pv_done"], b)
            nc.scalar.copy(acc[:, b - 1, :], ps[:, 4, 0:KVR]).then_inc(sa["acc_moved"], 1)

    def sampled_pool(pool, k):
        b, m = k // 4, k % 4
        if 0 < b <= DEC - NSLOT and m == 2:
            pool.wait_ge(sa["pv_done"], b)
            load_sequence(pool, b - 1 + NSLOT)

    AFTER_Y, AFTER_Z = 1, 1
    STEP_SCAN = (AFTER_Y + AFTER_Z) * (LEVELS - 1)
    PER_CHUNK = 2
    PER_HEAD = 2
    STEP_HEAD = STEP_SCAN + 2 * PER_CHUNK * (SEQ // CHUNK)
    STEP_REST = STEP_HEAD + 2 + PER_HEAD * H
    assert STEP_REST <= STEPS

    def level_steps(m, after_z):
        k = (AFTER_Y + AFTER_Z) * (m - 1)
        return range(k + AFTER_Y, k + AFTER_Y + AFTER_Z) if after_z else range(k, k + AFTER_Y)

    def head_steps(h):
        k = STEP_HEAD + 2 + PER_HEAD * h
        return range(k, k + PER_HEAD)

    def chunk_steps(i, second):
        k = STEP_SCAN + PER_CHUNK * (2 * i + second)
        return range(k, k + PER_CHUNK)

    x0, x_turned, x_ready = sem("inv_first"), sem("inv_turned"), sem("inv_x_ready")
    c_ready, y_made, y_moved, z_made = sem("inv_c_ready"), sem("inv_y_made"), sem("inv_y_moved"), sem("inv_z_made")
    uw_made = sem("uw_made")
    with nc.Block() as block:
        def level(m):
            return rep1(c_(C_LVL + m * P), [P, H, P])

        @block.vector
        def _(dve):
            link = lambda ins: dve_chain.link(dve, ins)
            for t in range(2):
                link(nc.vector.tensor_tensor(CT[:, t], LT[:, t], level(0), ALU.mult))
                nc.vector.tensor_tensor(XT[:, t], rep1(ident, [P, H, P]), CT[:, t], ALU.subtract).then_inc(x0, 1)
            for t in range(2):
                dve_chain.link(dve, nc.vector.tensor_tensor(CT[:, t], LT[:, t], level(1), ALU.mult))
                dve.wait_ge(x_turned, t + 1)
                nc.vector.tensor_copy(X[:, t], ps[:, 2 + t, :].rearrange("p (h n) -> p h n", h=H)).then_inc(x_ready, 1)
            for m in range(1, LEVELS):
                if m + 1 < LEVELS:
                    for t in range(2):
                        dve.wait_ge(y_made, 2 * (m - 1) + t + 1)
                        nc.vector.tensor_tensor(CT[:, t], LT[:, t], level(m + 1), ALU.mult).then_inc(c_ready, 1)
                for k in level_steps(m, False):
                    sampled_dve(dve, k)
                for t in range(2):
                    dve.wait_ge(z_made, 2 * (m - 1) + t + 1)
                    nc.vector.tensor_tensor(X[:, t], X[:, t], ps[:, t, :].rearrange("p (h n) -> p h n", h=H), ALU.subtract)
                    nc.vector.tensor_tensor(XT[:, t], XT[:, t], ps[:, 2 + t, :].rearrange("p (h n) -> p h n", h=H), ALU.subtract).then_inc(x_ready, 1)
                for k in level_steps(m, True):
                    sampled_dve(dve, k)
            for t in range(2):
                dve.wait_ge(uw_made, t + 1)
                nc.vector.tensor_copy(u[:, t], ps[:, t, :].rearrange("p (h n) -> p h n", h=H))
                nc.vector.tensor_copy(wT[:, t], ps[:, 2 + t, :].rearrange("p (h n) -> p h n", h=H))

        @block.scalar
        def _(act):
            for m in range(1, LEVELS):
                for t in range(2):
                    act.wait_ge(y_made, 2 * (m - 1) + t + 1)
                    if m > 1:
                        act.wait_ge(z_made, 2 * (m - 2) + t + 1)
                    nc.scalar.copy(Y[:, t], ps[:, t, :].rearrange("p (h n) -> p h n", h=H)).then_inc(y_moved, 1)
                for after_z in (False, True):
                    for k in level_steps(m, after_z):
                        sampled_act(act, k)

        @block.gpsimd
        def _(pool):
            for k in range(STEP_SCAN):
                sampled_pool(pool, k)

        @block.tensor
        def _(pe):
            for t in range(2):
                pe.wait_ge(x0, t + 1)
                for h in range(H):
                    last = pe.transpose(ps[:, 2 + t, h * P:(h + 1) * P], XT[:, t, h, :], ident)
                last.then_inc(x_turned, 1)
            for m in range(1, LEVELS):
                for t in range(2):
                    if m > 1:
                        pe.wait_ge(c_ready, 2 * (m - 2) + t + 1)
                    pe.wait_ge(x_ready, 2 * (m - 1) + t + 1)
                    for h in range(H):
                        last = pe.matmul(ps[:, t, h * P:(h + 1) * P], CT[:, t, h, :], X[:, t, h, :], start=True, stop=True)
                    last.then_inc(y_made, 1)
                for k in level_steps(m, False):
                    sampled_pe(pe, k)
                for t in range(2):
                    pe.wait_ge(y_moved, 2 * (m - 1) + t + 1)
                    for h in range(H):
                        pe.matmul(ps[:, t, h * P:(h + 1) * P], XT[:, t, h, :], Y[:, t, h, :], start=True, stop=True)
                        last = pe.matmul(ps[:, 2 + t, h * P:(h + 1) * P], Y[:, t, h, :], XT[:, t, h, :], start=True, stop=True)
                    last.then_inc(z_made, 1)
                for k in level_steps(m, True):
                    sampled_pe(pe, k)
            for t in range(2):
                pe.wait_ge(x_ready, 2 * (LEVELS - 1) + t + 1)
                for h in range(H):
                    pe.matmul(ps[:, t, h * P:(h + 1) * P], XT[:, t, h, :], vb[:, t, h, :], start=True, stop=True)
                    last = pe.matmul(ps[:, 2 + t, h * P:(h + 1) * P], kbe[:, t, h, :], XT[:, t, h, :], start=True, stop=True)
                last.then_inc(uw_made, 1)

    NC = SEQ // CHUNK
    seen, v_ready, add_made, s_ready, o_made = (sem(n) for n in ("scan_seen", "scan_v_ready", "scan_add_made", "scan_s_ready", "scan_o_made"))
    with nc.Block() as block:
        @block.scalar
        def _(act):
            for k in range(STEP_SCAN, STEP_HEAD):
                sampled_act(act, k)

        @block.gpsimd
        def _(pool):
            for k in range(STEP_SCAN, STEP_HEAD):
                sampled_pool(pool, k)

        @block.vector
        def _(dve):
            for i in range(NC):
                t, r = i // 2, CHUNK * (i % 2)
                rows = slice(r, r + CHUNK)
                if i == 0:
                    nc.vector.tensor_copy(vnew[rows, t], u[rows, t]).then_inc(v_ready, 1)
                else:
                    dve.wait_ge(seen, i)
                    nc.vector.tensor_tensor(vnew[rows, t], u[rows, t], ps[rows, 0, :].rearrange("p (h n) -> p h n", h=H), ALU.subtract).then_inc(v_ready, 1)
                for k in chunk_steps(i, 0):
                    sampled_dve(dve, k)
                dve.wait_ge(add_made, i + 1)
                for h in range(H):
                    made = ps[:, 1, h * P:(h + 1) * P]
                    a = G_CH + 2 * (4 * t + h) + i % 2
                    if i == 0:
                        last = nc.vector.tensor_copy(S[:, h, :], made)
                    else:
                        last = nc.vector.scalar_tensor_tensor(S[:, h, :], S[:, h, :], eg[:, a:a + 1], made, ALU.mult, ALU.add)
                last.then_inc(s_ready, 1)
                for k in chunk_steps(i, 1):
                    sampled_dve(dve, k)
            for t in range(2):
                dve.wait_ge(o_made, t + 1)
                dve_chain.link(dve, nc.vector.tensor_copy(otok[:, t], ps[:, t, :].rearrange("p (h n) -> p h n", h=H)))
                rows = slice(CHUNK if t == 0 else 0, P)
                nc.vector.tensor_tensor(otok[rows, t], otok[rows, t], ps[rows, 2 + t, :].rearrange("p (h n) -> p h n", h=H), ALU.add)

        @block.tensor
        def _(pe):
            for i in range(NC):
                t, r = i // 2, CHUNK * (i % 2)
                rows = slice(r, r + CHUNK)
                if i > 0:
                    pe.wait_ge(s_ready, i)
                    for h in range(H):
                        last = pe.matmul(ps[rows, 0, h * P:(h + 1) * P], wT[:, t, h, rows], S[:, h, :], start=True, stop=True)
                    last.then_inc(seen, 1)
                    for h in range(H):
                        pe.matmul(ps[rows, 2 + t, h * P:(h + 1) * P], qTe[:, t, h, rows], S[:, h, :], start=True, stop=True)
                for k in chunk_steps(i, 0):
                    sampled_pe(pe, k)
                pe.wait_ge(v_ready, i + 1)
                for h in range(H):
                    last = pe.matmul(ps[:, 1, h * P:(h + 1) * P], kd[rows, t, h, :], vnew[rows, t, h, :], start=True, stop=True)
                last.then_inc(add_made, 1)
                for k in chunk_steps(i, 1):
                    sampled_pe(pe, k)
            pe.wait_ge(s_ready, NC)
            for t in range(2):
                for h in range(H):
                    last = pe.matmul(ps[:, t, h * P:(h + 1) * P], iT[:, t, h, :], vnew[:, t, h, :], start=True, stop=True)
                last.then_inc(o_made, 1)

    AT_WK, AT_MEMT, AT_MV, AT_WOUT, AT_WV, AT_WXQ, AT_WXO = 0, 8192, 10240, 12288, 20480, 28672, 36864
    AT_QX, AT_MKT = AT_WOUT + 3 * D, AT_WOUT + 3 * D + KD * TOK
    weight = lambda at: Arena(arena, at).take([P, KD, D])
    wk, wv, wout, wxq, wxo = (weight(at) for at in (AT_WK, AT_WV, AT_WOUT, AT_WXQ, AT_WXO))
    memt = Arena(arena, AT_MEMT).take([P, 2, D])
    mem_loaded, wkv_loaded, wout_loaded, wxq_loaded, wxo_loaded = (
        sem(n, True) for n in ("mem_loaded", "wkv_loaded", "wout_loaded", "wxq_loaded", "wxo_loaded"))

    def load_w_out(sp, half):
        k = slice(4 * half, 4 * half + 4)
        sp.dma_start(wout[:, k], w_out[0, 512 * half:512 * (half + 1)].rearrange("(k p) n -> p k n", p=P)).then_inc(wout_loaded, 16)

    gn = {n: sem("gnorm_" + n) for n in ("sig", "var", "root", "ready", "turned")}

    def gate_and_squares(dve, tiles, osq, sig):
        link = lambda ins: dve_chain.link(dve, ins)
        a, n = tiles[0], len(tiles)
        o = otok[:, a:a + n].rearrange("p t h n -> p (t h) n")
        z = rest[:, a:a + n, Z0:Z0 + H * P]
        link(nc.vector.tensor_tensor(osq, o, o, ALU.mult))
        link(nc.vector.tensor_reduce(gw[:, 0, H * a:H * (a + n)], osq, AX, ALU.add))
        dve.wait_ge(gn["sig"], 1 + (a > 0))
        link(nc.vector.tensor_tensor(sig, sig, z, ALU.mult))
        link(nc.vector.tensor_tensor(o, o, sig.rearrange("p t (h n) -> p (t h) n", n=P), ALU.mult))

    sm = {n: sem("smp_" + n) for n in ("prod", "seen", "delta", "turned", "blocks", "outer", "updated")}
    with nc.Block() as block:
        place = Arena(arena, AT_SLOTS)
        osq01, sig01 = place.take([P, 2 * H, P]), place.take([P, 2, H * P])

        @block.sync
        def _(sp):
            load_w_out(sp, 0)
            store(sp, gdn_prompt[0, 0].rearrange("h k v -> k h v"), S[:, :, :])
            sp.wait_ge(sm["updated"], H)
            store(sp, gdn_sample[0].rearrange("b h k v -> k (b h) v"), st[:, :, :])

        @block.scalar
        def _(act):
            nc.scalar.activation(sig01, rest[:, 0:2, Z0:Z0 + H * P], ACT.Sigmoid).then_inc(gn["sig"], 1)
            for k in range(STEP_HEAD, STEP_REST):
                sampled_act(act, k)

        @block.gpsimd
        def _(pool):
            for k in range(STEP_HEAD, STEP_REST):
                sampled_pool(pool, k)

        @block.vector
        def _(dve):
            link = lambda ins: dve_chain.link(dve, ins)
            q_s, k_s, v_s = (qkv[:, i * H:(i + 1) * H, SEQ:TOK] for i in range(3))
            egs = eg[:, G_SMP:G_SMP + 32].rearrange("p (h b) -> p h b", h=H)
            bs = gsb[:, G_BSMP:G_BSMP + 32].rearrange("p (h b) -> p h b", h=H)
            nc.vector.memset(otok[:, 2], 0.0)
            nc.vector.tensor_tensor(pr[:, :, :], q_s, k_s, ALU.mult).then_inc(sm["prod"], 1)
            gate_and_squares(dve, (0, 1), osq01, sig01)
            sampled_dve(dve, STEP_HEAD)
            dve.wait_ge(sm["seen"], 1)
            sqk = ps[:, 0, 0:64].rearrange("p (h b j) -> p h b j", h=H, j=2)
            link(nc.vector.tensor_tensor(dT[:, :, :], sqk[:, :, :, 1], egs, ALU.mult))
            link(nc.vector.tensor_tensor(dT[:, :, :], v_s, dT[:, :, :], ALU.subtract))
            link(nc.vector.tensor_tensor(dT[:, :, :], dT[:, :, :], bs, ALU.mult))
            link(nc.vector.tensor_tensor(pr[:, :, :], dT[:, :, :], ps[:, 0, 64:96].rearrange("p (h b) -> p h b", h=H), ALU.mult))
            link(nc.vector.tensor_tensor(oT[:, :, :], sqk[:, :, :, 0], egs, ALU.mult))
            nc.vector.tensor_tensor(oT[:, :, :], oT[:, :, :], pr[:, :, :], ALU.add).then_inc(sm["delta"], 1)
            sampled_dve(dve, STEP_HEAD + 1)
            dve.wait_ge(sm["turned"], 1)
            nc.vector.tensor_copy(kts[:, :, :], ps[0:DEC, 1, :].rearrange("p (h n) -> p h n", h=H))
            link(nc.vector.tensor_copy(dts[:, :, :], ps[0:DEC, 2, :].rearrange("p (h n) -> p h n", h=H)))
            nc.vector.tensor_copy(otok[0:DEC, 2], ps[0:DEC, 3, :].rearrange("p (h n) -> p h n", h=H))
            for h in range(H):
                nc.vector.tensor_tensor(delta[:, h], rep1(dts[:, h, :], [DEC, DEC, P]), rep(c_(C_ID, DEC, DEC), [DEC, DEC, P]), ALU.mult).then_inc(sm["blocks"], 1)
            for h in range(H):
                dve.wait_ge(sm["outer"], h + 1)
                for b in range(DEC):
                    s = st[:, b * H + h, :]
                    last = nc.vector.scalar_tensor_tensor(s, s, eg[:, G_SMP + 8 * h + b:G_SMP + 8 * h + b + 1],
                                                          ps[:, 2 * (h % 2) + b // 4, (b % 4) * P:(b % 4 + 1) * P], ALU.mult, ALU.add)
                last.then_inc(sm["updated"], 1)
                for k in head_steps(h):
                    sampled_dve(dve, k)

        @block.tensor
        def _(pe):
            pe.wait_ge(state_loaded, 16)
            for h in range(H):
                for b in range(DEC):
                    a = 2 * (h * DEC + b)
                    pe.matmul(ps[:, 0, a:a + 2], st[:, b * H + h, :], qkv[:, h:h + 5:4, SEQ + b], start=True, stop=True)
            pe.wait_ge(sm["prod"], 1)
            pe.matmul(ps[:, 0, 64:96], c_(C_ONE), pr[:, :, :], start=True, stop=True).then_inc(sm["seen"], 1)
            sampled_pe(pe, STEP_HEAD)
            pe.wait_ge(sm["delta"], 1)
            for h in range(H):
                pe.transpose(ps[0:DEC, 1, h * P:(h + 1) * P], qkv[:, H + h, SEQ:TOK], ident)
                pe.transpose(ps[0:DEC, 2, h * P:(h + 1) * P], dT[:, h, :], ident)
                last = pe.transpose(ps[0:DEC, 3, h * P:(h + 1) * P], oT[:, h, :], ident)
            last.then_inc(sm["turned"], 1)
            sampled_pe(pe, STEP_HEAD + 1)
            for h in range(H):
                pe.wait_ge(sm["blocks"], h + 1)
                if h >= 2:
                    pe.wait_ge(sm["updated"], h - 1)
                for j in range(2):
                    last = pe.matmul(ps[:, 2 * (h % 2) + j, :], kts[:, h, :], delta[:, h, 4 * j:4 * j + 4, :], start=True, stop=True)
                last.then_inc(sm["outer"], 1)
                for k in head_steps(h):
                    sampled_pe(pe, k)

    with nc.Block() as block:
        place = Arena(arena, AT_HEADS)
        osq, sig = place.take([P, H, P]), place.take([P, 1, H * P])
        o3 = otok[:, :, :, :].rearrange("p t h n -> p (t h) n")

        @block.sync
        def _(sp):
            load_w_out(sp, 1)
            sp.wait_ge(sa["pv_done"], DEC)
            sp.dma_start(memt, mem_prompt[0].rearrange("(t p) d -> p t d", p=P)).then_inc(mem_loaded, 16)
            sp.dma_start(wk, w_xk[0].rearrange("(k p) n -> p k n", p=P)).then_inc(wkv_loaded, 16)

        @block.gpsimd
        def _(pool):
            for k in range(STEP_REST, STEPS):
                sampled_pool(pool, k)

        @block.scalar
        def _(act):
            nc.scalar.activation(sig, rest[:, 2:3, Z0:Z0 + H * P], ACT.Sigmoid).then_inc(gn["sig"], 1)
            act.wait_ge(gn["var"], 1)
            nc.scalar.activation(gw[:, 1, :], gw[:, 1, :], ACT.Sqrt).then_inc(gn["root"], 1)
            for k in range(STEP_REST, STEPS):
                sampled_act(act, k)

        @block.vector
        def _(dve):
            link = lambda ins: dve_chain.link(dve, ins)
            gate_and_squares(dve, (2,), osq, sig)
            nc.vector.tensor_scalar(gw[:, 1, :], gw[:, 0, :], 1.0 / P, EPS, ALU.mult, ALU.add).then_inc(gn["var"], 1)
            dve.wait_ge(gn["root"], 1)
            link(nc.vector.reciprocal(gw[:, 1, :], gw[:, 1, :]))
            nc.vector.tensor_tensor(o3, o3, rep(gw[:, 1, :], [P, NT * H, P]), ALU.mult).then_inc(gn["ready"], 1)
            for t in range(NT):
                dve.wait_ge(gn["turned"], t + 1)
                nc.vector.tensor_scalar(yT[:, 0:H, cols(t)], ps[:, t, :].rearrange("p (h n) -> p h n", h=H)[:, :, 0:ROWS[t]],
                                        vec[:, V_GDN:V_GDN + 1], None, ALU.mult)
            for k in range(STEP_REST, STEPS):
                sampled_dve(dve, k)

        @block.tensor
        def _(pe):
            pe.wait_ge(gn["ready"], 1)
            for t in range(NT):
                for h in range(H):
                    r = ROWS[t]
                    last = pe.transpose(ps[:, t, h * P:h * P + r], otok[0:r, t, h, :], c_(C_ID, r, r))
                last.then_inc(gn["turned"], 1)
            for k in range(STEP_REST, STEPS):
                sampled_pe(pe, k)

    clear_semaphores()

    jn = {n: sem("join_" + n) for n in ("turned", "max", "exp", "coef", "coef_turned", "ready", "summed", "out_ready", "out", "y")}
    place = Arena(arena, AT_HEADS)
    m8 = place.take([DEC, 4, 32])
    l8 = place.take([DEC, 4, 32])
    own, top, tot = (place.take([DEC, H]) for _ in range(3))
    coef8 = place.take([DEC, 4, 32])
    part = place.take([DEC, 4, H])
    ownm = place.take([DEC, DEC, H])
    csel = place.take([P, DEC, H])
    oLT = place.take([P, 2, DEC, H])

    def join_products(pe, stage):
        if stage == 0:
            pe.transpose(ps[0:DEC, 7, 0:P], lmax, ident)
            pe.transpose(ps[0:DEC, 7, P:2 * P], lsum, ident).then_inc(jn["turned"], 1)
        if stage == 1:
            pe.wait_ge(jn["coef"], 1)
            pe.transpose(ps[:, 7, 0:DEC], coef8.rearrange("p i n -> p (i n)"), c_(C_ID, DEC, DEC))
            for k in range(2):
                last = pe.matmul(ps[:, 7, 64 + 32 * k:96 + 32 * k], rest[0:DEC, 2, CKV0 + k * P:CKV0 + (k + 1) * P],
                                 ownm.rearrange("p b h -> p (b h)"), start=True, stop=True)
            last.then_inc(jn["coef_turned"], 1)
        if stage == 2:
            pe.wait_ge(jn["ready"], 1)
            for k in range(2):
                for b in range(DEC):
                    a = 32 * k + H * b
                    last = pe.matmul(ps[:, 7, a:a + H], acc[:, b, k * P:(k + 1) * P], csel[:, b, :], start=True, stop=True)
            last.then_inc(jn["summed"], 1)
        if stage == 3:
            pe.wait_ge(jn["out_ready"], 1)
            for h in range(H):
                for k in range(2):
                    last = pe.matmul(ps[:, 7, h * DEC:(h + 1) * DEC], uv[:, k, h, :], oLT[:, k, :, h], start=(k == 0), stop=(k == 1))
            last.then_inc(jn["out"], 1)

    def join_exps(act):
        act.wait_ge(jn["max"], 1)
        nc.scalar.activation(part, part, ACT.Exp, scale=MLA_SCALE)
        nc.scalar.activation(own, own, ACT.Exp, scale=MLA_SCALE).then_inc(jn["exp"], 1)

    def join_weights(dve):
        link = lambda ins: dve_chain.link(dve, ins)
        link(nc.vector.tensor_reduce(own, snew.rearrange("p b h -> p h b"), AX, ALU.add))
        nc.vector.memset(coef8, 0.0)
        dve.wait_ge(jn["turned"], 1)
        nc.vector.tensor_copy(m8.rearrange("p i n -> p (i n)"), ps[0:DEC, 7, 0:P])
        link(nc.vector.tensor_copy(l8.rearrange("p i n -> p (i n)"), ps[0:DEC, 7, P:2 * P]))
        link(nc.vector.tensor_reduce(top, m8[:, :, 0:H].rearrange("p i h -> p h i"), AX, ALU.max))
        link(nc.vector.tensor_tensor(top, top, own, ALU.max))
        nc.vector.tensor_tensor(part, m8[:, :, 0:H], rep1(top, [DEC, 4, H]), ALU.subtract)
        nc.vector.tensor_tensor(own, own, top, ALU.subtract).then_inc(jn["max"], 1)
        dve.wait_ge(jn["exp"], 1)
        link(nc.vector.tensor_tensor(l8[:, :, 0:H], l8[:, :, 0:H], part, ALU.mult))
        link(nc.vector.tensor_reduce(tot, l8[:, :, 0:H].rearrange("p i h -> p h i"), AX, ALU.add))
        link(nc.vector.tensor_tensor(tot, tot, own, ALU.add))
        link(nc.vector.reciprocal(tot, tot))
        link(nc.vector.tensor_tensor(own, own, tot, ALU.mult))
        nc.vector.tensor_tensor(coef8[:, :, 0:H], part, rep1(tot, [DEC, 4, H]), ALU.mult)
        nc.vector.tensor_tensor(ownm, rep1(own, [DEC, DEC, H]), rep(c_(C_ID, DEC, DEC), [DEC, DEC, H]), ALU.mult).then_inc(jn["coef"], 1)
        dve.wait_ge(jn["coef_turned"], 1)
        link(nc.vector.tensor_copy(csel, rep(ps[:, 7, 0:DEC], [P, DEC, H])))
        link(nc.vector.tensor_copy(oLT, ps[:, 7, 64:128].rearrange("p (k b h) -> p k b h", k=2, b=DEC)))
        nc.vector.tensor_tensor(csel, csel, rep1(c_(C_HEAD, H), [P, DEC, H]), ALU.mult).then_inc(jn["ready"], 1)

    def join_sum(dve):
        dve.wait_ge(jn["summed"], 1)
        nc.vector.tensor_tensor(oLT, oLT, ps[:, 7, 0:64].rearrange("p (k b h) -> p k b h", k=2, b=DEC), ALU.add).then_inc(jn["out_ready"], 1)

    def join_out(dve):
        dve.wait_ge(jn["out"], 1)
        nc.vector.tensor_copy(yT[:, H:2 * H, SEQ:TOK], ps[:, 7, 0:H * DEC].rearrange("p (h b) -> p h b", h=H)).then_inc(jn["y"], 1)

    def no_more(engine, stage=None):
        pass

    def add_projection(tag, src, w, loaded, at, sync, vector, tensor=no_more, scalar=no_more):
        made = sem(f"{tag}_made")
        with nc.Block() as block:
            @block.sync
            def _(sp):
                sync(sp)

            @block.scalar
            def _(act):
                scalar(act)

            @block.tensor
            def _(pe):
                tensor(pe, 0)
                pe.wait_ge(loaded, at)
                for t in range(2):
                    for n in range(2):
                        for k in range(KD):
                            last = pe.matmul(ps[:, 2 * t + n, :], src[:, k, cols(t)], w[:, k, n * 512:(n + 1) * 512],
                                             start=(k == 0), stop=(k == KD - 1))
                        last.then_inc(made, 1)
                        tensor(pe, 2 * t + n + 1)
                for k in range(KD):
                    for j in range(4):
                        last = pe.matmul(ps[32 * j:32 * j + DEC, 4, 0:D // 4], src[:, k, cols(2)], w[:, k, j * D // 4:(j + 1) * D // 4],
                                         start=(k == 0), stop=(k == KD - 1), tile_position=(0, 32 * j))
                last.then_inc(made, 1)

            @block.vector
            def _(dve):
                vector(dve, 0)
                dve.wait_ge(x_loaded, 64)
                for t in range(2):
                    for n in range(2):
                        dve.wait_ge(made, 2 * t + n + 1)
                        r = res[:, t, n * 512:(n + 1) * 512]
                        nc.vector.tensor_tensor(r, r, ps[:, 2 * t + n, :], ALU.add)
                        vector(dve, 2 * t + n + 1)
                dve.wait_ge(made, 5)
                for j in range(4):
                    r = res[0:DEC, 2, j * D // 4:(j + 1) * D // 4]
                    nc.vector.tensor_tensor(r, r, ps[32 * j:32 * j + DEC, 4, 0:D // 4], ALU.add)

    states_stored = n_stored[0]

    def load_cross_weights(sp):
        sp.wait_ge(jn["summed"], 1)
        sp.dma_start(res[:, 0:2, :], x_prompt[0].rearrange("(t p) d -> p t d", p=P)).then_inc(x_loaded, 16)
        sp.dma_start(res[0:DEC, 2, :], x_sample[:, 0, :]).then_inc(x_loaded, 16)
        sp.wait_ge(jn["out"], 1)
        sp.dma_start(wv, w_xv[0].rearrange("(k p) n -> p k n", p=P)).then_inc(wkv_loaded, 16)
        sp.wait_ge(stored, states_stored)
        sp.dma_start(wxq, w_xq[0].rearrange("(k p) n -> p k n", p=P)).then_inc(wxq_loaded, 16)

    memT = Arena(arena, AT_WXO).take([P, KD, MEM])
    squares, factors, scale, turn, take_out = norm_steps("mem", memt, (0, 1), V_MEM, mem_loaded, 16, AT_WXO + KD * MEM, dst=memT, banks=(5, 6))

    def scalar_beside_mix(act):
        join_exps(act)
        squares(act)

    def tensor_beside_mix(pe, stage):
        if stage < 4:
            join_products(pe, stage)
        if stage in (2, 3):
            turn(pe, stage - 2)
        if stage == 4:
            pe.wait_ge(jn["y"], 1)

    def vector_beside_mix(dve, stage):
        if stage == 0:
            join_weights(dve)
            factors(dve)
            scale(dve, 0)
            scale(dve, 1)
            join_sum(dve)
        if stage == 2:
            take_out(dve, 0)
            join_out(dve)
        if stage == 4:
            take_out(dve, 1)

    add_projection("mix_out", yT, wout, wout_loaded, 32, load_cross_weights, vector_beside_mix, tensor_beside_mix, scalar_beside_mix)

    mk = Arena(arena, AT_QX).take([P, 2, D])
    mkT = Arena(arena, AT_MKT).take([P, KD, MEM])
    mv = Arena(arena, AT_MV).take([P, 2, D])
    qxT = Arena(arena, AT_QX).take([P, KD, TOK])
    oxT = xnT

    G = 4
    Kx = Arena(arena, AT_WK).take([P, G, 2, D])
    Vx = Arena(arena, AT_WV).take([P, G, 2, D])
    kx_loaded = [sem(f"xkey{b}_loaded") for b in range(G)]
    vx_loaded = sem("xvalue_loaded")
    squares, factors, scale, turn, take_out = norm_steps("x", res, (0, 1, 2), V_X, x_loaded, 64, AT_WOUT, banks=(6, 7))
    keys_stored = [0]
    kv_made, kv_moved, mk_turned = sem("kv_made"), sem("kv_moved"), sem("mk_turned")
    with nc.Block() as block:
        @block.sync
        def _(sp):
            sp.wait_ge(kv_moved, 8)
            store(sp, memk_prompt[0, 0].rearrange("(t p) h n -> p t (h n)", p=P), mk)
            store(sp, memv_prompt[0, 0].rearrange("(t p) h n -> p t (h n)", p=P), mv)
            for b in range(G):
                sp.dma_start(Kx[:, b], cache_mem_k[0, b].rearrange("(s p) h n -> p s (h n)", p=P)).then_inc(kx_loaded[b], 16)
            sp.dma_start(Vx, cache_mem_v[0, 0:G].rearrange("b (s p) h n -> p b s (h n)", p=P)).then_inc(vx_loaded, 16)
            keys_stored[0] = n_stored[0]

        @block.tensor
        def _(pe):
            pe.wait_ge(wkv_loaded, 32)
            i = 0
            for w in range(2):
                for t in range(2):
                    for n in range(2):
                        if i >= 6:
                            pe.wait_ge(kv_moved, i - 5)
                        for k in range(KD):
                            last = pe.matmul(ps[:, i % 6, :], memT[:, k, cols(t)], (wk, wv)[w][:, k, n * 512:(n + 1) * 512], start=(k == 0), stop=(k == KD - 1))
                        last.then_inc(kv_made, 1)
                        if 1 <= i <= NT:
                            turn(pe, i - 1)
                        i += 1
            pe.wait_ge(kv_moved, 6)
            for j in range(4):
                for k in range(2):
                    for t in range(2):
                        b = 2 * j + k
                        last = pe.transpose(ps[:, 2 + j, (2 * k + t) * P:(2 * k + t + 1) * P], mk[:, t, b * P:(b + 1) * P], ident)
                last.then_inc(mk_turned, 1)

        @block.scalar
        def _(act):
            squares(act)

        @block.vector
        def _(dve):
            factors(dve)
            scale(dve, 0)
            for i in range(8):
                dve.wait_ge(kv_made, i + 1)
                dst = (mk if i < 4 else mv)[:, (i // 2) % 2, (i % 2) * 512:(i % 2 + 1) * 512]
                nc.vector.tensor_copy(dst, ps[:, i % 6, :]).then_inc(kv_moved, 1)
                if i < NT - 1:
                    scale(dve, i + 1)
                if 1 <= i <= NT:
                    take_out(dve, i - 1)
            for j in range(4):
                dve.wait_ge(mk_turned, j + 1)
                nc.vector.tensor_copy(mkT[:, 2 * j:2 * j + 2, :].rearrange("p k n -> p (k n)"), ps[:, 2 + j, :])

    RING = 12
    AT_RING = (AT_MEMT, AT_WOUT, AT_MV, AT_MKT, *(AT_WK + 2048 * i for i in range(4)), *(AT_WV + 2048 * i for i in range(4)))
    ring = [arena[:, at:at + 2048] for at in AT_RING]
    full = [sem(f"ring{s}_full", True) for s in range(RING)]
    free = [sem(f"ring{s}_free", True) for s in range(RING)]
    FILLS = 24

    def fill(sp, n, e):
        s, x = n % RING, n % 2
        if n < 16:
            k = n // 2
            src = w_e1[0, bass.ds(e + x, 1), k * P:(k + 1) * P, :].rearrange("a p n -> (a p) n")
            sp.dma_start(ring[s], src).then_inc(full[s], 16)
        else:
            k = 2 * ((n - 16) // 2)
            src = w_e2[0, bass.ds(e + x, 1), k * P:(k + 2) * P, :].rearrange("a (k p) n -> p (a k) n", p=P)
            sp.dma_start(ring[s].rearrange("p (k n) -> p k n", k=2), src).then_inc(full[s], 16)

    after_wxq = Arena(arena, AT_WXQ)
    scx = after_wxq.take([P, 8, MEM])
    pTx = after_wxq.take([P, H, 2, SEQ])
    X_SCALE = XD ** -0.5
    cx = {n: sem("cross_" + n) for n in ("q_made", "q_moved", "scored", "max", "exp", "probs", "turned", "pt_ready", "out", "out_moved")}
    with nc.Block() as block:
        @block.sync
        def _(sp):
            sp.dma_start(wxo, w_xo[0].rearrange("(k p) n -> p k n", p=P)).then_inc(wxo_loaded, 16)
            for n in range(2):
                fill(sp, n, 0)

        @block.tensor
        def _(pe):
            pe.wait_ge(wxq_loaded, 16)
            for c in range(KD):
                if c >= 4:
                    pe.wait_ge(cx["q_moved"], c - 3)
                for k in range(KD):
                    last = pe.matmul(ps[:, c % 4, 0:TOK], wxq[:, k, c * P:(c + 1) * P], xnT[:, k, :], start=(k == 0), stop=(k == KD - 1))
                last.then_inc(cx["q_made"], 1)
            pe.wait_ge(cx["q_moved"], KD)
            for h in range(H):
                for q in range(2):
                    for k in range(2):
                        last = pe.matmul(ps[:, 4 + h, q * MEM:(q + 1) * MEM], qxT[:, 2 * h + k, q * P:(q + 1) * P], mkT[:, 2 * h + k, :], start=(k == 0), stop=(k == 1))
                last.then_inc(cx["scored"], 1)
            for h in range(H):
                pe.wait_ge(cx["probs"], h + 1)
                for q in range(2):
                    for s in range(2):
                        last = pe.transpose(ps[:, h, s * SEQ + q * P:s * SEQ + (q + 1) * P], scx[:, 2 * h + q, s * P:(s + 1) * P], ident)
                last.then_inc(cx["turned"], 1)
            for k in range(KD):
                pe.wait_ge(cx["pt_ready"], k // 2 + 1)
                if k >= 4:
                    pe.wait_ge(cx["out_moved"], k - 3)
                for s in range(2):
                    last = pe.matmul(ps[:, 4 + k % 4, 0:SEQ], mv[:, s, k * P:(k + 1) * P], pTx[:, k // 2, s, :], start=(s == 0), stop=(s == 1))
                last.then_inc(cx["out"], 1)

        @block.scalar
        def _(act):
            act.wait_ge(stored, keys_stored[0])
            for c in range(KD):
                act.wait_ge(cx["q_made"], c + 1)
                nc.scalar.copy(qxT[:, c, :], ps[:, c % 4, 0:TOK]).then_inc(cx["q_moved"], 1)
            for h in range(H):
                act.wait_ge(cx["max"], h + 1)
                for i in (2 * h, 2 * h + 1):
                    last = nc.scalar.activation(scx[:, i, :], ps[:, 4 + h, (i % 2) * MEM:(i % 2 + 1) * MEM], ACT.Exp,
                                                bias=small[:, 30 + i:31 + i], scale=X_SCALE, accum_out=small[:, 38 + i:39 + i])
                last.then_inc(cx["exp"], 1)

        @block.vector
        def _(dve):
            link = lambda ins: dve_chain.link(dve, ins)

            def negative_max(h):
                dve.wait_ge(cx["scored"], h + 1)
                m = small[:, 30 + 2 * h:32 + 2 * h]
                link(nc.vector.tensor_reduce(m, ps[:, 4 + h, :].rearrange("p (q n) -> p q n", q=2), AX, ALU.max))
                nc.vector.tensor_scalar(m, m, -X_SCALE, None, ALU.mult).then_inc(cx["max"], 1)

            negative_max(0)
            for h in range(H):
                if h + 1 < H:
                    negative_max(h + 1)
                dve.wait_ge(cx["exp"], h + 1)
                total = small[:, 38 + 2 * h:40 + 2 * h]
                link(nc.vector.reciprocal(total, total))
                nc.vector.tensor_tensor(scx[:, 2 * h:2 * h + 2, :], scx[:, 2 * h:2 * h + 2, :], rep(total, [P, 2, MEM]), ALU.mult).then_inc(cx["probs"], 1)
            for h in range(H):
                dve.wait_ge(cx["turned"], h + 1)
                nc.vector.tensor_copy(pTx[:, h, :, :].rearrange("p s n -> p (s n)"), ps[:, h, :]).then_inc(cx["pt_ready"], 1)
            for k in range(KD):
                dve.wait_ge(cx["out"], k + 1)
                nc.vector.tensor_copy(oxT[:, k, 0:SEQ], ps[:, 4 + k % 4, 0:SEQ]).then_inc(cx["out_moved"], 1)

    after_wxq = Arena(arena, AT_WXQ)
    KTx = after_wxq.take([P, 2, KD, MEM])
    qpad = after_wxq.take([P, KD, DEC, 32])
    pS = after_wxq.take([P, MEM])
    pST = after_wxq.take([P, 2, P])
    oS = after_wxq.take([P, D])
    sx = {n: sem("scross_" + n) for n in ("q_ready", "turned", "moved_act", "moved_dve", "scored", "max", "exp", "probs", "p_turned", "pt_ready",
                                          "out", "o_moved", "o_turned", "o_done")}
    with nc.Block() as block:
        @block.sync
        def _(sp):
            for n in (2, 3):
                fill(sp, n, 0)
            for b in range(G):
                sp.wait_ge(sx["scored"], b + 1)
                sp.dma_start(Kx[:, b], cache_mem_k[0, G + b].rearrange("(s p) h n -> p s (h n)", p=P)).then_inc(kx_loaded[b], 16)
            sp.wait_ge(sx["out"], 1)
            sp.dma_start(Vx, cache_mem_v[0, G:2 * G].rearrange("b (s p) h n -> p b s (h n)", p=P)).then_inc(vx_loaded, 16)
            for b in range(G):
                sp.wait_ge(sx["scored"], G + b + 1)
                fill(sp, 4 + b, 0)
            sp.wait_ge(sx["out"], 2)
            for n in range(8, RING):
                fill(sp, n, 0)

        @block.tensor
        def _(pe):
            pe.wait_ge(sx["q_ready"], 1)
            for g in range(2):
                for b in range(G):
                    n = g * G + b
                    pe.wait_ge(kx_loaded[b], 16 * (g + 1))
                    for s in range(2):
                        m = 2 * n + s
                        if m >= 2:
                            pe.wait_ge(sx["moved_act"], m - 1)
                            pe.wait_ge(sx["moved_dve"], m - 1)
                        if g and b == 0:
                            pe.wait_ge(sx["o_done"], g)
                        for k in range(KD):
                            last = pe.transpose(ps[:, 2 * (m % 2) + k // 4, (k % 4) * P:(k % 4 + 1) * P], Kx[:, b, s, k * P:(k + 1) * P], ident)
                        last.then_inc(sx["turned"], 1)
                    pe.wait_ge(sx["moved_act"], 2 * n + 2)
                    pe.wait_ge(sx["moved_dve"], 2 * n + 2)
                    for k in range(KD):
                        last = pe.matmul(ps[32 * b:32 * b + 32, 4, 0:MEM], qpad[:, k, n, :], KTx[:, n % 2, k, :],
                                         start=(k == 0), stop=(k == KD - 1), tile_position=(0, 32 * b))
                    last.then_inc(sx["scored"], 1)
                pe.wait_ge(sx["probs"], g + 1)
                for s in range(2):
                    last = pe.transpose(ps[:, 5, s * P:(s + 1) * P], pS[:, s * P:(s + 1) * P], ident)
                last.then_inc(sx["p_turned"], 1)
                pe.wait_ge(sx["pt_ready"], g + 1)
                pe.wait_ge(vx_loaded, 16 * (g + 1))
                for j in range(2):
                    for s in range(2):
                        for b in range(G):
                            last = pe.matmul(ps[32 * b:32 * b + 32, 6 + j, :], pST[:, s, 32 * b:32 * b + 32], Vx[:, b, s, j * 512:(j + 1) * 512],
                                             start=(s == 0), stop=(s == 1), tile_position=(0, 32 * b))
                last.then_inc(sx["out"], 1)
                pe.wait_ge(sx["o_moved"], g + 1)
                for k in range(KD):
                    last = pe.transpose(ps[:, 2 + k // 4, (k % 4) * P:(k % 4 + 1) * P], oS[:, k * P:(k + 1) * P], ident)
                last.then_inc(sx["o_turned"], 1)

        @block.scalar
        def _(act):
            for g in range(2):
                for m in range(2 * G * g, 2 * G * (g + 1)):
                    act.wait_ge(sx["turned"], m + 1)
                    n = m // 2
                    if n >= 2:
                        act.wait_ge(sx["scored"], n - 1)
                    nc.scalar.copy(KTx[:, n % 2, 0:4, (m % 2) * P:(m % 2 + 1) * P], ps[:, 2 * (m % 2), :].rearrange("p (k n) -> p k n", k=4)).then_inc(sx["moved_act"], 1)
                act.wait_ge(sx["max"], g + 1)
                nc.scalar.activation(pS[:, :], ps[:, 4, 0:MEM], ACT.Exp, bias=small[:, 46:47], scale=X_SCALE, accum_out=small[:, 47:48]).then_inc(sx["exp"], 1)
                act.wait_ge(sx["out"], g + 1)
                nc.scalar.copy(oS.rearrange("p (a n) -> p a n", a=2), ps[:, 6:8, :]).then_inc(sx["o_moved"], 1)

        @block.vector
        def _(dve):
            link = lambda ins: dve_chain.link(dve, ins)
            link(nc.vector.memset(qpad, 0.0))
            for h in range(H):
                last = nc.vector.tensor_copy(qpad[:, 2 * h:2 * h + 2, :, h], qxT[:, 2 * h:2 * h + 2, SEQ:TOK])
            last.then_inc(sx["q_ready"], 1)
            for g in range(2):
                for m in range(2 * G * g, 2 * G * (g + 1)):
                    dve.wait_ge(sx["turned"], m + 1)
                    n = m // 2
                    if n >= 2:
                        dve.wait_ge(sx["scored"], n - 1)
                    nc.vector.tensor_copy(KTx[:, n % 2, 4:8, (m % 2) * P:(m % 2 + 1) * P], ps[:, 2 * (m % 2) + 1, :].rearrange("p (k n) -> p k n", k=4)).then_inc(sx["moved_dve"], 1)
                dve.wait_ge(sx["scored"], G * (g + 1))
                link(nc.vector.tensor_reduce(small[:, 46:47], ps[:, 4, 0:MEM], AX, ALU.max))
                nc.vector.tensor_scalar(small[:, 46:47], small[:, 46:47], -X_SCALE, None, ALU.mult).then_inc(sx["max"], 1)
                dve.wait_ge(sx["exp"], g + 1)
                link(nc.vector.reciprocal(small[:, 48:49], small[:, 47:48]))
                nc.vector.tensor_scalar(pS[:, :], pS[:, :], small[:, 48:49], None, ALU.mult).then_inc(sx["probs"], 1)
                dve.wait_ge(sx["p_turned"], g + 1)
                nc.vector.tensor_copy(pST[:, :, :].rearrange("p s n -> p (s n)"), ps[:, 5, 0:2 * P]).then_inc(sx["pt_ready"], 1)
                dve.wait_ge(sx["o_turned"], g + 1)
                for h in range(H):
                    src = ps[:, 2 + h // 2, :].rearrange("p (k b n) -> p k b n", k=4, b=G)[:, 2 * (h % 2):2 * (h % 2) + 2, :, h]
                    last = nc.vector.tensor_copy(oxT[:, 2 * h:2 * h + 2, SEQ + g * G:SEQ + (g + 1) * G], src)
                last.then_inc(sx["o_done"], 1)

    early_moe = Arena(arena, AT_WXQ)
    b1 = early_moe.take([3 * NE, 3 * D], BF16)
    pick = early_moe.take([3 * NE, NE * SLOTS], BF16)
    wr = early_moe.take([P, KD, NE])
    br = early_moe.take([P, NE])
    AT_MOE = early_moe.at
    bias = early_moe.take([NE, 3 * D])
    part = early_moe.take([NE, 3 * D], BF16)
    assert early_moe.at <= AT_WXO
    mo = {n: sem("moe_" + n, n.endswith("loaded")) for n in ("r_loaded", "b_loaded", "pick_loaded", "logits", "top", "exp", "sel", "pos", "rounds")}

    def load_router(sp):
        sp.dma_start(bias[:, 0:2 * D], b_e1[0]).then_inc(mo["b_loaded"], 16)
        sp.dma_start(bias[:, 2 * D:3 * D], b_e2[0]).then_inc(mo["b_loaded"], 16)
        sp.dma_start(wr, w_router[0].rearrange("(k p) n -> p k n", p=P)).then_inc(mo["r_loaded"], 16)
        sp.dma_start(br, b_router[0].partition_broadcast(P)).then_inc(mo["r_loaded"], 16)
        sp.dma_start(pick, const_bf16).then_inc(mo["pick_loaded"], 16)

    def split_biases(dve, stage):
        if stage > 0:
            return
        dve.wait_ge(mo["b_loaded"], 32)
        for i in range(3):
            dve_chain.link(dve, nc.vector.tensor_copy(b1[i * NE:(i + 1) * NE, :], bias[:, :]))
            if i < 2:
                dve_chain.link(dve, nc.vector.tensor_copy(part[:, :], bias[:, :]))
                dve_chain.link(dve, nc.vector.tensor_tensor(bias[:, :], bias[:, :], part[:, :], ALU.subtract))

    add_projection("cross_out", oxT, wxo, wxo_loaded, 16, load_router, split_biases)
    late_moe = Arena(arena, AT_MOE)
    xh = late_moe.take([P, NT, D])
    LG = late_moe.take([P, NT, NE + 8])
    LR = late_moe.take([P, NT, NE + 8])
    top = late_moe.take([P, NT, 8])
    sel = late_moe.take([P, NT, NE])
    gate = late_moe.take([P, NT, NE])
    MAXR = -(-TOK // SLOTS)
    slot = late_moe.take([P, NT, MAXR * NE + 2])
    cnt = late_moe.take([P, 8])
    rounds = late_moe.take([P, 2], I32)

    normed_transposed("ffn", res, (0, 1, 2), V_FFN, x_loaded, 64, late_moe.at, kept=xh)

    with nc.Block() as block:
        @block.tensor
        def _(pe):
            pe.wait_ge(mo["r_loaded"], 32)
            for t in range(NT):
                for k in range(KD):
                    last = pe.matmul(ps[0:ROWS[t], t, 0:NE], xnT[:, k, cols(t)], wr[:, k, :], start=(k == 0), stop=(k == KD - 1))
            last.then_inc(mo["logits"], 1)
            pe.wait_ge(mo["sel"], 1)
            for t in range(NT):
                r = ROWS[t]
                for j in range(t):
                    pe.matmul(ps[0:r, 4 + t, 0:NE], c_(C_ONE, r), sel[:, j, :], start=(j == 0), stop=False)
                pe.matmul(ps[0:r, 4 + t, 0:NE], c_(C_BEF, r, r), sel[0:r, t, :], start=(t == 0), stop=True)
            for t in range(NT):
                last = pe.matmul(ps[:, 7, 0:NE], c_(C_ONE), sel[:, t, :], start=(t == 0), stop=(t == NT - 1))
            last.then_inc(mo["pos"], 1)

        @block.scalar
        def _(act):
            act.wait_ge(mo["top"], NT)
            for t in range(NT):
                r = ROWS[t]
                last = nc.scalar.activation(gate[0:r, t, :], LG[0:r, t, 0:NE], ACT.Exp, bias=cnt[0:r, t:t + 1])
            last.then_inc(mo["exp"], 1)

        @block.vector
        def _(dve):
            link = lambda ins: dve_chain.link(dve, ins)
            nc.vector.memset(LG[:, :, NE:NE + 8], 3 * NEG)
            nc.vector.memset(sel[:, :, :], 0.0)
            nc.vector.memset(slot, -1.0)
            link(nc.vector.memset(gate[:, :, :], 0.0))
            dve.wait_ge(mo["logits"], 1)
            for t in range(NT):
                r = ROWS[t]
                link(nc.vector.tensor_tensor(LG[0:r, t, 0:NE], ps[0:r, t, 0:NE], br[0:r, :], ALU.add))
                link(nc.vector.max(top[0:r, t, :], LG[0:r, t, :]))
                nc.vector.tensor_scalar(cnt[0:r, t:t + 1], top[0:r, t, 0:1], -1.0, None, ALU.mult).then_inc(mo["top"], 1)
                link(nc.vector.memset(top[0:r, t, TOPK:8], 3 * NEG))
                link(nc.vector.match_replace(LR[0:r, t, :], top[0:r, t, :], LG[0:r, t, :], 4 * NEG))
                link(nc.vector.tensor_tensor(sel[0:r, t, :], LR[0:r, t, 0:NE], LG[0:r, t, 0:NE], ALU.not_equal))
            nc.vector.tensor_copy(small[:, 61:62], small[:, 62:63]).then_inc(mo["sel"], 1)
            dve.wait_ge(mo["exp"], 1)
            link(nc.vector.tensor_tensor(gate[:, :, :], gate[:, :, :], sel[:, :, :], ALU.mult))
            link(nc.vector.tensor_reduce(cnt[:, 3:6], gate[:, :, :], AX, ALU.add))
            link(nc.vector.tensor_scalar(cnt[:, 3:6], cnt[:, 3:6], 1e-30, None, ALU.max))
            link(nc.vector.reciprocal(cnt[:, 3:6], cnt[:, 3:6]))
            nc.vector.tensor_tensor(gate[:, :, :], gate[:, :, :], rep(cnt[:, 3:6], [P, NT, NE]), ALU.mult)
            dve.wait_ge(mo["pos"], 1)
            for t in range(NT):
                r = ROWS[t]
                first = slot[0:r, t, 0:NE]
                link(nc.vector.scalar_tensor_tensor(first, ps[0:r, 4 + t, 0:NE], 1.0, sel[0:r, t, :], ALU.add, ALU.mult))
                link(nc.vector.tensor_scalar(first, first, -1.0, None, ALU.add))
                for i in range(1, MAXR):
                    nc.vector.tensor_scalar(slot[0:r, t, i * NE:(i + 1) * NE], first, -float(SLOTS * i), None, ALU.add)
            link(nc.vector.tensor_reduce(cnt[:, 6:7], ps[:, 7, 0:NE], AX, ALU.max))
            link(nc.vector.memset(cnt[:, 7:8], 1.0))
            for i in range(1, MAXR):
                link(nc.vector.scalar_tensor_tensor(cnt[:, 7:8], cnt[:, 6:7], float(SLOTS * i), cnt[:, 7:8], ALU.is_gt, ALU.add))
            link(nc.vector.tensor_scalar(cnt[:, 6:7], cnt[:, 7:8], float(NE // 2), -1.0, ALU.mult, ALU.add))
            nc.vector.tensor_copy(rounds[:, 0:1], cnt[:, 7:8])
            nc.vector.tensor_copy(rounds[:, 1:2], cnt[:, 6:7]).then_inc(mo["rounds"], 1)

    PAIRS = NE // 2
    picked = late_moe.take([P, NT, P])
    gated = late_moe.take([P, NT, P])
    gT = late_moe.take([P, NT, P])
    xe = late_moe.take([P, KD, P])
    glu = late_moe.take([P, D])
    lin = late_moe.take([P, D])
    sg = late_moe.take([P, D])
    aT = late_moe.take([P, KD, P])
    ye = late_moe.take([P, D])
    lp = {n: sem("pair_" + n) for n in ("picked", "gathered", "xe_ready", "gt_turned", "gt_ready", "glu", "clipped", "joined", "sig", "act", "a_turned",
                                        "a_act", "a_dve", "y_act", "y_dve", "combined", "added")}

    COMBINE_BANKS = (6, 7, 4, 5, 6, 7)

    def wait_hidden(eng, it):
        eng.wait_ge(free[15 % RING], it * 2 + 2)

    def wait_y(eng, it):
        eng.wait_ge(free[23 % RING], it * 2 + 2)

    def n_rounds(eng):
        return eng.value_load(rounds[0:1, 0:1], min_val=1, max_val=MAXR)

    def last_pair(eng):
        return eng.value_load(rounds[0:1, 1:2], min_val=PAIRS - 1, max_val=MAXR * PAIRS - 1)

    with nc.Block() as block:
        @block.sync
        def _(sp):
            nr = n_rounds(sp)
            with sp.Fori(0, nr * PAIRS - 1) as it:
                e = sp.snap((it % PAIRS) * 2)
                after = sp.snap(((it + 1) % PAIRS) * 2)
                for n in range(RING, FILLS):
                    sp.wait_ge(free[n % RING], it * 2 + 1)
                    fill(sp, n, e)
                for n in range(RING):
                    sp.wait_ge(free[n % RING], it * 2 + 2)
                    fill(sp, n, after)
            final = last_pair(sp)
            for n in range(RING, FILLS):
                sp.wait_ge(free[n % RING], final * 2 + 1)
                fill(sp, n, NE - 2)

        @block.tensor
        def _(pe):
            def gather(done):
                pe.wait_ge(lp["picked"], done + 1)
                for k in range(KD):
                    for t in range(NT):
                        last = pe.matmul(ps[:, 6 + k // 4, (k % 4) * P:(k % 4 + 1) * P], xh[0:ROWS[t], t, k * P:(k + 1) * P],
                                         picked[0:ROWS[t], t, :], start=(t == 0), stop=(t == NT - 1))
                last.then_inc(lp["gathered"], 1)

            def expert_bias(it, a, banks):
                mine = pick[:, bass.ds(pe.snap((it % PAIRS) * P), P)] if type(it) is not int else pick[:, 0:P]
                for i, bank in enumerate(banks):
                    pe.matmul(ps[:, bank, :], mine, b1[:, a + i * 512:a + (i + 1) * 512], start=True, stop=True)

            def hidden(it, k):
                for x in range(2):
                    n = 2 * k + x
                    pe.wait_ge(full[n % RING], (it * 2 + n // RING + 1) * 16)
                for c in range(4):
                    for x in range(2):
                        n = 2 * k + x
                        last = pe.matmul(ps[64 * x:64 * x + 64, c, :], xe[:, k, 64 * x:64 * x + 64], ring[n % RING][:, c * 512:(c + 1) * 512],
                                         start=False, stop=(k == KD - 1), skip_group_check=True)
                        if c == 3:
                            last.then_inc(free[n % RING], 1)

            def start_hidden(it):
                expert_bias(it, 0, range(4))
                pe.wait_ge(lp["xe_ready"], it + 1)
                hidden(it, 0)

            def turn_gates(it):
                pe.wait_ge(lp["added"], it * 6 + 3)
                for t in range(NT):
                    last = pe.transpose(ps[:, 4, t * P:t * P + ROWS[t]], gated[0:ROWS[t], t, :], c_(C_ID, ROWS[t], ROWS[t]))
                last.then_inc(lp["gt_turned"], 1)

            def output(it):
                pe.wait_ge(lp["act"], it + 1)
                for k in range(KD):
                    last = pe.transpose(ps[:, 6 + k // 4, (k % 4) * P:(k % 4 + 1) * P], lin[:, k * P:(k + 1) * P], ident)
                last.then_inc(lp["a_turned"], 1)
                pe.wait_ge(lp["gt_ready"], it + 1)
                expert_bias(it, 2 * D, (4, 5))
                pe.wait_ge(lp["a_act"], it + 1)
                pe.wait_ge(lp["a_dve"], it + 1)
                for n in range(16, FILLS, 2):
                    for x in range(2):
                        pe.wait_ge(full[(n + x) % RING], (it * 2 + (n + x) // RING + 1) * 16)
                    for j in range(2):
                        k = n - 16 + j
                        for c in range(2):
                            for x in range(2):
                                last = pe.matmul(ps[64 * x:64 * x + 64, 4 + c, :], aT[:, k, 64 * x:64 * x + 64],
                                                 ring[(n + x) % RING][:, j * D + c * 512:j * D + (c + 1) * 512],
                                                 start=False, stop=(k == KD - 1), skip_group_check=True)
                                if c == 1 and j == 1:
                                    last.then_inc(free[(n + x) % RING], 1)

            def combine(it):
                pe.wait_ge(lp["y_act"], it + 1)
                pe.wait_ge(lp["y_dve"], it + 1)
                for t in range(NT):
                    for c in range(2):
                        if t == 2:
                            pe.wait_ge(lp["added"], it * 6 + (7 + c))
                        pe.matmul(ps[0:ROWS[t], COMBINE_BANKS[2 * t + c], :], gT[:, t, 0:ROWS[t]], ye[:, c * 512:(c + 1) * 512],
                                  start=True, stop=True).then_inc(lp["combined"], 1)

            pe.wait_ge(mo["pick_loaded"], 16)
            nr = n_rounds(pe)
            gather(0)
            start_hidden(0)
            with pe.Fori(0, nr * PAIRS - 1) as it:
                hidden(it, 1)
                turn_gates(it)
                for k in range(2, KD):
                    hidden(it, k)
                after = pe.snap(it + 1)
                pe.wait_ge(lp["added"], it * 6 + 6)
                gather(after)
                pe.wait_ge(lp["xe_ready"], it + 2)
                output(it)
                start_hidden(after)
                combine(it)
            final = last_pair(pe)
            hidden(final, 1)
            turn_gates(final)
            for k in range(2, KD):
                hidden(final, k)
            pe.wait_ge(lp["added"], final * 6 + 6)
            output(final)
            combine(final)

        @block.scalar
        def _(act):
            def pair(it):
                act.wait_ge(lp["gt_turned"], it + 1)
                nc.scalar.copy(gT[:, 0:2, :], ps[:, 4, 0:2 * P].rearrange("p (t n) -> p t n", t=2))
                nc.scalar.copy(gT[:, 2, 0:DEC], ps[:, 4, 2 * P:2 * P + DEC]).then_inc(lp["gt_ready"], 1)
                act.wait_ge(lp["glu"], it + 1)
                nc.scalar.activation(sg[:, :], glu[:, :], ACT.Sigmoid, scale=1.702).then_inc(lp["sig"], 1)
                act.wait_ge(lp["a_turned"], it + 1)
                nc.scalar.copy(aT[:, 0:4, :].rearrange("p k n -> p (k n)"), ps[:, 6, :]).then_inc(lp["a_act"], 1)
                wait_y(act, it)
                nc.scalar.copy(ye[:, 0:512], ps[:, 4, :]).then_inc(lp["y_act"], 1)

            nr = n_rounds(act)
            with act.Fori(0, nr * PAIRS) as it:
                pair(it)

        @block.vector
        def _(dve):
            def tables(done):
                for x in range(2):
                    for t in range(NT):
                        q = ROWS[t]
                        io = c_(C_IOTA, SLOTS, q)
                        if type(done) is int:
                            place, mine = slice(x, x + 1), slice(x, x + 1)
                        else:
                            place, mine = bass.ds(done * 2 + x, 1), bass.ds((done % PAIRS) * 2 + x, 1)
                        nc.vector.tensor_scalar(picked[0:q, t, 64 * x:64 * x + 64], io, slot[0:q, t, place], None, ALU.is_equal)
                        last = nc.vector.tensor_scalar(gated[0:q, t, 64 * x:64 * x + 64], io, slot[0:q, t, place], gate[0:q, t, mine], ALU.is_equal, ALU.mult)
                last.then_inc(lp["picked"], 1)

            def expert_input(done):
                dve.wait_ge(lp["gathered"], done + 1)
                for j in range(2):
                    last = nc.vector.tensor_tensor(xe[:, 4 * j:4 * j + 4, :], ps[:, 6 + j, :].rearrange("p (k n) -> p k n", k=4),
                                                   rep(vec[:, V_FFN + 4 * j:V_FFN + 4 * j + 4], [P, 4, P]), ALU.mult)
                last.then_inc(lp["xe_ready"], 1)

            def activation(it):
                wait_hidden(dve, it)
                hid = ps[:, 0:4, :].rearrange("p c (n j) -> p c n j", j=2)
                nc.vector.tensor_scalar(glu[:, :].rearrange("p (c n) -> p c n", c=4), hid[:, :, :, 0], 7.0, None, ALU.min).then_inc(lp["glu"], 1)
                nc.vector.tensor_scalar(lin[:, :].rearrange("p (c n) -> p c n", c=4), hid[:, :, :, 1], 7.0, -7.0, ALU.min, ALU.max).then_inc(lp["clipped"], 1)
                dve.wait_ge(lp["clipped"], it + 1)
                nc.vector.scalar_tensor_tensor(lin[:, :], lin[:, :], 1.0, glu[:, :], ALU.add, ALU.mult).then_inc(lp["joined"], 1)
                dve.wait_ge(lp["joined"], it + 1)
                dve.wait_ge(lp["sig"], it + 1)
                nc.vector.tensor_tensor(lin[:, :], lin[:, :], sg[:, :], ALU.mult).then_inc(lp["act"], 1)

            def add_outputs(it):
                dve.wait_ge(lp["a_turned"], it + 1)
                nc.vector.tensor_copy(aT[:, 4:8, :].rearrange("p k n -> p (k n)"), ps[:, 7, :]).then_inc(lp["a_dve"], 1)
                wait_y(dve, it)
                nc.vector.tensor_copy(ye[:, 512:D], ps[:, 5, :]).then_inc(lp["y_dve"], 1)
                for t in range(NT):
                    for c in range(2):
                        i = 2 * t + c
                        dve.wait_ge(lp["combined"], it * 6 + (i + 1))
                        a = res[0:ROWS[t], t, c * 512:(c + 1) * 512]
                        nc.vector.tensor_tensor(a, a, ps[0:ROWS[t], COMBINE_BANKS[i], :], ALU.add).then_inc(lp["added"], 1)

            nr = n_rounds(dve)
            dve.sem_inc(lp["added"], 6)
            tables(0)
            expert_input(0)
            with dve.Fori(0, nr * PAIRS - 1) as it:
                after = dve.snap(it + 1)
                dve.wait_ge(lp["gt_turned"], it + 1)
                tables(after)
                activation(it)
                expert_input(after)
                add_outputs(it)
            final = last_pair(dve)
            activation(final)
            add_outputs(final)

    fn = {n: sem("final_" + n) for n in ("gain", "sq", "var", "root", "done")}
    with nc.Block() as block:
        place = Arena(arena, AT_MOE)
        nf, junk = place.take([P, D]), place.take([P, D])

        @block.sync
        def _(sp):
            sp.dma_start(nf[:, :], norm_final.partition_broadcast(P)).then_inc(fn["gain"], 16)
            sp.wait_ge(fn["done"], 1)
            store(sp, y_prompt[0, 0:P, :], res[:, 0, :])
            sp.wait_ge(fn["done"], 2)
            store(sp, y_prompt[0, P:SEQ, :], res[:, 1, :])
            sp.wait_ge(fn["done"], 3)
            store(sp, y_sample[:, 0, :], res[0:DEC, 2, :])
            sp.wait_ge(stored, n_stored[0])

        @block.scalar
        def _(act):
            for t in range(NT):
                act_chain.link(act, nc.scalar.activation(junk[0:ROWS[t], :], res[0:ROWS[t], t, :], ACT.Square, accum_out=small[0:ROWS[t], t:t + 1]))
            nc.scalar.copy(small[:, 3:4], small[:, 3:4]).then_inc(fn["sq"], 1)
            act.wait_ge(fn["var"], 1)
            nc.scalar.activation(small[:, 4:7], small[:, 4:7], ACT.Sqrt).then_inc(fn["root"], 1)

        @block.vector
        def _(dve):
            dve.wait_ge(fn["sq"], 1)
            nc.vector.tensor_scalar(small[:, 4:7], small[:, 0:3], 1.0 / D, EPS, ALU.mult, ALU.add).then_inc(fn["var"], 1)
            dve.wait_ge(fn["root"], 1)
            dve_chain.link(dve, nc.vector.reciprocal(small[:, 8:11], small[:, 4:7]))
            dve.wait_ge(fn["gain"], 16)
            for t in range(NT):
                a = res[0:ROWS[t], t, :]
                nc.vector.scalar_tensor_tensor(a, a, small[0:ROWS[t], 8 + t:9 + t], nf[0:ROWS[t], :], ALU.mult, ALU.mult).then_inc(fn["done"], 1)

INPUTS = ("x_prompt", "x_sample", "state_gdn", "state_conv", "cache_latent", "cache_krope", "page_table",
          "cache_mem_k", "cache_mem_v", "mem_prompt", "norm_mix", "w_in", "conv_w", "a_log", "dt_bias", "gdn_norm",
          "q_norm", "w_uq", "kv_norm", "w_uk", "w_uv", "w_out", "norm_x", "mem_norm", "w_xq", "w_xk", "w_xv", "w_xo",
          "norm_ffn", "w_router", "b_router", "w_e1", "b_e1", "w_e2", "b_e2", "norm_final")
OUTPUTS = ((1, SEQ, D), (DEC, 1, D), (1, 1, H, P, P), (1, 1, 3, CONV), (1, 1, SEQ, KVR), (1, 1, SEQ, ROPE),
           (1, 1, MEM, H, XD), (1, 1, MEM, H, XD), (1, DEC, H, P, P), (1, DEC, 3, CONV), (DEC, 1, 1, KVR),
           (DEC, 1, 1, ROPE))


def kernel(**inputs):
    import concourse.bacc as bacc
    from concourse.bass_utils import run_bass_kernel_spmd

    nc = bacc.Bacc("TRN2", target_bir_lowering=False, num_devices=1)
    arrays = {name: np.ascontiguousarray(inputs[name]) for name in INPUTS}
    arrays["const_f32"], arrays["const_bf16"] = constants()
    args = [nc.dram_tensor(f"in_{n}", a.shape, mybir.dt.from_np(a.dtype), kind="ExternalInput").ap()
            for n, a in arrays.items()]
    args += [nc.dram_tensor(f"out_{i}", s, F32, kind="ExternalOutput").ap() for i, s in enumerate(OUTPUTS)]
    build(nc, *args)
    ran = run_bass_kernel_spmd(nc, [{f"in_{n}": a for n, a in arrays.items()}], core_ids=[0])
    return tuple(ran.results[0][f"out_{i}"] for i in range(len(OUTPUTS)))
```
